# Optimizing a Trainium2 kernel written in Bass

```python
import jax, jax.numpy as jnp
from jax import lax
import numpy as np

D_MODEL = 1024
BATCH = 1
SEQ = 256
DEPTH = 2
DEC_BATCH = 8
DEC_SEQ = 4
PAST_LEN = 2048
PAGE_SIZE = 128

D_PLE = 256
CHUNK = 64
CONV_W = 4
EPS = 1e-6
N_BRANCH = 4
GLA_H = 4
GLA_DK = 64
GLA_DV = 128
GLA_RANK = 16
GLA_GATE_NORM = 16.0
RET_H = 4
RET_DK = 64
RET_DV = 128
ROPE_BASE = 10000.0
GDN_H = 4
GDN_DK = 64
GDN_DV = 128
GDN_CONV_C = 2 * GDN_H * GDN_DK + GDN_H * GDN_DV
SSD_H = 8
SSD_P = 64
SSD_N = 64
SSD_G = 2
SSD_DI = SSD_H * SSD_P
SSD_CONV_C = SSD_DI + 2 * SSD_G * SSD_N
BRANCH_W = 512
D_FF = 2816
N_EXPERTS = 8
TOP_K = 2
N_DENSE = (DEPTH + 1) // 2
N_MOE = DEPTH // 2
SPLITS = (GLA_H * GLA_DK, GLA_H * GLA_DK, GLA_H * GLA_DV, GLA_RANK, GLA_H * GLA_DV,
          RET_H * RET_DK, RET_H * RET_DK, RET_H * RET_DV, RET_H * RET_DV,
          GDN_CONV_C, GDN_H, GDN_H, GDN_H * GDN_DV,
          SSD_DI, SSD_CONV_C, SSD_H,
          N_BRANCH * D_MODEL)
D_IN = sum(SPLITS)

kernel_name = "hybrid_gla_ret_gdn_ssd_decode_step"

def rmsnorm(x, g):
    x32 = x.astype(jnp.float32)
    y = x32 * lax.rsqrt(jnp.mean(x32 * x32, axis=-1, keepdims=True) + EPS)
    return (y * g.astype(jnp.float32)).astype(x.dtype)

def l2norm(x):
    x32 = x.astype(jnp.float32)
    return (x32 * lax.rsqrt(jnp.sum(x32 * x32, axis=-1, keepdims=True) + EPS)).astype(x.dtype)

def causal_conv(u, buf, w):
    L = u.shape[1]
    full = jnp.concatenate([buf.astype(u.dtype), u], axis=1)
    out = full[:, 0:L] * w[0]
    for t in range(1, CONV_W):
        out = out + full[:, t:t + L] * w[t]
    return out, full[:, L:]

def rope(t, pos):
    half = t.shape[-1] // 2
    inv = ROPE_BASE ** (-jnp.arange(half, dtype=jnp.float32) / half)
    ang = pos.astype(jnp.float32)[:, None] * inv[None, :]
    cos = jnp.cos(ang)[:, None, :]
    sin = jnp.sin(ang)[:, None, :]
    t32 = t.astype(jnp.float32)
    t1, t2 = t32[..., :half], t32[..., half:]
    return jnp.concatenate([t1 * cos - t2 * sin, t1 * sin + t2 * cos], axis=-1).astype(t.dtype)

def _chunk_size(L):
    return CHUNK if L % CHUNK == 0 else L

def _to_chunks(t, c):
    B_, L, H = t.shape[:3]
    rest = t.shape[3:]
    t = t.reshape((B_, L // c, c, H) + rest)
    perm = (1, 0, 3, 2) + tuple(range(4, t.ndim))
    return jnp.transpose(t, perm).astype(jnp.float32)

def _from_chunks(o):
    n, B_, H, c, d = o.shape
    return jnp.transpose(o, (1, 0, 3, 2, 4)).reshape(B_, n * c, H, d)

def _masks(c):
    idx = jnp.arange(c)
    return idx[:, None] >= idx[None, :], idx[:, None] > idx[None, :]

def _pair_decay(G, mask):
    diff = G[..., :, None] - G[..., None, :]
    return jnp.where(mask, jnp.exp(jnp.where(mask, diff, 0.0)), 0.0)

def chunked_scalar_decay(q, k, v, logd, S0):
    c = _chunk_size(q.shape[1])
    incl, _ = _masks(c)

    def step(S, blk):
        qc, kc, vc, lc = blk
        G = jnp.cumsum(lc, axis=-1)
        A = jnp.einsum('bhid,bhjd->bhij', qc, kc) * _pair_decay(G, incl)
        o = (jnp.einsum('bhij,bhjv->bhiv', A, vc)
             + jnp.einsum('bhid,bhdv->bhiv', qc * jnp.exp(G)[..., None], S))
        S = (S * jnp.exp(G[..., -1])[..., None, None]
             + jnp.einsum('bhjd,bhjv->bhdv', kc * jnp.exp(G[..., -1:] - G)[..., None], vc))
        return S, o

    S, o = lax.scan(step, S0.astype(jnp.float32),
                    (_to_chunks(q, c), _to_chunks(k, c), _to_chunks(v, c), _to_chunks(logd, c)))
    return _from_chunks(o).astype(v.dtype), S.astype(S0.dtype)

def chunked_vector_decay(q, k, v, logd, S0):
    c = _chunk_size(q.shape[1])
    incl, _ = _masks(c)
    m = incl[:, :, None]

    def step(S, blk):
        qc, kc, vc, lc = blk
        G = jnp.cumsum(lc, axis=-2)
        diff = G[:, :, :, None, :] - G[:, :, None, :, :]
        D = jnp.where(m, jnp.exp(jnp.where(m, diff, 0.0)), 0.0)
        A = jnp.einsum('bhid,bhjd,bhijd->bhij', qc, kc, D)
        o = (jnp.einsum('bhij,bhjv->bhiv', A, vc)
             + jnp.einsum('bhid,bhdv->bhiv', qc * jnp.exp(G), S))
        S = (S * jnp.exp(G[:, :, -1, :])[..., None]
             + jnp.einsum('bhjd,bhjv->bhdv', kc * jnp.exp(G[:, :, -1:, :] - G), vc))
        return S, o

    S, o = lax.scan(step, S0.astype(jnp.float32),
                    (_to_chunks(q, c), _to_chunks(k, c), _to_chunks(v, c), _to_chunks(logd, c)))
    return _from_chunks(o).astype(v.dtype), S.astype(S0.dtype)

def chunked_gated_delta(q, k, v, beta, logd, S0):
    c = _chunk_size(q.shape[1])
    incl, strict = _masks(c)
    eye = jnp.eye(c, dtype=jnp.float32)

    def step(S, blk):
        qc, kc, vc, bc, lc = blk
        G = jnp.cumsum(lc, axis=-1)
        Dm = _pair_decay(G, incl)
        kb = kc * bc[..., None]
        M = jnp.einsum('bhid,bhjd->bhij', kb, kc) * jnp.where(strict, Dm, 0.0)
        T = eye + M
        u = lax.linalg.triangular_solve(T, vc * bc[..., None], left_side=True, lower=True)
        w = lax.linalg.triangular_solve(T, kb * jnp.exp(G)[..., None], left_side=True, lower=True)
        vn = u - jnp.einsum('bhid,bhdv->bhiv', w, S)
        A = jnp.einsum('bhid,bhjd->bhij', qc, kc) * Dm
        o = (jnp.einsum('bhij,bhjv->bhiv', A, vn)
             + jnp.einsum('bhid,bhdv->bhiv', qc * jnp.exp(G)[..., None], S))
        S = (S * jnp.exp(G[..., -1])[..., None, None]
             + jnp.einsum('bhjd,bhjv->bhdv', kc * jnp.exp(G[..., -1:] - G)[..., None], vn))
        return S, o

    S, o = lax.scan(step, S0.astype(jnp.float32),
                    (_to_chunks(q, c), _to_chunks(k, c), _to_chunks(v, c),
                     _to_chunks(beta, c), _to_chunks(logd, c)))
    return _from_chunks(o).astype(v.dtype), S.astype(S0.dtype)

def token_mixers(u, gla0, ret0, gdn0, gdnc0, ssd0, ssdc0, prm, i, pos0):
    B_, L, _ = u.shape
    f32 = jnp.float32
    z = u @ prm['w_in'][i]
    cuts = [int(s) for s in np.cumsum(SPLITS)[:-1]]
    (gq, gk, gv, glr, gg, rq, rk, rv, rg, dqkv, db, da, dg, sz, sxbc, sdt, mg) = jnp.split(z, cuts, axis=-1)

    def heads(t, h):
        return t.reshape(B_, L, h, -1)

    q = heads(gq, GLA_H) * GLA_DK ** -0.5
    k = heads(gk, GLA_H)
    v = heads(gv, GLA_H)
    lg = jax.nn.log_sigmoid((glr @ prm['gla_w_gk'][i] + prm['gla_b_gk'][i]).astype(f32)) / GLA_GATE_NORM
    oa, gla1 = chunked_vector_decay(q, k, v, heads(lg, GLA_H), gla0)
    oa = (rmsnorm(oa, prm['gla_norm'][i]) * jax.nn.silu(heads(gg, GLA_H))).reshape(B_, L, -1)

    pos = pos0 + jnp.arange(L)
    q = rope(heads(rq, RET_H), pos)
    k = rope(heads(rk, RET_H), pos) * RET_DK ** -0.5
    v = heads(rv, RET_H)
    log_gamma = jnp.log(1.0 - 2.0 ** (-5.0 - jnp.arange(RET_H, dtype=f32)))
    ob, ret1 = chunked_scalar_decay(q, k, v, jnp.broadcast_to(log_gamma, (B_, L, RET_H)), ret0)
    ob = (rmsnorm(ob, prm['ret_norm'][i]) * jax.nn.silu(heads(rg, RET_H))).reshape(B_, L, -1)

    cqkv, gdnc1 = causal_conv(dqkv, gdnc0, prm['gdn_conv_w'][i])
    cqkv = jax.nn.silu(cqkv)
    cq, ck, cv = jnp.split(cqkv, [GDN_H * GDN_DK, 2 * GDN_H * GDN_DK], axis=-1)
    q = l2norm(heads(cq, GDN_H)) * GDN_DK ** -0.5
    k = l2norm(heads(ck, GDN_H))
    v = heads(cv, GDN_H)
    beta = jax.nn.sigmoid(db.astype(f32))
    lgd = -jnp.exp(prm['gdn_a_log'][i].astype(f32)) * jax.nn.softplus(da.astype(f32) + prm['gdn_dt_bias'][i].astype(f32))
    oc, gdn1 = chunked_gated_delta(q, k, v, beta, lgd, gdn0)
    oc = (rmsnorm(oc, prm['gdn_norm'][i]) * jax.nn.silu(heads(dg, GDN_H))).reshape(B_, L, -1)

    xbc, ssdc1 = causal_conv(sxbc, ssdc0, prm['ssd_conv_w'][i])
    xbc = jax.nn.silu(xbc + prm['ssd_conv_b'][i])
    sx, sB, sC = jnp.split(xbc, [SSD_DI, SSD_DI + SSD_G * SSD_N], axis=-1)
    xh = heads(sx, SSD_H)
    rep = SSD_H // SSD_G
    Bh = jnp.repeat(heads(sB, SSD_G), rep, axis=2)
    Ch = jnp.repeat(heads(sC, SSD_G), rep, axis=2)
    dt = jax.nn.softplus(sdt.astype(f32) + prm['ssd_dt_bias'][i].astype(f32))
    lsd = dt * -jnp.exp(prm['ssd_a_log'][i].astype(f32))
    yd, ssd1 = chunked_scalar_decay(Ch, Bh, xh * dt[..., None].astype(xh.dtype), lsd, ssd0)
    yd = yd + xh * prm['ssd_d'][i][:, None]
    yd = (yd.reshape(B_, L, SSD_DI) * jax.nn.silu(sz)).reshape(B_, L, SSD_G, SSD_DI // SSD_G)
    od = rmsnorm(yd, prm['ssd_norm'][i].reshape(SSD_G, -1)).reshape(B_, L, SSD_DI)

    br = jnp.stack([oa, ob, oc, od], axis=2)
    proj = jnp.einsum('blnv,nvd->blnd', br, prm['w_branch'][i])
    gates = jax.nn.sigmoid(mg.reshape(B_, L, N_BRANCH, D_MODEL))
    out = jnp.sum(gates * proj, axis=2) @ prm['w_out'][i]
    return out, (gla1, ret1, gdn1, gdnc1, ssd1, ssdc1)

def swiglu(x, wg, wu, wd):
    return (jax.nn.silu(x @ wg) * (x @ wu)) @ wd

def moe_swiglu(x, router, wg, wu, wd):
    logits = (x @ router).astype(jnp.float32)
    top_v, top_i = lax.top_k(logits, TOP_K)
    w = jax.nn.softmax(top_v, axis=-1)
    comb = jnp.einsum('blk,blke->ble', w, jax.nn.one_hot(top_i, N_EXPERTS, dtype=jnp.float32)).astype(x.dtype)
    y = jnp.zeros_like(x)
    for e in range(N_EXPERTS):
        y = y + comb[..., e:e + 1] * swiglu(x, wg[e], wu[e], wd[e])
    return y

def trunk(x, p, gla0, ret0, gdn0, gdnc0, ssd0, ssdc0, prm, pos0):
    h = x
    new = ([], [], [], [], [], [])
    for i in range(DEPTH):
        mix, st = token_mixers(rmsnorm(h, prm['norm_mix'][i]), gla0[i], ret0[i], gdn0[i],
                               gdnc0[i], ssd0[i], ssdc0[i], prm, i, pos0)
        h = h + mix
        u = rmsnorm(h, prm['norm_ffn'][i])
        j = i // 2
        if i % 2 == 0:
            h = h + swiglu(u, prm['ffn_w_gate'][j], prm['ffn_w_up'][j], prm['ffn_w_down'][j])
        else:
            h = h + moe_swiglu(u, prm['moe_router'][j], prm['moe_w_gate'][j], prm['moe_w_up'][j], prm['moe_w_down'][j])
        gate = jax.nn.sigmoid(rmsnorm(h, prm['norm_ple'][i]) @ prm['ple_w_gate'][i])
        h = h + gate * (p[i] @ prm['ple_w_proj'][i])
        for lst, s in zip(new, st):
            lst.append(s)
    y = rmsnorm(h, prm['norm_final'])
    return y, [jnp.stack(lst) for lst in new]

def setup_inputs(seed: int = 0) -> dict:
    key = jax.random.key(seed)
    ks = iter(jax.random.split(key, 64))
    f32 = jnp.float32

    def nrm(shape, scale):
        return jax.random.normal(next(ks), shape, f32) * scale

    def gain(shape):
        return 1.0 + nrm(shape, 0.01)

    def dt_bias(shape):
        dt = jnp.exp(jax.random.uniform(next(ks), shape, f32, minval=np.log(1e-3), maxval=np.log(1e-1)))
        return dt + jnp.log(-jnp.expm1(-dt))

    def a_log(shape):
        return jnp.log(jax.random.uniform(next(ks), shape, f32, minval=1.0, maxval=16.0))

    return {
        'x_prompt': nrm((BATCH, SEQ, D_MODEL), 1.0),
        'x_sample': nrm((DEC_BATCH, DEC_SEQ, D_MODEL), 1.0),
        'state_gla': nrm((DEPTH, DEC_BATCH, GLA_H, GLA_DK, GLA_DV), 1.0),
        'state_ret': nrm((DEPTH, DEC_BATCH, RET_H, RET_DK, RET_DV), 1.0),
        'state_gdn': nrm((DEPTH, DEC_BATCH, GDN_H, GDN_DK, GDN_DV), 1.0),
        'state_gdn_conv': nrm((DEPTH, DEC_BATCH, CONV_W - 1, GDN_CONV_C), 1.0),
        'state_ssd': nrm((DEPTH, DEC_BATCH, SSD_H, SSD_N, SSD_P), 1.0),
        'state_ssd_conv': nrm((DEPTH, DEC_BATCH, CONV_W - 1, SSD_CONV_C), 1.0),
        'p_prompt': nrm((DEPTH, BATCH, SEQ, D_PLE), 1.0),
        'p_sample': nrm((DEPTH, DEC_BATCH, DEC_SEQ, D_PLE), 1.0),
        'norm_mix': gain((DEPTH, D_MODEL)),
        'w_in': nrm((DEPTH, D_MODEL, D_IN), D_MODEL ** -0.5),
        'gla_w_gk': nrm((DEPTH, GLA_RANK, GLA_H * GLA_DK), GLA_RANK ** -0.5),
        'gla_b_gk': nrm((DEPTH, GLA_H * GLA_DK), 0.1),
        'gla_norm': gain((DEPTH, GLA_DV)),
        'ret_norm': gain((DEPTH, RET_DV)),
        'gdn_conv_w': nrm((DEPTH, CONV_W, GDN_CONV_C), CONV_W ** -0.5),
        'gdn_a_log': a_log((DEPTH, GDN_H)),
        'gdn_dt_bias': dt_bias((DEPTH, GDN_H)),
        'gdn_norm': gain((DEPTH, GDN_DV)),
        'ssd_conv_w': nrm((DEPTH, CONV_W, SSD_CONV_C), CONV_W ** -0.5),
        'ssd_conv_b': nrm((DEPTH, SSD_CONV_C), 0.02),
        'ssd_a_log': a_log((DEPTH, SSD_H)),
        'ssd_dt_bias': dt_bias((DEPTH, SSD_H)),
        'ssd_d': gain((DEPTH, SSD_H)),
        'ssd_norm': gain((DEPTH, SSD_DI)),
        'w_branch': nrm((DEPTH, N_BRANCH, BRANCH_W, D_MODEL), BRANCH_W ** -0.5),
        'w_out': nrm((DEPTH, D_MODEL, D_MODEL), D_MODEL ** -0.5),
        'norm_ffn': gain((DEPTH, D_MODEL)),
        'ffn_w_gate': nrm((N_DENSE, D_MODEL, D_FF), D_MODEL ** -0.5),
        'ffn_w_up': nrm((N_DENSE, D_MODEL, D_FF), D_MODEL ** -0.5),
        'ffn_w_down': nrm((N_DENSE, D_FF, D_MODEL), D_FF ** -0.5),
        'moe_router': nrm((N_MOE, D_MODEL, N_EXPERTS), D_MODEL ** -0.5),
        'moe_w_gate': nrm((N_MOE, N_EXPERTS, D_MODEL, D_FF), D_MODEL ** -0.5),
        'moe_w_up': nrm((N_MOE, N_EXPERTS, D_MODEL, D_FF), D_MODEL ** -0.5),
        'moe_w_down': nrm((N_MOE, N_EXPERTS, D_FF, D_MODEL), D_FF ** -0.5),
        'norm_ple': gain((DEPTH, D_MODEL)),
        'ple_w_gate': nrm((DEPTH, D_MODEL, D_MODEL), D_MODEL ** -0.5),
        'ple_w_proj': nrm((DEPTH, D_PLE, D_MODEL), D_PLE ** -0.5),
        'norm_final': gain((D_MODEL,)),
    }

def reference(x_prompt, x_sample, state_gla, state_ret, state_gdn, state_gdn_conv, state_ssd,
              state_ssd_conv, p_prompt, p_sample, norm_mix, w_in, gla_w_gk, gla_b_gk, gla_norm,
              ret_norm, gdn_conv_w, gdn_a_log, gdn_dt_bias, gdn_norm, ssd_conv_w, ssd_conv_b,
              ssd_a_log, ssd_dt_bias, ssd_d, ssd_norm, w_branch, w_out, norm_ffn, ffn_w_gate,
              ffn_w_up, ffn_w_down, moe_router, moe_w_gate, moe_w_up, moe_w_down, norm_ple,
              ple_w_gate, ple_w_proj, norm_final):
    prm = dict(norm_mix=norm_mix, w_in=w_in, gla_w_gk=gla_w_gk, gla_b_gk=gla_b_gk, gla_norm=gla_norm,
               ret_norm=ret_norm, gdn_conv_w=gdn_conv_w, gdn_a_log=gdn_a_log, gdn_dt_bias=gdn_dt_bias,
               gdn_norm=gdn_norm, ssd_conv_w=ssd_conv_w, ssd_conv_b=ssd_conv_b, ssd_a_log=ssd_a_log,
               ssd_dt_bias=ssd_dt_bias, ssd_d=ssd_d, ssd_norm=ssd_norm, w_branch=w_branch, w_out=w_out,
               norm_ffn=norm_ffn, ffn_w_gate=ffn_w_gate, ffn_w_up=ffn_w_up, ffn_w_down=ffn_w_down,
               moe_router=moe_router, moe_w_gate=moe_w_gate, moe_w_up=moe_w_up, moe_w_down=moe_w_down,
               norm_ple=norm_ple, ple_w_gate=ple_w_gate, ple_w_proj=ple_w_proj, norm_final=norm_final)
    bp = x_prompt.shape[0]
    dtp = x_prompt.dtype
    y_prompt, sp = trunk(
        x_prompt, p_prompt,
        jnp.zeros((DEPTH, bp, GLA_H, GLA_DK, GLA_DV), dtp),
        jnp.zeros((DEPTH, bp, RET_H, RET_DK, RET_DV), dtp),
        jnp.zeros((DEPTH, bp, GDN_H, GDN_DK, GDN_DV), dtp),
        jnp.zeros((DEPTH, bp, CONV_W - 1, GDN_CONV_C), dtp),
        jnp.zeros((DEPTH, bp, SSD_H, SSD_N, SSD_P), dtp),
        jnp.zeros((DEPTH, bp, CONV_W - 1, SSD_CONV_C), dtp),
        prm, 0)
    y_sample, ss = trunk(x_sample, p_sample, state_gla, state_ret, state_gdn, state_gdn_conv,
                         state_ssd, state_ssd_conv, prm, PAST_LEN)
    return (y_prompt, y_sample, sp[0], sp[1], sp[2], sp[3], sp[4], sp[5],
            ss[0], ss[1], ss[2], ss[3], ss[4], ss[5])


_drawn_inputs = setup_inputs


def setup_inputs(seed=0):
    import zlib

    import numpy as np

    out = dict(_drawn_inputs(seed))
    spreads = {}
    factors = {'gla_norm': 7.174,
     'ret_norm': 8.0,
     'gdn_norm': 8.0,
     'ssd_d': 5.01,
     'ssd_norm': 4.805,
     'norm_ffn': 2.724,
     'norm_ple': 8.0,
     'norm_final': 5.448}
    for name, (base, spread) in spreads.items():
        noise = np.random.default_rng([zlib.crc32(name.encode()), seed]).standard_normal(out[name].shape)
        drawn = base * np.exp(spread * noise) if base else spread * noise
        out[name] = __import__('jax').numpy.asarray(drawn.astype(out[name].dtype))
    for name, factor in factors.items():
        out[name] = (out[name] * factor).astype(out[name].dtype)
    return out
```

```python
from contextlib import ExitStack
import concourse.bass as bass
from concourse import mybir
import numpy as np

F32 = mybir.dt.float32
I32 = mybir.dt.int32
ALU = mybir.AluOpType
ACT = mybir.ActivationFunctionType
AX = mybir.AxisListType

P = 128
D_MODEL, DEPTH = 1024, 2
SEQ, NSEQ, DSEQ, PAST = 256, 8, 4, 2048
SAMP = NSEQ * DSEQ
TOK = SEQ + SAMP
KD = D_MODEL // P
D_PLE, D_FF, NE, TOP_K, NF = 256, 2816, 8, 2, 2816 // 128
EPS = 1e-6
PAIR = 416
RING, TILE = 11, 1024
ZW = 320
TB = [(0, 128), (128, 128), (256, 32)]
SEGS = [(128, 0, 256, 0), (128, 128, 256, 256), (32, 256, 288, 384)]

GLA, RET, GDN, SSD = range(4)
HEADS = [4, 4, 4, 8]
HBASE = [0, 4, 8, 12]
NHEAD = 20
DV = [128, 128, 128, 64]
ZBLOCKS = [12, 12, 12, 10]
NCONV = [0, 0, 8, 6]
CONV0 = [0, 0, 0, 8]
GATE0 = [8, 8, 8, 6]
OUT0 = [4, 4, 0, 0]
SSD_COL = {GDN: 4, SSD: 8}

_SP = (256, 256, 512, 16, 512, 256, 256, 512, 512, 1024, 4, 4, 512, 512, 768, 8, 4096)
_C = np.concatenate([[0], np.cumsum(_SP)]).tolist()
ZCOLS = [
    [_C[0] + 128 * i for i in range(8)] + [_C[4] + 128 * i for i in range(4)],
    [_C[5] + 128 * i for i in range(12)],
    [_C[9] + 128 * i for i in range(8)] + [_C[12] + 128 * i for i in range(4)],
    [_C[14] + 128 * i for i in range(6)] + [_C[13] + 128 * i for i in range(4)],
]
ZSCALE = [
    [0.125] * 2 + [1.0] * 6 + [0.5] * 4,
    [1.0] * 2 + [0.125] * 2 + [1.0] * 4 + [0.5] * 4,
    [1.0] * 8 + [0.5] * 4,
    [1.0] * 6 + [0.5] * 4,
]


def half_pair(n, h):
    return (h // 4, h % 4) if n == SSD else (h % 2, h // 2)


def _block_masks():
    j, i = np.arange(P)[:, None], np.arange(P)[None, :]
    s, t = np.arange(SAMP)[:, None], np.arange(SAMP)[None, :]
    same = (s // DSEQ) == (t // DSEQ)
    return j, i, s, t, same


def constants():
    j, i, s, t, same = _block_masks()
    f = np.float32

    def packed(big, off, small):
        m = np.zeros((P, PAIR), f)
        m[:, 0:128], m[:, 128:256], m[:, 256:384], m[:32, 384:416] = big, off, big, small
        return m

    def pad(a):
        m = np.zeros((P, a.shape[1]), f)
        m[:a.shape[0]] = a
        return m

    c = {}
    c["ident"] = np.eye(P)
    c["ones"] = np.ones((P, P))
    c["halfones"] = (j // 64 == i // 64) * 1.0
    c["upto"] = np.concatenate([j <= i, np.ones((P, P))], 1)
    c["after"] = (j > i) * 1.0
    c["upto_s"] = pad((same & (s <= t)) * 1.0)
    c["after_s"] = pad((same & (s > t)) * 1.0)
    c["future"] = packed(np.where(j <= i, 0, -1e30), 0, np.where(same & (s <= t), 0, -1e30))
    c["strict"] = packed(j < i, 1, same & (s < t))
    c["seq_of"] = pad((np.arange(SAMP)[:, None] // DSEQ == np.arange(NSEQ)[None, :]) * 1.0)
    pos = np.concatenate([np.arange(SEQ), PAST + np.tile(np.arange(DSEQ), NSEQ)]).astype(np.float64)
    inv = 10000.0 ** (-np.arange(32, dtype=np.float32).astype(np.float64) / 32)
    inv = inv.astype(f)
    ang = (pos.astype(f)[None, :] * np.tile(inv, 4)[:, None]).astype(f).astype(np.float64)
    c["cos"], c["sin"] = np.cos(ang), np.sin(ang)
    rot = np.zeros((P, P))
    for q in range(P):
        d = q % 64
        if d < 32:
            rot[q + 32, q] = -1.0
        else:
            rot[q - 32, q] = 1.0
    c["rot"] = rot
    lgam = np.log(1.0 - 2.0 ** (-5.0 - np.arange(4)))
    seg, kd = [], np.zeros((P, 3, 16))
    eg = np.zeros((P, 2, SAMP))
    for h in range(4):
        big = np.where(j <= i, np.exp(np.minimum(i - j, 999) * lgam[h] * (j <= i)), 0)
        off = np.exp((i + P - j) * lgam[h])
        small = np.where(same & (s <= t), np.exp(np.where(same & (s <= t), t - s, 0) * lgam[h]), 0)
        seg.append(packed(big, off, small))
        kd[:, 0, h] = np.exp((SEQ - 1 - np.arange(P)) * lgam[h])
        kd[:, 1, h] = np.exp((P - 1 - np.arange(P)) * lgam[h])
        kd[:SAMP, 2, h] = np.exp((DSEQ - 1 - np.arange(SAMP) % DSEQ) * lgam[h])
        eg[64 * (h % 2):64 * (h % 2) + 64, h // 2, :] = np.exp((np.arange(SAMP) % DSEQ + 1) * lgam[h])
    c["ret_decay"] = np.concatenate(seg, 1)
    c["ret_kd"] = kd.reshape(P, 48)
    c["ret_eg"] = eg.reshape(P, 64)
    lv = []
    for w in (1, 2, 4, 8, 16, 32, 64):
        lv.append((j // (2 * w) == i // (2 * w)) & (j % (2 * w) < w) & (i % (2 * w) >= w))
    c["levels"] = np.concatenate(lv, 1)
    hs = np.zeros((P, 48))
    hs[:64, 15], hs[64:, 31] = 1, 1
    c["row_pick"] = hs
    rep = np.zeros((P, 2, P))
    reps = np.zeros((P, 2, SAMP))
    for h in range(2):
        for q in range(P):
            rep[16 * h + q % 16, h, q] = 1
        for q in range(SAMP):
            reps[16 * h + q % DSEQ, h, q] = 1
    c["spread"] = rep.reshape(P, -1)
    c["spread_s"] = reps.reshape(P, -1)
    dm = np.zeros((P, TOK))
    dm[:, :128] = (j // 16 == i // 16) & (j <= i)
    dm[:, 128:256] = dm[:, :128]
    dm[:SAMP, 256:] = same & (s <= t)
    c["sub_diag"] = dm
    c["less"] = np.tile((np.arange(8)[None, :] < np.arange(8)[:, None]).reshape(1, 64) * 1.0, (P, 1))
    c["slot_row"] = np.tile(np.arange(P)[None, :] * 1.0, (P, 1))
    c["slot_col"] = np.arange(P)[:, None] * 1.0
    c["eps"] = np.full((P, 1), EPS)
    return {k: np.ascontiguousarray(v, dtype=f) for k, v in c.items()}


CONST = constants()
CAT = {}
_n = 0
for _k, _v in CONST.items():
    CAT[_k] = (_n, _v.shape[1])
    _n += _v.shape[1]
NCONST = _n

PV = {}
_n = 0
for _k, _w in (("norm_mix", 8), ("norm_ffn", 8), ("norm_ple", 8), ("norm_final", 8), ("gla_norm", 1),
               ("ret_norm", 1), ("gdn_norm", 1), ("ssd_norm", 4), ("conv_w", 56), ("conv_b", 14), ("ssd_d", 4)):
    PV[_k] = (_n, _w)
    _n += _w
NPV = _n


def tile_table():
    out = []
    for L in range(DEPTH):
        def z(n):
            return [("z", L, n, b) for b in range(ZBLOCKS[n])]

        def mg(n):
            return [("mg", L, n, b) for b in range(KD)]

        def br(n):
            return [("br", L, n, b) for b in range(4)]

        out += z(0)
        out += z(1) + mg(0)
        out += br(0) + z(2) + mg(1)
        out += br(1) + z(3) + mg(2)
        out += br(2) + mg(3)
        out += br(3)
        out += [("out", L, 0, b) for b in range(KD)]
        if L % 2 == 0:
            for b in range(NF):
                out += [("gate", L, 0, b), ("up", L, 0, b)]
            out += [("down", L, 0, b) for b in range(NF)]
        else:
            out += [("experts", L, 0, 0)]
        out += [("pproj", L, 0, b) for b in range(2)]
        out += [("pgate", L, 0, b) for b in range(KD)]
    return out

TABLE = tile_table()
EXPERT_AT = next(i for i, x in enumerate(TABLE) if x[0] == "experts")
PLAIN = [x for x in TABLE if x[0] != "experts"]
T_OF = {x: i for i, x in enumerate(PLAIN)}
E_TILES = 3 * NF
NSLOT = [38, 10, 34, 18]


def fill_tiles(L):
    out = []
    for n in range(4):
        mine = [x for x in PLAIN if x[1] == L and ((x[0] == "z" and x[2] == n + 1 and n + 1 > 0) or
                                                  (x[0] == "mg" and x[2] == n) or (x[0] == "br" and x[2] == n - 1))]
        mine = [x for x in mine if not (x[0] == "br" and x[2] == 3)]
        mine.sort(key=lambda x: T_OF[x])
        k = NSLOT[n]
        out.append([mine[len(mine) * s // k:len(mine) * (s + 1) // k] for s in range(k)])
    return out


FILL = [fill_tiles(L) for L in range(DEPTH)]
TAKER = {"z": "act", "mg": "act", "br": "dve", "out": "dve", "gate": "ffn", "up": "ffn", "down": "ffn",
         "pproj": "act", "pgate": "ple"}


def taken_before(t, who):
    return sum(TAKER[x[0]] == who for x in PLAIN[:max(t, 0)])


def build(nc, io):
    ctx = ExitStack()
    with ctx:
        def semaphore(name):
            return ctx.enter_context(nc.semaphore(name))

        slot_in = [semaphore(f"slot{j}_in") for j in range(RING)]
        expert_slot_in = [semaphore(f"expert_slot{j}_in") for j in range(RING)]
        const_in = semaphore("const_in")
        x_in = semaphore("x_in")
        tile_done = semaphore("tile_done")
        rounds_ready = semaphore("rounds_ready")
        expert_slots = semaphore("expert_slots")
        experts_done = semaphore("experts_done")
        o_final = semaphore("o_final")
        square_ready = semaphore("square_ready")
        sumsq_ps = semaphore("sumsq_ps")
        u_ready = semaphore("u_ready")
        small_in = semaphore("small_in")
        small_ps = semaphore("small_ps")
        glr_ready = semaphore("glr_ready")
        gk_ps = semaphore("gk_ps")
        logd_ready = semaphore("logd_ready")
        cum_ps = semaphore("cum_ps")
        vk_ps = semaphore("vk_ps")
        grow_taken = semaphore("grow_taken")
        vk_taken = semaphore("vk_taken")
        grow_ps = semaphore("grow_ps")
        pt_ready = semaphore("pt_ready")
        o_taken = semaphore("o_taken")
        qg_ready = semaphore("qg_ready")
        state_in = semaphore("state_in")
        o_ps = semaphore("o_ps")
        scores_ps = semaphore("scores_ps")
        vmask_ready = semaphore("vmask_ready")
        vmask_used = semaphore("vmask_used")
        state_new = semaphore("state_new")
        osq_ready = semaphore("osq_ready")
        osum_ps = semaphore("osum_ps")
        cross_zero = semaphore("cross_zero")
        kt_ready = semaphore("kt_ready")
        cross_ps = semaphore("cross_ps")
        sub_ready = semaphore("sub_ready")
        sub_ps = semaphore("sub_ps")
        band_ready = semaphore("band_ready")
        spread_ps = semaphore("spread_ps")
        qksq_ready = semaphore("qksq_ready")
        qksum_ps = semaphore("qksum_ps")
        qk_ready = semaphore("qk_ready")
        beta_ps = semaphore("beta_ps")
        kb_ready = semaphore("kb_ready")
        kk_ps = semaphore("kk_ps")
        mask_s_ready = semaphore("mask_s_ready")
        inv_s_ready = semaphore("inv_s_ready")
        p_s_ps = semaphore("p_s_ps")
        p_s_ready = semaphore("p_s_ready")
        x_s_ps = semaphore("x_s_ps")
        mask_ready = semaphore("mask_ready")
        inv_ready = semaphore("inv_ready")
        p_ps = semaphore("p_ps")
        p_ready = semaphore("p_ready")
        x_ps = semaphore("x_ps")
        vn0_ps = semaphore("vn0_ps")
        kbg_ready = semaphore("kbg_ready")
        ks_ps = semaphore("ks_ps")
        vn0_ready = semaphore("vn0_ready")
        r1_ps = semaphore("r1_ps")
        ks_ready = semaphore("ks_ready")
        kst_ps = semaphore("kst_ps")
        r1_ready = semaphore("r1_ready")
        vn1_ps = semaphore("vn1_ps")
        vn1_ready = semaphore("vn1_ready")
        rot_ps = semaphore("rot_ps")
        rope_ready = semaphore("rope_ready")
        conv_ready = semaphore("conv_ready")
        hid_ready = semaphore("hid_ready")
        router_in = semaphore("router_in")
        logit_ps = semaphore("logit_ps")
        utok_ps = semaphore("utok_ps")
        sel_ready = semaphore("sel_ready")
        utok_ready = semaphore("utok_ready")
        pos_ps = semaphore("pos_ps")
        pos_ready = semaphore("pos_ready")
        rows_taken = semaphore("rows_taken")
        rows_ps = semaphore("rows_ps")
        gather_ready = semaphore("gather_ready")
        gather_ps = semaphore("gather_ps")
        xg_ready = semaphore("xg_ready")
        ehid_ready = semaphore("ehid_ready")
        scatter_ready = semaphore("scatter_ready")
        y_taken = semaphore("y_taken")
        scatter_ps = semaphore("scatter_ps")
        expert_added = semaphore("expert_added")
        ple_loaded = semaphore("ple_loaded")
        stream_act = semaphore("stream_act")
        stream_ple = semaphore("stream_ple")
        cum_taken_dve = semaphore("cum_taken_dve")
        cum_taken_act = semaphore("cum_taken_act")
        acc_ready = semaphore("acc_ready")
        ffn_added = semaphore("ffn_added")
        stream_dve = semaphore("stream_dve")
        rt_ready = semaphore("rt_ready")
        abs_small = semaphore("abs_small")
        abs_gate = semaphore("abs_gate")
        act_step = semaphore("act_step")
        logs_ready = semaphore("logs_ready")
        rows_saved = semaphore("rows_saved")
        gate_tanh = semaphore("gate_tanh")
        y_ready = semaphore("y_ready")
        ort_ready = semaphore("ort_ready")
        decay_ready = semaphore("decay_ready")
        eg_ready = semaphore("eg_ready")
        convsum_ready = semaphore("convsum_ready")
        ctan_ready = semaphore("ctan_ready")
        qd_ready = semaphore("qd_ready")
        qe_ready = semaphore("qe_ready")
        e_ready = semaphore("e_ready")
        diff_ready = semaphore("diff_ready")
        ediff_ready = semaphore("ediff_ready")
        qkrt_ready = semaphore("qkrt_ready")
        tanh_ready = semaphore("tanh_ready")
        shifted_ready = semaphore("shifted_ready")
        expw_ready = semaphore("expw_ready")
        etanh_ready = semaphore("etanh_ready")
        gate_used = semaphore("gate_used")
        dve_step = semaphore("dve_step")
        stp_out = semaphore("stp_out")
        state_decayed = semaphore("state_decayed")
        pads_ready = semaphore("pads_ready")
        qk_prod = semaphore("qk_prod")
        mt_ready = semaphore("mt_ready")
        esilu_ready = semaphore("esilu_ready")
        round_step = semaphore("round_step")
        state_out = semaphore("state_out")
        conv_out = semaphore("conv_out")
        y_out = semaphore("y_out")

        def sb(name, cols, dt=F32):
            return ctx.enter_context(nc.sbuf_tensor(name, [P, cols], dt))

        h = sb("h", KD * TOK)[:, :].rearrange("p (k t) -> p k t", k=KD)
        u = sb("u", KD * TOK)[:, :].rearrange("p (k t) -> p k t", k=KD)
        acc_t = sb("acc", KD * TOK)
        acc = acc_t[:, :].rearrange("p (k t) -> p k t", k=KD)
        ring = sb("ring", RING * TILE)
        const = sb("const", NCONST)
        pv = sb("pv", NPV)
        wsm = sb("wsm", 8 * 32)[:, :].rearrange("p (k c) -> p k c", k=KD)
        wgk = sb("wgk", 256)
        rows = sb("rows", 32)
        used = NCONST + 3 * KD * TOK + RING * TILE + NPV + 256 + 256 + 32
        arena = sb("arena", 212600 // 4 - used - 8)
        at = [0]

        def carve(cols):
            at[0] += cols
            assert at[0] <= 212600 // 4 - used - 8, at[0]
            return arena[:, at[0] - cols:at[0]]

        def C(name, a=0, b=None):
            o, w = CAT[name]
            return const[:, o + a:o + (w if b is None else b)]

        def PVc(name, k=0):
            return pv[:, PV[name][0] + k:PV[name][0] + k + 1]

        ps_t = ctx.enter_context(nc.psum_tensor("ps", [P, 8, 512], F32))

        def bank(k):
            return ps_t[:, k, :]

        M = 2

        zset = [carve(12 * ZW).rearrange("p (b w) -> p b w", w=ZW) for _ in range(2)]
        mg = carve(KD * TOK).rearrange("p (k t) -> p k t", k=KD)
        cv = carve(KD * TOK).rearrange("p (k t) -> p k t", k=KD)
        vtok = carve(3 * 512).rearrange("p (b c) -> p b c", b=3)
        kdec = carve(3 * 512).rearrange("p (b c) -> p b c", b=3)
        st = carve(2048)
        stp = carve(256)
        vmask = carve(1024)
        pt = carve(4 * PAIR).rearrange("p (h c) -> p h c", h=4)
        xs, ab, ls, gcol, kde = [carve(48).rearrange("p (b c) -> p b c", b=3) for _ in range(5)]
        ea = carve(16)
        egp = carve(4 * SAMP).rearrange("p (q t) -> p q t", q=4)
        qg = carve(4 * SAMP).rearrange("p (q t) -> p q t", q=4)
        tmp4 = carve(4 * TOK).rearrange("p (k t) -> p k t", k=4)
        rs4 = carve(4 * TOK).rearrange("p (k t) -> p k t", k=4)
        csave = carve(14 * 27).rearrange("p (b c) -> p b c", b=14)
        hist = carve(14 * 24).rearrange("p (b c) -> p b c", b=14)
        brt = carve(2 * TOK).rearrange("p (k t) -> p k t", k=2)
        shared = at[0]
        glrt = carve(TOK)
        gx = carve(3 * 256).rearrange("p (b c) -> p b c", b=3)
        gt = carve(2 * TOK).rearrange("p (q t) -> p q t", q=2)
        qt = carve(2 * 256).rearrange("p (q t) -> p q t", q=2)
        ex = carve(2 * 480).rearrange("p (a q t) -> p a q t", a=2, q=2)
        kt = ex
        dd = tmp4.rearrange("p (a q) t -> p a q t", a=2)
        qk = rs4.rearrange("p (a q) t -> p a q t", a=2)
        band = brt
        dtmp = carve(TOK)
        gkd = kdec
        at[0] = shared
        dmat = carve(8 * PAIR).rearrange("p (h c) -> p h c", h=8)
        at[0] = shared + 4 * PAIR
        xm = rs4.rearrange("p k t -> p (k t)")[:, 0:1024].rearrange("p (h b c) -> p h b c", h=4, b=2)
        xt = carve(1024).rearrange("p (h b c) -> p h b c", h=4, b=2)
        msk = tmp4.rearrange("p k t -> p (k t)")[:, 0:1024].rearrange("p (h b c) -> p h b c", h=4, b=2)
        pb = vmask.rearrange("p (h b c) -> p h b c", h=4, b=2)
        kb = carve(2 * TOK).rearrange("p (q t) -> p q t", q=2)
        kbg = carve(2 * SAMP).rearrange("p (q t) -> p q t", q=2)
        xs_s, xt_s, ms_s, pb_s = [carve(128).rearrange("p (h c) -> p h c", h=4) for _ in range(4)]
        at[0] = 0
        hid = carve(NF * TOK).rearrange("p (f t) -> p f t", f=NF)
        at[0] = 12 * 2 * ZW
        tanh_t = carve(2 * TOK).rearrange("p (a t) -> p a t", a=2)
        silu_t = carve(2 * TOK).rearrange("p (a t) -> p a t", a=2)
        at[0] = 12 * 2 * ZW + KD * TOK
        ple_in = carve(2 * TOK).rearrange("p (k t) -> p k t", k=2)
        ple_pj = hid[:, 0:KD, :]
        at[0] = 12 * 2 * ZW + 2 * KD * TOK
        utok = carve(3 * D_MODEL).rearrange("p (b c) -> p b c", b=3)
        rank_t, less_t = [carve(3 * 64).rearrange("p (b e f) -> p b e f", b=3, e=8) for _ in range(2)]
        logit, sel, wts, posm = [carve(3 * 8).rearrange("p (b e) -> p b e", b=3) for _ in range(4)]
        mx = carve(4)
        nrt = carve(1).bitcast(I32)
        cnt = carve(8)
        slotrow, slotcol = carve(P), carve(1)
        gath = carve(3 * P).rearrange("p (b c) -> p b c", b=3)
        scat = carve(TOK)
        yt = carve(D_MODEL)
        router = carve(64).rearrange("p (k e) -> p k e", k=KD)
        at[0] = 0
        posrow, wrow = [carve(NE * TOK).rearrange("p (e t) -> p e t", e=NE) for _ in range(2)]
        ehid = carve(NF * P).rearrange("p (f c) -> p f c", f=NF)
        at[0] = 12 * 2 * ZW
        etanh, esilu = [carve(2 * P).rearrange("p (a t) -> p a t", a=2) for _ in range(2)]
        xg = carve(KD * P).rearrange("p (k c) -> p k c", k=KD)

        cbuf = pt.rearrange("p h c -> p (h c)")[:, 0:640].rearrange("p (a c) -> p a c", a=2)
        ctan = pt.rearrange("p h c -> p (h c)")[:, 640:1280].rearrange("p (a c) -> p a c", a=2)

        class Steps:

            def __init__(self):
                self.n = 0

            def next(self):
                self.n += 1
                return self.n

        def zblk(n, b):
            return zset[n % 2][:, b, :]

        def ob(n, hh):
            if n == SSD:
                return zblk(n, hh // 2)[64 * (hh % 2):64 * (hh % 2) + 64, 0:TOK]
            return zblk(n, OUT0[n] + hh)[:, 0:TOK]

        def qk_of(n, hh):
            half, pair = half_pair(n, hh)
            r = slice(64 * half, 64 * half + 64)
            if n == GDN:
                return cv[r, 2 + pair, :], cv[r, pair, :]
            if n == SSD:
                return cv[r, 4, :], cv[r, 5, :]
            return zblk(n, 2 + pair)[r, 0:TOK], zblk(n, pair)[r, 0:TOK]

        def st_of(n):
            return st.rearrange("p (q b v) -> p q b v", b=NSEQ, v=DV[n])

        def pads(rows_first):
            return [(P, slice(0, 2)), (SAMP, slice(2, 3))]

        block = ctx.enter_context(nc.Block())

        @block.sync
        def _(sp):
            sp.dma_start(const[:, :], io["const"]).then_inc(const_in, 16)
            sp.dma_start(h.rearrange("p k t -> p (k t)"), io["x"]).then_inc(x_in, 16)
            def plain(lo, hi):
                for t in range(lo, hi):
                    if t >= RING:
                        sp.wait_ge(tile_done, t - RING + 1)
                    row = t if t < EXPERT_AT else t + NE * E_TILES
                    sp.dma_start(ring[:, (t % RING) * TILE:(t % RING + 1) * TILE],
                                 io["stream"][row]).then_inc(slot_in[t % RING], 16)

            plain(0, RING)
            turns = EXPERT_AT // RING
            with sp.Fori(1, turns) as g:
                for j in range(RING):
                    sp.wait_ge(tile_done, (g - 1) * RING + (j + 1))
                    sp.dma_start(ring[:, j * TILE:(j + 1) * TILE],
                                 io["stream"][bass.ds(g * RING + j, 1)].rearrange("a p c -> p (a c)")
                                 ).then_inc(slot_in[j], 16)
            plain(turns * RING, EXPERT_AT)
            sp.wait_ge(rounds_ready, 1)
            rounds = sp.value_load(nrt[0:1, 0:1], min_val=1, max_val=3)
            with sp.Fori(0, rounds) as r:
                with sp.Fori(0, NE) as e:
                    for k in range(E_TILES):
                        j = k % RING
                        sp.wait_ge(expert_slots, r * (NE * E_TILES) + e * E_TILES + (k + 1))
                        sp.dma_start(ring[:, j * TILE:(j + 1) * TILE],
                                     io["stream"][bass.ds(e * E_TILES + (EXPERT_AT + k), 1)].rearrange("a p c -> p (a c)")
                                     ).then_inc(expert_slot_in[j], 16)
            sp.wait_ge(experts_done, 1)
            plain(EXPERT_AT, len(PLAIN))

        @block.tensor
        def _(pe):
            mm = nc.tensor.matmul

            def weights(x):
                t = T_OF[x]
                pe.wait_ge(slot_in[t % RING], 16 * (t // RING + 1))
                return [ring[:, (t % RING) * TILE + P * i:(t % RING) * TILE + P * i + P] for i in range(8)]

            def stream_tile(x):
                t = T_OF[x]
                kind, L, n, b = x
                both = kind in ("br", "pproj") or PLAIN[t - 1][0] in ("br", "pproj")
                last = t if both else t - 1
                if taken_before(last, "act") > 0:
                    pe.wait_ge(stream_act, taken_before(last, "act"))
                if taken_before(last, "dve") > 0:
                    pe.wait_ge(stream_dve, taken_before(last, "dve"))
                if taken_before(last, "ple") > 0:
                    pe.wait_ge(stream_ple, taken_before(last, "ple"))
                if kind == "br":
                    pe.wait_ge(o_final, 4 * L + n + 1)
                w = weights(x)
                if kind in ("z", "mg", "pgate"):
                    for k in range(KD):
                        last = mm(bank(t % 2)[:, 0:TOK], w[k], u[:, k, :], start=k == 0, stop=k == KD - 1)
                elif kind == "br":
                    for o in range(2):
                        for k in range(4):
                            src = zblk(n, (0 if n == SSD else OUT0[n]) + k)[:, 0:TOK]
                            last = mm(bank(o)[:, 0:TOK], w[4 * o + k], src, start=k == 0, stop=k == 3)
                elif kind == "out":
                    for k in range(KD):
                        last = mm(bank(t % 2)[:, 0:TOK], w[k], acc[:, k, :], start=k == 0, stop=k == KD - 1)
                elif kind == "pproj":
                    for o in range(4):
                        for k in range(2):
                            last = mm(bank(M + o)[:, 0:TOK], w[2 * o + k], ple_in[:, k, :], start=k == 0, stop=k == 1)
                last.then_inc(tile_done, 1)

            def fill(L, n, s):
                for x in FILL[L][n][s]:
                    stream_tile(x)

            def norm(k, final=False):
                pe.wait_ge(square_ready, k + 1)
                for i in range(KD):
                    last = mm(bank(M)[:, 0:TOK], C("ones"), acc[:, i, :], start=i == 0, stop=i == KD - 1)
                last.then_inc(sumsq_ps, 1)
                if not final:
                    pe.wait_ge(u_ready, k + 1)

            def pair_scores(dst, lhs, rhs):
                for n_rows, i0, i1, c0 in SEGS:
                    j0 = {0: 0, 256: 128, 384: 256}[c0]
                    last = mm(dst[0:n_rows, c0:c0 + i1 - i0], lhs[:, j0:j0 + n_rows], rhs[:, i0:i1],
                              start=True, stop=True)
                return last

            def prep(L):
                pe.wait_ge(small_in, 16 * 5 * (L + 1))
                for k in range(KD):
                    mm(bank(M)[0:16, 0:TOK], wsm[:, k, 0:16], u[:, k, :], start=k == 0, stop=k == KD - 1)
                for b, (t0, nt) in enumerate(TB):
                    for k in range(KD):
                        last = mm(bank(M + 1)[0:nt, 16 * b:16 * b + 16], u[:, k, t0:t0 + nt], wsm[:, k, 16:32],
                                  start=k == 0, stop=k == KD - 1)
                last.then_inc(small_ps, 1)
                pe.wait_ge(glr_ready, L + 1)
                for b, (t0, nt) in enumerate(TB):
                    last = mm(bank(M + 2 + b // 2)[0:nt, 256 * (b % 2):256 * (b % 2) + 256],
                              glrt[0:17, t0:t0 + nt], wgk[0:17, :], start=True, stop=True)
                last.then_inc(gk_ps, 1)
                for b in range(4, ZBLOCKS[0]):
                    stream_tile(("z", L, 0, b))
                pe.wait_ge(logd_ready, L + 1)
                up, af, on = C("upto", 0, 128), C("after"), C("ones")
                g, r = bank(M), bank(M)[:, 48:96]
                mm(g[:, 0:16], up, ls[:, 0, :], start=True, stop=True)
                mm(g[:, 16:32], on, ls[:, 0, :], start=True, stop=False)
                mm(g[:, 16:32], up, ls[:, 1, :], start=False, stop=True)
                mm(g[0:32, 32:48], C("upto_s")[0:32], ls[0:32, 2, :], start=True, stop=True)
                mm(r[:, 0:16], on, ls[:, 1, :], start=True, stop=False)
                mm(r[:, 0:16], af, ls[:, 0, :], start=False, stop=True)
                mm(r[:, 16:32], af, ls[:, 1, :], start=True, stop=True)
                mm(r[0:32, 32:48], C("after_s")[0:32], ls[0:32, 2, :], start=True, stop=True)
                mm(bank(M + 1)[:, 0:256], on, gx[:, 1, :], start=True, stop=False)
                mm(bank(M + 1)[:, 0:256], af, gx[:, 0, :], start=False, stop=True)
                mm(bank(M + 1)[:, 256:512], af, gx[:, 1, :], start=True, stop=True)
                mm(bank(M + 2)[0:32, 0:256], C("after_s")[0:32], gx[0:32, 2, :], start=True, stop=True)
                for q in range(2):
                    c = slice(128 * q, 128 * q + 128)
                    d = bank(M + 3 + q)
                    mm(d[:, 0:256], gx[:, 0, c], C("upto"), start=True, stop=True)
                    mm(d[:, 128:256], gx[:, 1, c], up, start=False, stop=True, skip_group_check=True)
                    last = mm(d[:, 256:288], gx[0:32, 2, c], C("upto_s")[0:32], start=False, stop=True,
                              skip_group_check=True)
                last.then_inc(cum_ps, 1)

            def transposes(L, n):
                tr = nc.tensor.transpose
                for b, (t0, nt) in enumerate(TB):
                    for c in range(4):
                        if n == GDN:
                            src = cv[:, 4 + c, t0:t0 + nt]
                        elif n == SSD:
                            src = cv[:, c, t0:t0 + nt]
                        else:
                            src = zblk(n, 4 + c)[:, t0:t0 + nt]
                        tr(bank(M + b)[0:nt, 128 * c:128 * c + 128], src, C("ident"))
                    for c in range(1 if n == SSD else 2):
                        ksrc = {GDN: cv[:, 2 + c, :], SSD: cv[:, 4, :]}.get(n, None)
                        if ksrc is None:
                            ksrc = zblk(n, 2 + c)[:, 0:TOK]
                        last = tr(bank(M + 3 + b // 2)[0:nt, 256 * (b % 2) + 128 * c:256 * (b % 2) + 128 * c + 128],
                                  ksrc[:, t0:t0 + nt], C("ident"))
                last.then_inc(vk_ps, 1)

            def decays(L, n):
                for hh in range(HEADS[n]):
                    k = L * 12 + (hh if n == GDN else 4 + hh)
                    if hh >= 2:
                        pe.wait_ge(grow_taken, k - 1)
                    else:
                        pe.wait_ge(vk_taken, 4 * L + n + 1)
                    d = bank(M + 2 + hh % 2)
                    c = SSD_COL[n] + hh
                    mm(d[:, 0:256], ls[:, 0, c:c + 1].to_broadcast([P, P]), C("upto"), start=True, stop=True)
                    mm(d[:, 128:256], ls[:, 1, c:c + 1].to_broadcast([P, P]), C("upto", 0, 128),
                       start=False, stop=True, skip_group_check=True)
                    mm(d[:, 256:288], ls[0:32, 2, c:c + 1].to_broadcast([32, P]), C("upto_s")[0:32],
                       start=False, stop=True, skip_group_check=True).then_inc(grow_ps, 1)
                    if hh % 2:
                        fill(L, n, 4 + hh // 2)

            def core(L, n, slot):
                m, dv = 4 * L + n, DV[n]

                def outputs(hh):
                    half, pair = half_pair(n, hh)
                    kr = slice(64 * half, 64 * half + 64)
                    orow = slice(64 * (hh % 2), 64 * (hh % 2) + 64) if n == SSD else slice(0, P)
                    gh = L * NHEAD + HBASE[n] + hh
                    pe.wait_ge(pt_ready, gh + 1)
                    if (gh - 1 if hh >= 2 else gh - hh) > 0:
                        pe.wait_ge(o_taken, gh - 1 if hh >= 2 else gh - hh)
                    if hh == 0:
                        pe.wait_ge(qg_ready, m + 1)
                        pe.wait_ge(state_in, 16 * (m + 1))
                    o = bank(M + 4 + ((hh // 2) if n == SSD else hh) % 2)[orow, :]
                    if n == SSD and hh >= 4:
                        pe.wait_ge(o_taken, gh - gh % 2 - 2)
                    p = pt[:, hh % 4, :]
                    v = [vtok[0:nt, b, dv * hh:dv * hh + dv] for b, (t0, nt) in enumerate(TB)]
                    mm(o[:, 0:256], v[0], p[:, 0:256], start=True, stop=True)
                    mm(o[:, 128:256], v[1], p[:, 256:384], start=False, stop=True, skip_group_check=True)
                    mm(o[:, 256:288], v[2], p[0:32, 384:416], start=False, stop=False, skip_group_check=True)
                    for b in range(NSEQ):
                        last = mm(o[:, 256 + 4 * b:260 + 4 * b], st_of(n)[kr, pair, b, :],
                                  qg[kr, pair, 4 * b:4 * b + 4], start=False, stop=True, skip_group_check=True)
                    last.then_inc(o_ps, 1)

                for hh in range(HEADS[n]):
                    gh = L * NHEAD + HBASE[n] + hh
                    if n != GLA:
                        kT, qT = qk_of(n, hh)
                        if hh >= 2:
                            pe.wait_ge(pt_ready, gh - 1)
                        else:
                            pe.wait_ge(qg_ready, m + 1)
                        pair_scores(bank(M + hh % 2), kT, qT).then_inc(scores_ps, 1)
                        if hh >= 1:
                            outputs(hh - 1)
                    else:
                        outputs(hh)
                    fill(L, n, slot + hh)
                if n != GLA:
                    outputs(HEADS[n] - 1)

            def states(L, n):
                m, dv = 4 * L + n, DV[n]
                kd = kdec.rearrange("p b c -> p (b c)")
                for hh in range(HEADS[n]):
                    half, pair = half_pair(n, hh)
                    r = slice(64 * half, 64 * half + 64)
                    gh = L * NHEAD + HBASE[n] + hh
                    if hh == 0:
                        pe.wait_ge(o_taken, L * NHEAD + HBASE[n] + HEADS[n])
                    kc = slice(64 * hh, 64 * hh + 64)
                    o = bank(M + 4)[r, dv * pair:dv * pair + dv]
                    mm(o, kdec[:, 0, kc], vtok[:, 0, dv * hh:dv * hh + dv], start=True, stop=False)
                    mm(o, kdec[:, 1, kc], vtok[:, 1, dv * hh:dv * hh + dv], start=False, stop=True)
                    pe.wait_ge(vmask_ready, gh + 1)
                    vm = vmask[0:32, 0:NSEQ * dv]
                    if n == SSD:
                        last = mm(bank(M + pair)[r, :], kdec[0:32, 2, kc],
                                  vmask[0:32, 512 * (hh % 2):512 * (hh % 2) + 512], start=True, stop=True)
                    else:
                        for g in range(2):
                            last = mm(bank(M + 2 * pair + g)[r, :], kdec[0:32, 2, kc],
                                      vmask[0:32, 512 * g:512 * g + 512], start=True, stop=True)
                    last.then_inc(vmask_used, 1)

            def out_norm(L, n):
                m = 4 * L + n
                pe.wait_ge(state_new, m + 1)
                pe.wait_ge(osq_ready, m + 1)
                if n == SSD:
                    for g in range(2):
                        for b in range(2):
                            last = mm(bank(M + g)[:, 0:TOK], C("ones"), tmp4[:, 2 * g + b, :], start=b == 0, stop=b == 1)
                else:
                    for b in range(4):
                        last = mm(bank(M + b)[:, 0:TOK], C("ones"), tmp4[:, b, :], start=True, stop=True)
                last.then_inc(osum_ps, 1)

            def gla(L):
                m = 4 * L
                pe.wait_ge(cross_zero, L + 1)
                for a in range(1, 16):
                    pe.wait_ge(kt_ready, L * 15 + a)
                    for hh in range(4):
                        r = slice(64 * (hh % 2), 64 * (hh % 2) + 64)
                        q = qt[r, hh // 2, 16 * a:16 * a + 16]
                        k = kt[:, a % 2, hh // 2, :][r, :]
                        d = bank(M + hh)
                        if a <= 8:
                            last = mm(d[0:16 * a, 16 * a:16 * a + 16] if a < 8 else d[:, 128:144], k[:, 0:16 * a], q,
                                      start=True, stop=True)
                        else:
                            mm(d[:, 16 * a:16 * a + 16], k[:, 0:128], q, start=True, stop=True)
                            w = 16 * a - 128
                            last = mm(d[0:w, 256 + w:272 + w], k[:, 128:16 * a], q, start=True, stop=True)
                    last.then_inc(cross_ps, 1)
                    fill(L, GLA, a - 1)
                for jj in range(16):
                    pe.wait_ge(sub_ready, 16 * L + jj + 1)
                    for q in range(2):
                        last = mm(bank(M + 4 + q)[0:32, 0:TOK], C("row_pick", 15 - jj, 47 - jj), dd[:, jj % 2, q, :],
                                  start=jj == 0, stop=jj == 15)
                    last.then_inc(sub_ps, 1)
                    fill(L, GLA, 15 + jj)
                pe.wait_ge(band_ready, L + 1)
                for hh in range(4):
                    if hh >= 2:
                        pe.wait_ge(pt_ready, L * NHEAD + hh - 1)
                    d = bank(M + 4 + hh % 2)
                    mm(d[:, 0:256], C("spread", 128 * (hh % 2), 128 * (hh % 2) + 128)[0:32], band[0:32, hh // 2, 0:256],
                       start=True, stop=True)
                    mm(d[0:32, 256:288], C("spread_s", 32 * (hh % 2), 32 * (hh % 2) + 32)[0:32],
                       band[0:32, hh // 2, 256:288], start=True, stop=True).then_inc(spread_ps, 1)
                fill(L, GLA, 31)
                pe.wait_ge(pt_ready, L * NHEAD + 4)
                core(L, GLA, 32)
                states(L, GLA)
                fill(L, GLA, 36)
                out_norm(L, GLA)
                fill(L, GLA, 37)

            def gdn(L):
                pe.wait_ge(qksq_ready, L + 1)
                for b in range(4):
                    last = mm(bank(M + b)[:, 0:TOK], C("halfones"), tmp4[:, b, :], start=True, stop=True)
                last.then_inc(qksum_ps, 1)
                fill(L, GDN, 1)
                pe.wait_ge(qk_ready, L + 1)
                transposes(L, GDN)
                fill(L, GDN, 2)
                pe.wait_ge(vk_taken, 4 * L + GDN + 1)
                for hh in range(4):
                    r = slice(64 * (hh % 2), 64 * (hh % 2) + 64)
                    for b, (t0, nt) in enumerate(TB):
                        last = mm(bank(M + 4 + hh // 2)[r, t0:t0 + nt], ls[0:nt, b, hh:hh + 1].to_broadcast([nt, 64]),
                                  C("ident")[0:nt, 0:nt], start=True, stop=True)
                last.then_inc(beta_ps, 1)
                fill(L, GDN, 3)
                decays(L, GDN)
                pe.wait_ge(kb_ready, L + 1)
                pe.wait_ge(grow_taken, 12 * L + 4)
                for hh in range(4):
                    r = slice(64 * (hh % 2), 64 * (hh % 2) + 64)
                    pair_scores(bank(M + hh), cv[r, 2 + hh // 2, :], kb[r, hh // 2, :]).then_inc(kk_ps, 1)
                fill(L, GDN, 6)
                for lv in range(2):
                    pe.wait_ge(mask_s_ready, 2 * L + lv + 1)
                    pe.wait_ge(inv_s_ready, 3 * L + lv + 1)
                    for hh in range(4):
                        last = mm(bank(M + 4)[0:32, 32 * hh:32 * hh + 32], ms_s[0:32, hh, :], xs_s[0:32, hh, :],
                                  start=True, stop=True)
                    last.then_inc(p_s_ps, 1)
                    pe.wait_ge(p_s_ready, 2 * L + lv + 1)
                    for hh in range(4):
                        mm(bank(M + 4)[0:32, 128 + 32 * hh:160 + 32 * hh], xt_s[0:32, hh, :], pb_s[0:32, hh, :],
                           start=True, stop=True)
                        last = mm(bank(M + 4)[0:32, 256 + 32 * hh:288 + 32 * hh], pb_s[0:32, hh, :], xt_s[0:32, hh, :],
                                  start=True, stop=True)
                    last.then_inc(x_s_ps, 1)
                    fill(L, GDN, 7 + lv)
                pe.wait_ge(inv_s_ready, 3 * L + 3)
                for lv in range(7):
                    pe.wait_ge(mask_ready, 7 * L + lv + 1)
                    pe.wait_ge(inv_ready, 8 * L + lv + 1)
                    for g in range(8):
                        last = mm(bank(M + g // 4)[:, 128 * (g % 4):128 * (g % 4) + 128], msk[:, g // 2, g % 2, :],
                                  xm[:, g // 2, g % 2, :], start=True, stop=True)
                    last.then_inc(p_ps, 1)
                    fill(L, GDN, 9 + 2 * lv)
                    pe.wait_ge(p_ready, 7 * L + lv + 1)
                    for g in range(8):
                        c = slice(128 * (g % 4), 128 * (g % 4) + 128)
                        mm(bank(M + 2 + g // 4)[:, c], xt[:, g // 2, g % 2, :], pb[:, g // 2, g % 2, :],
                           start=True, stop=True)
                        last = mm(bank(M + 4 + g // 4)[:, c], pb[:, g // 2, g % 2, :], xt[:, g // 2, g % 2, :],
                                  start=True, stop=True)
                    last.then_inc(x_ps, 1)
                    fill(L, GDN, 10 + 2 * lv)
                pe.wait_ge(inv_ready, 8 * L + 8)
                for hh in range(4):
                    last = mm(bank(M)[:, 128 * hh:128 * hh + 128], xt[:, hh, 0, :], vtok[:, 0, 128 * hh:128 * hh + 128],
                              start=True, stop=True)
                last.then_inc(vn0_ps, 1)
                pe.wait_ge(kbg_ready, L + 1)
                pe.wait_ge(state_in, 16 * (4 * L + GDN + 1))
                for hh in range(4):
                    r = slice(64 * (hh % 2), 64 * (hh % 2) + 64)
                    for b in range(NSEQ):
                        last = mm(bank(M + 1 + 4 * (hh % 2))[:, 32 * (hh // 2) + 4 * b:32 * (hh // 2) + 4 * b + 4], st_of(GDN)[r, hh // 2, b, :],
                                  kbg[r, hh // 2, 4 * b:4 * b + 4], start=True, stop=True)
                last.then_inc(ks_ps, 1)
                fill(L, GDN, 23)
                pe.wait_ge(vn0_ready, L + 1)
                for hh in range(4):
                    last = mm(bank(M + 2)[:, 128 * hh:128 * hh + 128], pt[:, hh, 128:256],
                              vtok[:, 0, 128 * hh:128 * hh + 128], start=True, stop=True)
                last.then_inc(r1_ps, 1)
                pe.wait_ge(ks_ready, L + 1)
                for hh in range(4):
                    last = nc.tensor.transpose(bank(M + 3)[0:32, 128 * hh:128 * hh + 128],
                                               pb.rearrange("p h b c -> p (h b c)")[:, 32 * hh:32 * hh + 32], C("ident"))
                last.then_inc(kst_ps, 1)
                fill(L, GDN, 24)
                pe.wait_ge(r1_ready, L + 1)
                for hh in range(4):
                    mm(bank(M + 4)[:, 128 * hh:128 * hh + 128], xt[:, hh, 1, :], vtok[:, 1, 128 * hh:128 * hh + 128],
                       start=True, stop=True)
                for hh in range(4):
                    last = mm(bank(M + 5)[0:32, 128 * hh:128 * hh + 128], xt_s[0:32, hh, :],
                              vtok[0:32, 2, 128 * hh:128 * hh + 128], start=True, stop=True)
                last.then_inc(vn1_ps, 1)
                fill(L, GDN, 25)
                pe.wait_ge(vn1_ready, L + 1)
                core(L, GDN, 26)
                states(L, GDN)
                fill(L, GDN, 30)
                out_norm(L, GDN)
                for s in range(31, NSLOT[GDN]):
                    fill(L, GDN, s)

            def ret(L):
                for b in range(4):
                    last = mm(bank(M + b)[:, 0:TOK], C("rot"), zblk(RET, b)[:, 0:TOK], start=True, stop=True)
                last.then_inc(rot_ps, 1)
                fill(L, RET, 0)
                pe.wait_ge(rope_ready, L + 1)
                transposes(L, RET)
                fill(L, RET, 1)
                pe.wait_ge(vk_taken, 4 * L + RET + 1)
                core(L, RET, 2)
                states(L, RET)
                fill(L, RET, 6)
                out_norm(L, RET)
                for s in range(7, NSLOT[RET]):
                    fill(L, RET, s)

            def ssd(L):
                fill(L, SSD, 0)
                pe.wait_ge(conv_ready, 14 * L + 14)
                transposes(L, SSD)
                for s in range(1, 4):
                    fill(L, SSD, s)
                decays(L, SSD)
                core(L, SSD, 8)
                states(L, SSD)
                fill(L, SSD, 16)
                out_norm(L, SSD)
                fill(L, SSD, 17)

            def dense(L):
                norm(3 * L + 1)
                for f in range(NF):
                    for kind in ("gate", "up"):
                        if f - 1 > 0:
                            pe.wait_ge(hid_ready, f - 1)
                        x = (kind, L, 0, f)
                        w = weights(x)
                        for k in range(KD):
                            last = mm(bank(M + 2 * (f % 2) + (kind == "up"))[:, 0:TOK], w[k], u[:, k, :],
                                      start=k == 0, stop=k == KD - 1)
                        last.then_inc(tile_done, 1)
                pe.wait_ge(hid_ready, NF)
                for f in range(NF):
                    w = weights(("down", L, 0, f))
                    for k in range(KD):
                        last = mm(bank(k)[:, 0:TOK], w[k], hid[:, f, :], start=f == 0, stop=f == NF - 1)
                    last.then_inc(tile_done, 1)

            def experts(L):
                norm(3 * L + 1)
                pe.wait_ge(router_in, 16)
                for b, (t0, nt) in enumerate(TB):
                    for k in range(KD):
                        last = mm(bank(M)[0:nt, 8 * b:8 * b + 8], u[:, k, t0:t0 + nt], router[:, k, :],
                                  start=k == 0, stop=k == KD - 1)
                        if b == 0 and k == 0:
                            last.then_inc(expert_slots, RING)
                last.then_inc(logit_ps, 1)
                for b, (t0, nt) in enumerate(TB):
                    for k in range(KD):
                        last = nc.tensor.transpose(bank((M + 1 + 2 * b + k // 4) % 8)[0:nt, P * (k % 4):P * (k % 4) + P],
                                                   u[:, k, t0:t0 + nt], C("ident"))
                last.then_inc(utok_ps, 1)
                pe.wait_ge(sel_ready, 1)
                pe.wait_ge(utok_ready, 1)
                d, before, on = bank(M), C("strict", 0, 128), C("ones")
                mm(d[:, 0:8], before, sel[:, 0, :], start=True, stop=True)
                mm(d[:, 8:16], on, sel[:, 0, :], start=True, stop=False)
                mm(d[:, 8:16], before, sel[:, 1, :], start=False, stop=True)
                for c, nr in ((16, 32), (24, 128)):
                    mm(d[0:nr, c:c + 8], on[:, 0:nr], sel[:, 0, :], start=True, stop=False)
                    mm(d[0:nr, c:c + 8], on[:, 0:nr], sel[:, 1, :], start=False, stop=False)
                    last = mm(d[0:nr, c:c + 8], (before if c == 16 else on)[0:32, 0:nr], sel[0:32, 2, :], start=False, stop=True)
                last.then_inc(pos_ps, 1)
                pe.wait_ge(pos_ready, 1)
                for e in range(NE):
                    if e - 1 > 0:
                        pe.wait_ge(rows_taken, e - 1)
                    for g, src in enumerate((posm, wts)):
                        for b, (t0, nt) in enumerate(TB):
                            last = mm(bank(M + 2 * (e % 2) + g)[:, t0:t0 + nt], src[0:nt, b, e:e + 1].to_broadcast([nt, P]),
                                      C("ident")[0:nt, 0:nt], start=True, stop=True)
                    last.then_inc(rows_ps, 1)
                pe.wait_ge(rows_taken, NE)
                pe.wait_ge(rounds_ready, 1)
                rounds = pe.value_load(nrt[0:1, 0:1], min_val=1, max_val=3)
                with pe.Fori(0, rounds) as r:
                    with pe.Fori(0, NE) as e:
                        it = pe.snap(r * NE + e)

                        def expert_tile(k):
                            pe.wait_ge(expert_slot_in[k % RING], it * (16 * E_TILES // RING) + 16 * (k // RING + 1))
                            o = (k % RING) * TILE
                            return [ring[:, o + P * i:o + P * i + P] for i in range(8)], ring[:, o:o + TILE]

                        pe.wait_ge(gather_ready, it + 1)
                        for k in range(KD):
                            for b, (t0, nt) in enumerate(TB):
                                last = mm(bank(k // 4)[:, P * (k % 4):P * (k % 4) + P], utok[0:nt, b, P * k:P * k + P],
                                          gath[0:nt, b, :], start=b == 0, stop=b == 2)
                        last.then_inc(gather_ps, 1)
                        pe.wait_ge(xg_ready, it + 1)
                        for f in range(NF):
                            if f >= 2:
                                pe.wait_ge(ehid_ready, it * NF + (f - 1))
                            for g in range(2):
                                w, _ = expert_tile(2 * f + g)
                                for k in range(KD):
                                    last = mm(bank(M + 2 * (f % 2) + g)[:, 0:P], w[k], xg[:, k, :], start=k == 0, stop=k == KD - 1)
                                last.then_inc(expert_slots, 1)
                        for f in range(NF):
                            pe.wait_ge(ehid_ready, it * NF + (f + 1))
                            _, w = expert_tile(2 * NF + f)
                            for g in range(2):
                                last = mm(bank(M + 4 + g), ehid[:, f, :], w[:, 512 * g:512 * g + 512], start=f == 0, stop=f == NF - 1)
                            last.then_inc(expert_slots, 1)
                        pe.wait_ge(scatter_ready, it + 1)
                        pe.wait_ge(y_taken, it + 1)
                        for g, b0 in enumerate((M, 0, M + 4)):
                            for k in ((0, 1, 2, 3), (4, 5), (6, 7))[g]:
                                last = mm(bank(b0 + k - (0, 4, 6)[g])[:, 0:TOK], yt[:, P * k:P * k + P], scat, start=True, stop=True)
                            last.then_inc(scatter_ps, 1)
                        pe.wait_ge(expert_added, it + 1)
                mm(bank(0)[0:32, 0:32], C("ident", 0, 32), C("ident", 0, 32), start=True, stop=True).then_inc(experts_done, 1)

            def ple(L):
                pe.wait_ge(ple_loaded, 16 * (L + 1))
                for b in range(2):
                    stream_tile(("pproj", L, 0, b))
                pe.wait_ge(stream_act, taken_before(T_OF[("pproj", L, 0, 1)] + 1, "act"))
                norm(3 * L + 2)
                for b in range(KD):
                    stream_tile(("pgate", L, 0, b))
                pe.wait_ge(stream_ple, taken_before(T_OF[("pgate", L, 0, 7)] + 1, "ple"))

            pe.wait_ge(const_in, 16)
            for L in range(DEPTH):
                norm(3 * L)
                for b in range(4):
                    stream_tile(("z", L, 0, b))
                prep(L)
                pe.wait_ge(cum_taken_dve, L + 1)
                pe.wait_ge(cum_taken_act, L + 1)
                pe.wait_ge(stream_act, taken_before(T_OF[("z", L, 0, 11)] + 1, "act"))
                transposes(L, GLA)
                gla(L)
                pe.wait_ge(o_final, 4 * L + 1)
                pe.wait_ge(stream_act, taken_before(T_OF[("z", L, 1, 11)] + 1, "act"))
                ret(L)
                fill(L, GDN, 0)
                gdn(L)
                ssd(L)
                pe.wait_ge(o_final, 4 * L + 4)
                for b in range(4):
                    stream_tile(("br", L, 3, b))
                pe.wait_ge(acc_ready, L + 1)
                for b in range(KD):
                    stream_tile(("out", L, 0, b))
                dense(L) if L % 2 == 0 else experts(L)
                pe.wait_ge(ffn_added, L + 1)
                ple(L)
            norm(3 * DEPTH, True)

        @block.scalar
        def _(act):
            steps = Steps()
            A = nc.scalar.activation

            def fill(L, n, s):
                for x in FILL[L][n][s]:
                    take(x)

            def take(x):
                kind, L, n, b = x
                if TAKER[kind] != "act":
                    return
                t = T_OF[x]
                act.wait_ge(tile_done, t + 1)
                src = bank(t % 2)
                if kind == "mg":
                    if n > 0:
                        act.wait_ge(stream_dve, taken_before(T_OF[("br", L, n - 1, 3)] + 1, "dve"))
                    elif L > 0:
                        act.wait_ge(stream_dve, taken_before(T_OF[("br", L - 1, 3, 3)] + 1, "dve"))
                    A(mg[:, b, :], src[:, 0:TOK], ACT.Tanh, scale=0.5).then_inc(stream_act, 1)
                elif kind == "pproj":
                    A(ple_pj[:, 4 * b:4 * b + 4, :], ps_t[:, M:M + 4, 0:TOK], ACT.Copy).then_inc(stream_act, 1)
                elif b < NCONV[n]:
                    A(zblk(n, b)[:, 3:259], src[:, 0:SEQ], ACT.Copy)
                    A(zblk(n, b)[:, 259:315].rearrange("p (s w) -> p s w", w=7)[:, :, 3:7],
                      src[:, SEQ:TOK].rearrange("p (s w) -> p s w", w=4), ACT.Copy).then_inc(stream_act, 1)
                else:
                    A(zblk(n, b)[:, 0:TOK], src[:, 0:TOK], ACT.Copy, scale=ZSCALE[n][b]).then_inc(stream_act, 1)

            def norm(k):
                act.wait_ge(sumsq_ps, k + 1)
                A(rs4[:, 0, :], bank(M)[:, 0:TOK], ACT.Sqrt, scale=1.0 / D_MODEL, bias=C("eps")).then_inc(rt_ready, 1)

            def prep(L):
                gab = tmp4.rearrange("p k t -> p (k t)")[:, 0:768].rearrange("p (b c) -> p b c", b=3)
                act.wait_ge(abs_small, L + 1)
                act.wait_ge(small_in, 16 * 5 * (L + 1))
                for r, bs in pads(0):
                    A(ab[0:r, bs, 4:16], ab[0:r, bs, 4:16], ACT.Exp, scale=-1.0)
                    A(ab[0:r, bs, 0:4], xs[0:r, bs, 0:4], ACT.Tanh, scale=0.5)
                act.wait_ge(abs_gate, L + 1)
                for r, bs in pads(0):
                    A(gab[0:r, bs, :], gab[0:r, bs, :], ACT.Exp, scale=-1.0)
                A(ea, rows[:, 16:32], ACT.Exp).then_inc(act_step, 1)
                act.wait_ge(act_step, steps.next())
                for r, bs in pads(0):
                    A(ab[0:r, bs, 4:16], ab[0:r, bs, 4:16], ACT.Ln, bias=1.0)
                    last = A(gab[0:r, bs, :], gab[0:r, bs, :], ACT.Ln, bias=1.0)
                last.then_inc(logs_ready, 1)
                for b in range(4, ZBLOCKS[0]):
                    take(("z", L, 0, b))
                act.wait_ge(cum_ps, L + 1)
                for r, bs in pads(0):
                    b0, b1 = bs.start, bs.stop
                    A(kdec[0:r, bs, 0:256], bank(M + 1 + b0 // 2)[0:r, 0:256 * (b1 - b0)].rearrange("p (b c) -> p b c", c=256),
                      ACT.Exp)
                act.wait_ge(cum_taken_dve, L + 1)
                for r, bs in pads(0):
                    b0, b1 = bs.start, bs.stop
                    A(kde[0:r, bs, 4:16], bank(M)[0:r, 48 + 16 * b0:48 + 16 * b1].rearrange("p (b c) -> p b c", c=16)[:, :, 4:16],
                      ACT.Exp)
                A(egp[:, 0:2, :], gt[:, :, 256:288], ACT.Exp).then_inc(cum_taken_act, 1)

            def core(L, n, slot):
                for hh in range(HEADS[n]):
                    gh = L * NHEAD + HBASE[n] + hh

                    def take_o(q):
                        g = L * NHEAD + HBASE[n] + q
                        act.wait_ge(o_ps, g + 1)
                        r = slice(64 * (q % 2), 64 * (q % 2) + 64) if n == SSD else slice(0, P)
                        src = bank(M + 4 + (q // 2 if n == SSD else q) % 2)[r, 0:TOK]
                        if n in (GDN, SSD) and q == 0:
                            act.wait_ge(rows_saved, 2 * L + (1 if n == GDN else 2))
                        A(ob(n, q), src, ACT.Copy).then_inc(o_taken, 1)

                    if n == GLA:
                        take_o(hh)
                    elif hh >= 1:
                        take_o(hh - 1)
                    fill(L, n, slot + hh)
                if n != GLA:
                    take_o(HEADS[n] - 1)

            def out_norm(L, n, slot):
                m = 4 * L + n
                vt4 = vtok.rearrange("p b c -> p (b c)")[:, 0:4 * TOK].rearrange("p (k t) -> p k t", k=4)
                gates = zset[n % 2][:, GATE0[n]:GATE0[n] + 4, 0:TOK]
                act.wait_ge(vmask_used, L * NHEAD + HBASE[n] + HEADS[n])
                A(vt4, gates, ACT.Tanh).then_inc(gate_tanh, 1)
                o4 = zset[n % 2][:, OUT0[n]:OUT0[n] + 4, 0:TOK]
                if n == SSD:
                    act.wait_ge(y_ready, L + 1)
                else:
                    act.wait_ge(o_taken, L * NHEAD + HBASE[n] + HEADS[n])
                A(tmp4, o4, ACT.Square).then_inc(osq_ready, 1)
                act.wait_ge(osum_ps, m + 1)
                if n == SSD:
                    A(rs4[:, 0:2, :], ps_t[:, M:M + 2, 0:TOK], ACT.Sqrt, scale=1.0 / 256, bias=C("eps")).then_inc(ort_ready, 1)
                else:
                    A(rs4, ps_t[:, M:M + 4, 0:TOK], ACT.Sqrt, scale=1.0 / 128, bias=C("eps")).then_inc(ort_ready, 1)
                fill(L, n, slot)

            def decays(L, n):
                for hh in range(HEADS[n]):
                    k = L * 12 + (hh if n == GDN else 4 + hh)
                    act.wait_ge(grow_taken, k + 1)
                    A(dmat[:, hh, 0:384], dmat[:, hh, 0:384], ACT.Exp)
                    A(dmat[0:32, hh, 384:416], dmat[0:32, hh, 384:416], ACT.Exp).then_inc(decay_ready, 1)
                    if hh % 2:
                        fill(L, n, 4 + hh // 2)
                q = HEADS[n] // 2
                A(egp[:, 0:q, :], egp[:, 0:q, :], ACT.Exp).then_inc(eg_ready, 1)

            def conv(L, n):
                for b in range(NCONV[n]):
                    c = 14 * L + CONV0[n] + b
                    act.wait_ge(convsum_ready, c + 1)
                    if c - 1 > 0:
                        act.wait_ge(conv_ready, c - 1)
                    A(ctan[:, b % 2, 0:312], cbuf[:, b % 2, 0:312], ACT.Tanh).then_inc(ctan_ready, 1)

            def gla(L):
                act.wait_ge(qd_ready, L + 1)
                A(qt[:, :, 16:256], qt[:, :, 16:256], ACT.Exp).then_inc(qe_ready, 1)
                for a in range(1, 16):
                    c = 15 * L + a
                    if c - 2 > 0:
                        act.wait_ge(cross_ps, c - 2)
                    for q in range(2):
                        last = A(ex[:, a % 2, q, 0:16 * a], gt[:, q, 0:16 * a], ACT.Exp, scale=-1.0,
                                 bias=gt[:, q, 16 * a - 1:16 * a])
                    last.then_inc(e_ready, 1)
                    fill(L, GLA, a - 1)
                for jj in range(16):
                    act.wait_ge(diff_ready, 16 * L + jj + 1)
                    for q in range(2):
                        d = dd[:, jj % 2, q, 0:256].rearrange("p (s w) -> p s w", w=16)[:, :, jj:16]
                        last = A(d, d, ACT.Exp)
                    if jj < 4:
                        for q in range(2):
                            d = dd[:, jj % 2, q, 256:288].rearrange("p (s w) -> p s w", w=4)[:, :, jj:4]
                            last = A(d, d, ACT.Exp)
                    last.then_inc(ediff_ready, 1)
                    fill(L, GLA, 15 + jj)
                fill(L, GLA, 31)
                core(L, GLA, 32)
                fill(L, GLA, 36)
                out_norm(L, GLA, 37)

            def ret(L):
                fill(L, RET, 0)
                fill(L, RET, 1)
                core(L, RET, 2)
                fill(L, RET, 6)
                out_norm(L, RET, 7)
                for s in range(8, NSLOT[RET]):
                    fill(L, RET, s)

            def gdn(L):
                fill(L, GDN, 0)
                conv(L, GDN)
                act.wait_ge(conv_ready, 14 * L + 4)
                A(tmp4, cv[:, 0:4, :], ACT.Square).then_inc(qksq_ready, 1)
                act.wait_ge(qksum_ps, L + 1)
                A(rs4, ps_t[:, M:M + 4, 0:TOK], ACT.Sqrt, bias=C("eps")).then_inc(qkrt_ready, 1)
                fill(L, GDN, 1)
                fill(L, GDN, 2)
                fill(L, GDN, 3)
                decays(L, GDN)
                fill(L, GDN, 6)
                for lv in range(2):
                    act.wait_ge(p_s_ps, 2 * L + lv + 1)
                    A(pb_s[0:32], bank(M + 4)[0:32, 0:128].rearrange("p (h c) -> p h c", h=4),
                      ACT.Copy).then_inc(p_s_ready, 1)
                    fill(L, GDN, 7 + lv)
                for lv in range(7):
                    act.wait_ge(p_ps, 7 * L + lv + 1)
                    A(pb.rearrange("p h b c -> p (h b c)").rearrange("p (k c) -> p k c", k=2), ps_t[:, M:M + 2, :],
                      ACT.Copy).then_inc(p_ready, 1)
                    fill(L, GDN, 9 + 2 * lv)
                    fill(L, GDN, 10 + 2 * lv)
                for s in (23, 24, 25):
                    fill(L, GDN, s)
                core(L, GDN, 26)
                fill(L, GDN, 30)
                out_norm(L, GDN, 31)
                for s in range(32, NSLOT[GDN]):
                    fill(L, GDN, s)

            def ssd(L):
                conv(L, SSD)
                fill(L, SSD, 0)
                for s in range(1, 4):
                    fill(L, SSD, s)
                decays(L, SSD)
                core(L, SSD, 8)
                fill(L, SSD, 16)
                out_norm(L, SSD, 17)

            def dense(L):
                for f in range(NF):
                    act.wait_ge(tile_done, T_OF[("gate", L, 0, f)] + 1)
                    if f - 1 > 0:
                        act.wait_ge(hid_ready, f - 1)
                    A(tanh_t[:, f % 2, :], bank(M + 2 * (f % 2))[:, 0:TOK], ACT.Tanh, scale=0.5).then_inc(tanh_ready, 1)

            def experts(L):
                act.wait_ge(utok_ps, 1)
                A(utok[:, 0:2, :].rearrange("p b (g c) -> p (b g) c", g=2), ps_t[:, M + 1:M + 5, :], ACT.Copy)
                A(utok[0:32, 2, 0:512], bank(M + 5)[0:32, :], ACT.Copy)
                A(utok[0:32, 2, 512:1024], bank(0)[0:32, :], ACT.Copy).then_inc(utok_ready, 1)
                act.wait_ge(shifted_ready, 1)
                for r, bs in pads(0):
                    last = A(wts[0:r, bs, :], wts[0:r, bs, :], ACT.Exp)
                last.then_inc(expw_ready, 1)
                act.wait_ge(rounds_ready, 1)
                rounds = act.value_load(nrt[0:1, 0:1], min_val=1, max_val=3)
                with act.Fori(0, rounds) as r:
                    with act.Fori(0, NE) as e:
                        it = act.snap(r * NE + e)
                        act.wait_ge(gather_ps, it + 1)
                        A(xg.rearrange("p (g k) c -> p g (k c)", g=2), ps_t[:, 0:2, :], ACT.Copy).then_inc(xg_ready, 1)
                        for f in range(NF):
                            act.wait_ge(expert_slots, it * E_TILES + (RING + 2 * f + 1))
                            if f >= 2:
                                act.wait_ge(ehid_ready, it * NF + (f - 1))
                            A(etanh[:, f % 2, :], bank(M + 2 * (f % 2))[:, 0:P], ACT.Tanh, scale=0.5).then_inc(etanh_ready, 1)
                        act.wait_ge(expert_slots, it * E_TILES + (RING + E_TILES))
                        A(yt.rearrange("p (g c) -> p g c", g=2), ps_t[:, M + 4:M + 6, :], ACT.Copy).then_inc(y_taken, 1)

            act.wait_ge(const_in, 16)
            for L in range(DEPTH):
                norm(3 * L)
                for b in range(4):
                    take(("z", L, 0, b))
                prep(L)
                gla(L)
                ret(L)
                gdn(L)
                ssd(L)
                norm(3 * L + 1)
                dense(L) if L % 2 == 0 else experts(L)
                for b in range(2):
                    take(("pproj", L, 0, b))
                norm(3 * L + 2)
                for b in range(KD):
                    t = T_OF[("pgate", L, 0, b)]
                    act.wait_ge(tile_done, t + 1)
                    if KD * L + b - 1 > 0:
                        act.wait_ge(gate_used, KD * L + b - 1)
                    A(tanh_t[:, b % 2, :], bank(t % 2)[:, 0:TOK], ACT.Tanh, scale=0.5).then_inc(stream_ple, 1)
            norm(3 * DEPTH)

        @block.vector
        def _(dve):
            steps = Steps()
            V = nc.vector
            tt, ts, stt, cp = V.tensor_tensor, V.tensor_scalar, V.scalar_tensor_tensor, V.tensor_copy

            def fill(L, n, s):
                for x in FILL[L][n][s]:
                    if x[0] == "br":
                        branch_tile(x)

            def branch_tile(x):
                _, L, n, b = x
                t = T_OF[x]
                dve.wait_ge(tile_done, t + 1)
                dve.wait_ge(stream_act, taken_before(T_OF[("mg", L, n, 7)] + 1, "act"))
                g = mg[:, 2 * b:2 * b + 2, :]
                if n == 0:
                    stt(acc[:, 2 * b:2 * b + 2, :], g, 1.0, ps_t[:, 0:2, 0:TOK], ALU.add, ALU.mult).then_inc(stream_dve, 1)
                else:
                    stt(brt, g, 1.0, ps_t[:, 0:2, 0:TOK], ALU.add, ALU.mult).then_inc(stream_dve, 1)
                    dve.wait_ge(stream_dve, taken_before(t + 1, "dve"))
                    tt(acc[:, 2 * b:2 * b + 2, :], acc[:, 2 * b:2 * b + 2, :], brt, ALU.add).then_inc(dve_step, 1)
                    dve.wait_ge(dve_step, steps.next())

            def norm(k, gain):
                tt(acc, h, h, ALU.mult).then_inc(square_ready, 1)
                dve.wait_ge(rt_ready, k + 1)
                V.reciprocal(rs4[:, 1, :], rs4[:, 0, :]).then_inc(dve_step, 1)
                dve.wait_ge(dve_step, steps.next())
                for b in range(KD):
                    last = stt(u[:, b, :], h[:, b, :], PVc(gain, b), rs4[:, 1, :], ALU.mult, ALU.mult)
                last.then_inc(u_ready, 1)

            def prep(L):
                gab = tmp4.rearrange("p k t -> p (k t)")[:, 0:768].rearrange("p (b c) -> p b c", b=3)
                dve.wait_ge(small_ps, L + 1)
                ts(pv[:, PV["conv_w"][0]:PV["conv_w"][0] + 70], pv[:, PV["conv_w"][0]:PV["conv_w"][0] + 70],
                          0.5, None, ALU.mult).then_inc(dve_step, 1)
                dve.wait_ge(dve_step, steps.next())
                V.memset(glrt[0:32, :], 1.0).then_inc(dve_step, 1)
                dve.wait_ge(dve_step, steps.next())
                cp(glrt[0:16, :], bank(M)[0:16, 0:TOK])
                for r, bs in pads(0):
                    b0, b1 = bs.start, bs.stop
                    last = tt(xs[0:r, bs, :], bank(M + 1)[0:r, 16 * b0:16 * b1].rearrange("p (b c) -> p b c", c=16),
                              rows[0:r, 0:16].unsqueeze(1).to_broadcast([r, b1 - b0, 16]), ALU.add)
                last.then_inc(glr_ready, 1)
                dve.wait_ge(glr_ready, L + 1)
                for r, bs in pads(0):
                    last = stt(ab[0:r, bs, :], xs[0:r, bs, :], -1.0, xs[0:r, bs, :], ALU.mult, ALU.max)
                last.then_inc(abs_small, 1)
                dve.wait_ge(gk_ps, L + 1)
                for r, bs in pads(0):
                    b0, b1 = bs.start, bs.stop
                    last = cp(gx[0:r, bs, :], bank(M + 2 + b0 // 2)[0:r, 0:256 * (b1 - b0)].rearrange("p (b c) -> p b c", c=256))
                last.then_inc(dve_step, 1)
                dve.wait_ge(dve_step, steps.next())
                for r, bs in pads(0):
                    last = stt(gab[0:r, bs, :], gx[0:r, bs, :], -1.0, gx[0:r, bs, :], ALU.mult, ALU.max)
                last.then_inc(abs_gate, 1)
                dve.wait_ge(logs_ready, L + 1)
                for r, bs in pads(0):
                    nb = bs.stop - bs.start
                    stt(xs[0:r, bs, 4:16], xs[0:r, bs, 4:16], 0.0, ab[0:r, bs, 4:16], ALU.max, ALU.add)
                    ts(ls[0:r, bs, 0:4], ab[0:r, bs, 0:4], 0.5, 0.5, ALU.mult, ALU.add)
                    last = stt(gx[0:r, bs, :], gx[0:r, bs, :], 0.0, gab[0:r, bs, :], ALU.min, ALU.subtract)
                last.then_inc(dve_step, 1)
                dve.wait_ge(dve_step, steps.next())
                for r, bs in pads(0):
                    nb = bs.stop - bs.start
                    stt(ls[0:r, bs, 4:16], xs[0:r, bs, 4:16], -1.0,
                        ea[0:r, 4:16].unsqueeze(1).to_broadcast([r, nb, 12]), ALU.mult, ALU.mult)
                    last = ts(gx[0:r, bs, :], gx[0:r, bs, :], 1.0 / 16, None, ALU.mult)
                last.then_inc(logd_ready, 1)
                dve.wait_ge(cum_ps, L + 1)
                for r, bs in pads(0):
                    b0, b1 = bs.start, bs.stop
                    cp(gcol[0:r, bs, :], bank(M)[0:r, 16 * b0:16 * b1].rearrange("p (b c) -> p b c", c=16))
                cp(gt, ps_t[:, M + 3:M + 5, 0:TOK]).then_inc(cum_taken_dve, 1)
                dve.wait_ge(cum_taken_dve, L + 1)
                dve.wait_ge(cum_taken_act, L + 1)

            def take_vk(L, n):
                dve.wait_ge(vk_ps, 4 * L + n + 1)
                for r, bs in pads(0):
                    b0, b1 = bs.start, bs.stop
                    nb = b1 - b0
                    src = ps_t[0:r, M + b0:M + b1, :]
                    ks = bank(M + 3 + b0 // 2)[0:r, 0:256 * nb].rearrange("p (b c) -> p b c", c=256)
                    if n in (GLA, RET):
                        cp(vtok[0:r, bs, :], src)
                    else:
                        nh = HEADS[n]
                        f = ls[0:r, bs, 0:4] if n == GDN else xs[0:r, bs, 8:16]
                        tt(vtok[0:r, bs, :].rearrange("p b (h v) -> p b h v", h=nh), src.rearrange("p b (h v) -> p b h v", h=nh),
                           f.unsqueeze(3).to_broadcast([r, nb, nh, DV[n]]), ALU.mult)
                    if n == GLA:
                        last = tt(kdec[0:r, bs, 0:256], kdec[0:r, bs, 0:256], ks, ALU.mult)
                    elif n in (RET, GDN):
                        f = (C("ret_kd").rearrange("p (b c) -> p b c", b=3)[0:r, bs, 0:4] if n == RET else kde[0:r, bs, 4:8])
                        last = tt(kdec[0:r, bs, 0:256].rearrange("p b (h v) -> p b h v", h=4),
                                  ks.rearrange("p b (h v) -> p b h v", h=4), f.unsqueeze(3).to_broadcast([r, nb, 4, 64]), ALU.mult)
                    else:
                        for g in range(2):
                            for b in range(b0, b1):
                                last = tt(kdec[0:r, b, 256 * g:256 * g + 256].rearrange("p (h v) -> p h v", h=4),
                                          ks[:, b - b0, 64 * g:64 * g + 64].unsqueeze(1).to_broadcast([r, 4, 64]),
                                          kde[0:r, b, 8 + 4 * g:12 + 4 * g].unsqueeze(2).to_broadcast([r, 4, 64]), ALU.mult)
                last.then_inc(vk_taken, 1)
                dve.wait_ge(vk_taken, 4 * L + n + 1)

            def scores(L, n, slot):
                for hh in range(HEADS[n]):
                    gh = L * NHEAD + HBASE[n] + hh
                    dve.wait_ge(scores_ps, L * 16 + HBASE[n] - 4 + hh + 1)
                    if hh >= 4:
                        dve.wait_ge(o_ps, gh - 3)
                    d = C("ret_decay", PAIR * hh, PAIR * hh + PAIR) if n == RET else dmat[:, hh, :]
                    if n != RET:
                        dve.wait_ge(decay_ready, L * 12 + (0 if n == GDN else 4) + HEADS[n])
                    s = bank(M + hh % 2)
                    tt(pt[:, hh % 4, 0:384], s[:, 0:384], d[:, 0:384], ALU.mult)
                    tt(pt[0:32, hh % 4, 384:416], s[0:32, 384:416], d[0:32, 384:416], ALU.mult).then_inc(pt_ready, 1)
                    fill(L, n, slot + hh)

            def state(L, n):
                m = 4 * L + n
                dve.wait_ge(vmask_used, L * NHEAD + HBASE[n] + HEADS[n])
                if 16 * m > 0:
                    dve.wait_ge(stp_out, 16 * m)
                dve.wait_ge(state_decayed, m + 1)
                cp(stp, bank(M + 4)[:, 0:256])
                tt(st.rearrange("p (k c) -> p k c", k=4), st.rearrange("p (k c) -> p k c", k=4), ps_t[:, M:M + 4, :],
                   ALU.add).then_inc(state_new, 1)

            def out_norm(L, n, slot):
                m = 4 * L + n
                vt4 = vtok.rearrange("p b c -> p (b c)")[:, 0:4 * TOK].rearrange("p (k t) -> p k t", k=4)
                gates = zset[n % 2][:, GATE0[n]:GATE0[n] + 4, 0:TOK]
                o4 = zset[n % 2][:, OUT0[n]:OUT0[n] + 4, 0:TOK]
                dve.wait_ge(gate_tanh, m + 1)
                dve.wait_ge(o_taken, L * NHEAD + HBASE[n] + HEADS[n])
                if n == SSD:
                    for b in range(4):
                        stt(o4[:, b, :], cv[:, b, :], PVc("ssd_d", b), o4[:, b, :], ALU.mult, ALU.add)
                stt(vt4, vt4, 1.0, gates, ALU.add, ALU.mult).then_inc(dve_step, 1)
                dve.wait_ge(dve_step, steps.next())
                if n == SSD:
                    tt(o4, o4, vt4, ALU.mult).then_inc(y_ready, 1)
                dve.wait_ge(ort_ready, m + 1)
                w = 2 if n == SSD else 4
                V.reciprocal(rs4[:, 0:w, :], rs4[:, 0:w, :]).then_inc(dve_step, 1)
                dve.wait_ge(dve_step, steps.next())
                if n == SSD:
                    for b in range(4):
                        last = stt(o4[:, b, :], o4[:, b, :], PVc("ssd_norm", b), rs4[:, b // 2, :], ALU.mult, ALU.mult)
                else:
                    stt(o4, o4, PVc(("gla_norm", "ret_norm", "gdn_norm")[n]), rs4, ALU.mult, ALU.mult).then_inc(dve_step, 1)
                    dve.wait_ge(dve_step, steps.next())
                    last = tt(o4, o4, vt4, ALU.mult)
                last.then_inc(o_final, 1)
                dve.wait_ge(o_final, m + 1)
                fill(L, n, slot)

            def decays(L, n):
                for hh in range(HEADS[n]):
                    k = L * 12 + (hh if n == GDN else 4 + hh)
                    c = SSD_COL[n] + hh
                    half, pair = half_pair(n, hh)
                    dve.wait_ge(grow_ps, k + 1)
                    g = bank(M + 2 + hh % 2)
                    for b, (r, i0, i1, c0) in enumerate(SEGS):
                        stt(dmat[0:r, hh, c0:c0 + i1 - i0], g[0:r, i0:i1], gcol[0:r, b, c:c + 1],
                            C("future")[0:r, c0:c0 + i1 - i0], ALU.subtract, ALU.add)
                    cp(egp[64 * half:64 * half + 64, pair, :], g[64 * half:64 * half + 64, 256:288]).then_inc(grow_taken, 1)
                    if hh % 2:
                        fill(L, n, 4 + hh // 2)
                dve.wait_ge(eg_ready, 2 * L + (1 if n == GDN else 2))

            def conv(L, n):
                nb = NCONV[n]
                wv = pv[:, PV["conv_w"][0]:PV["conv_w"][0] + 56].rearrange("p (k b) -> p k b", b=14)

                def finish(b):
                    dve.wait_ge(ctan_ready, 14 * L + CONV0[n] + b + 1)
                    c, t = cbuf[:, b % 2, :], ctan[:, b % 2, :]
                    stt(cv[:, b, 0:256], t[:, 0:256], 1.0, c[:, 0:256], ALU.add, ALU.mult)
                    s7 = [q[:, 259:315].rearrange("p (s w) -> p s w", w=7)[:, :, 0:4] for q in (t, c)]
                    stt(cv[:, b, 256:288].rearrange("p (s w) -> p s w", w=4), s7[0], 1.0, s7[1],
                        ALU.add, ALU.mult).then_inc(conv_ready, 1)
                    dve.wait_ge(conv_ready, 14 * L + CONV0[n] + b + 1)

                for b in range(nb):
                    ci = CONV0[n] + b
                    dve.wait_ge(stream_act, taken_before(T_OF[("z", L, n, b)] + 1, "act"))
                    dve.wait_ge(pads_ready, 2 * L + (1 if n == GDN else 2))
                    src = zblk(n, b)
                    out = cbuf[:, b % 2, 0:312]
                    ts(out, src[:, 0:312], wv[:, 0, ci:ci + 1], PVc("conv_b", ci), ALU.mult, ALU.add).then_inc(dve_step, 1)
                    dve.wait_ge(dve_step, steps.next())
                    stt(out, src[:, 1:313], wv[:, 1, ci:ci + 1], out, ALU.mult, ALU.add).then_inc(dve_step, 1)
                    dve.wait_ge(dve_step, steps.next())
                    stt(out, src[:, 2:314], wv[:, 2, ci:ci + 1], out, ALU.mult, ALU.add).then_inc(dve_step, 1)
                    dve.wait_ge(dve_step, steps.next())
                    stt(out, src[:, 3:315], wv[:, 3, ci:ci + 1], out, ALU.mult, ALU.add).then_inc(convsum_ready, 1)
                    if b >= 1:
                        finish(b - 1)
                finish(nb - 1)

            def gla(L):
                zq, zk = zset[0][:, 0:2, 0:TOK], zset[0][:, 2:4, 0:TOK]
                take_vk(L, GLA)
                V.memset(ps_t[:, M:M + 4, 0:PAIR], 0.0).then_inc(cross_zero, 1)
                for q in range(2):
                    ref = gt[:, q, 15:255:16].unsqueeze(2).to_broadcast([P, 15, 16])
                    last = tt(qt[:, q, 16:256].rearrange("p (s w) -> p s w", w=16),
                              gt[:, q, 16:256].rearrange("p (s w) -> p s w", w=16), ref, ALU.subtract)
                last.then_inc(qd_ready, 1)
                tt(qg[:, 0:2, :], zq[:, :, 256:288], egp[:, 0:2, :], ALU.mult).then_inc(qg_ready, 1)
                dve.wait_ge(qe_ready, L + 1)
                tt(qt[:, :, 16:256], qt[:, :, 16:256], zq[:, :, 16:256], ALU.mult).then_inc(dve_step, 1)
                dve.wait_ge(dve_step, steps.next())
                for a in range(1, 16):
                    dve.wait_ge(e_ready, 15 * L + a)
                    tt(kt[:, a % 2, :, 0:16 * a], kt[:, a % 2, :, 0:16 * a], zk[:, :, 0:16 * a],
                       ALU.mult).then_inc(kt_ready, 1)
                    fill(L, GLA, a - 1)
                V.memset(dd, 0.0).then_inc(dve_step, 1)
                dve.wait_ge(dve_step, steps.next())

                def views(x, jj):
                    out = []
                    for q in range(2):
                        out.append((x[:, q, 0:256].rearrange("p (s w) -> p s w", w=16), 16, 16))
                        if jj < 4:
                            out.append((x[:, q, 256:288].rearrange("p (s w) -> p s w", w=4), 8, 4))
                    return out

                def sub(jj):
                    if jj >= 2:
                        dve.wait_ge(sub_ps, 16 * L + jj - 1)
                    for (o, ns, w), (g, _, _) in zip(views(dd[:, jj % 2], jj), views(gt, jj)):
                        last = tt(o[:, :, jj:w], g[:, :, jj:w], g[:, :, jj:jj + 1].to_broadcast([P, ns, w - jj]), ALU.subtract)
                    last.then_inc(diff_ready, 1)

                def mul(jj):
                    dve.wait_ge(ediff_ready, 16 * L + jj + 1)
                    dve.wait_ge(qk_prod, 16 * L + jj + 1)
                    for (o, ns, w), (g, _, _) in zip(views(dd[:, jj % 2], jj), views(qk[:, jj % 2], jj)):
                        last = tt(o[:, :, jj:w], o[:, :, jj:w], g[:, :, jj:w], ALU.mult)
                    last.then_inc(sub_ready, 1)
                    fill(L, GLA, 15 + jj)

                sub(0)
                for jj in range(1, 16):
                    sub(jj)
                    mul(jj - 1)
                mul(15)
                dve.wait_ge(sub_ps, 16 * L + 16)
                cp(band[0:32], ps_t[0:32, M + 4:M + 6, 0:TOK]).then_inc(band_ready, 1)
                for hh in range(4):
                    dve.wait_ge(spread_ps, 4 * L + hh + 1)
                    if L * NHEAD + hh > 0:
                        dve.wait_ge(pt_ready, L * NHEAD + hh)
                    d, x = bank(M + 4 + hh % 2), bank(M + hh)
                    tt(dtmp[:, 0:256], d[:, 0:256], C("sub_diag", 0, 256), ALU.mult)
                    cp(pt[:, hh, 128:256], x[:, 128:256])
                    tt(pt[0:32, hh, 384:416], d[0:32, 256:288], C("sub_diag", 256, 288)[0:32], ALU.mult).then_inc(dve_step, 1)
                    dve.wait_ge(dve_step, steps.next())
                    tt(pt[:, hh, 0:128], dtmp[:, 0:128], x[:, 0:128], ALU.add)
                    tt(pt[:, hh, 256:384], dtmp[:, 128:256], x[:, 256:384], ALU.add).then_inc(pt_ready, 1)
                dve.wait_ge(pt_ready, L * NHEAD + 4)
                fill(L, GLA, 31)
                for s in range(32, 36):
                    fill(L, GLA, s)
                state(L, GLA)
                fill(L, GLA, 36)
                out_norm(L, GLA, 37)

            def ret(L):
                fill(L, RET, 0)
                z4 = zset[1][:, 0:4, 0:TOK]
                dve.wait_ge(rot_ps, L + 1)
                tt(tmp4, z4, C("cos").unsqueeze(1).to_broadcast([P, 4, TOK]), ALU.mult).then_inc(dve_step, 1)
                dve.wait_ge(dve_step, steps.next())
                tt(z4, ps_t[:, M:M + 4, 0:TOK], C("sin").unsqueeze(1).to_broadcast([P, 4, TOK]), ALU.mult).then_inc(dve_step, 1)
                dve.wait_ge(dve_step, steps.next())
                tt(z4, z4, tmp4, ALU.add).then_inc(rope_ready, 1)
                dve.wait_ge(rope_ready, L + 1)
                tt(qg[:, 0:2, :], z4[:, 0:2, 256:288], C("ret_eg").rearrange("p (q t) -> p q t", q=2),
                   ALU.mult).then_inc(qg_ready, 1)
                take_vk(L, RET)
                fill(L, RET, 1)
                scores(L, RET, 2)
                state(L, RET)
                fill(L, RET, 6)
                out_norm(L, RET, 7)
                for s in range(8, NSLOT[RET]):
                    fill(L, RET, s)

            def gdn(L):
                fill(L, GDN, 0)
                conv(L, GDN)
                dve.wait_ge(qkrt_ready, L + 1)
                V.reciprocal(rs4, rs4).then_inc(dve_step, 1)
                dve.wait_ge(dve_step, steps.next())
                stt(cv[:, 0:2, :], cv[:, 0:2, :], 0.125, rs4[:, 0:2, :], ALU.mult, ALU.mult)
                tt(cv[:, 2:4, :], cv[:, 2:4, :], rs4[:, 2:4, :], ALU.mult).then_inc(qk_ready, 1)
                dve.wait_ge(qk_ready, L + 1)
                fill(L, GDN, 1)
                take_vk(L, GDN)
                fill(L, GDN, 2)
                dve.wait_ge(beta_ps, L + 1)
                tt(kb, cv[:, 2:4, :], ps_t[:, M + 4:M + 6, 0:TOK], ALU.mult).then_inc(kb_ready, 1)
                dve.wait_ge(kb_ready, L + 1)
                fill(L, GDN, 3)
                decays(L, GDN)
                tt(qg[:, 0:2, :], cv[:, 0:2, 256:288], egp[:, 0:2, :], ALU.mult).then_inc(qg_ready, 1)
                tt(kbg, kb[:, :, 256:288], egp[:, 0:2, :], ALU.mult).then_inc(kbg_ready, 1)
                for hh in range(4):
                    dve.wait_ge(kk_ps, 4 * L + hh + 1)
                    tt(pt[:, hh, 0:384], bank(M + hh)[:, 0:384], dmat[:, hh, 0:384], ALU.mult)
                    last = tt(pt[0:32, hh, 384:416], bank(M + hh)[0:32, 384:416], dmat[0:32, hh, 384:416], ALU.mult)
                last.then_inc(dve_step, 1)
                dve.wait_ge(dve_step, steps.next())
                tt(pt[:, :, 0:384], pt[:, :, 0:384], C("strict", 0, 384).unsqueeze(1).to_broadcast([P, 4, 384]), ALU.mult)
                tt(pt[0:32, :, 384:416], pt[0:32, :, 384:416],
                   C("strict", 384, 416)[0:32].unsqueeze(1).to_broadcast([32, 4, 32]), ALU.mult).then_inc(mt_ready, 1)
                fill(L, GDN, 6)
                for lv in range(2):
                    dve.wait_ge(x_s_ps, 2 * L + lv + 1)
                    d = bank(M + 4)
                    tt(xs_s[0:32], xs_s[0:32], d[0:32, 128:256].rearrange("p (h c) -> p h c", h=4), ALU.subtract)
                    tt(xt_s[0:32], xt_s[0:32], d[0:32, 256:384].rearrange("p (h c) -> p h c", h=4),
                       ALU.subtract).then_inc(inv_s_ready, 1)
                    fill(L, GDN, 7 + lv)
                v2 = [q.rearrange("p h b c -> p (h b c)").rearrange("p (k c) -> p k c", k=2) for q in (xm, xt)]
                for lv in range(7):
                    fill(L, GDN, 9 + 2 * lv)
                    dve.wait_ge(x_ps, 7 * L + lv + 1)
                    tt(v2[0], v2[0], ps_t[:, M + 2:M + 4, :], ALU.subtract)
                    tt(v2[1], v2[1], ps_t[:, M + 4:M + 6, :], ALU.subtract).then_inc(inv_ready, 1)
                    fill(L, GDN, 10 + 2 * lv)
                dve.wait_ge(vn0_ps, L + 1)
                cp(vtok[:, 0, :], bank(M)).then_inc(vn0_ready, 1)
                dve.wait_ge(ks_ps, L + 1)
                for f in range(2):
                    last = cp(pb.rearrange("p h b c -> p (h b c)")[:, 0:128].rearrange("p (q f c) -> p q f c", q=2, f=2)[:, :, f, :],
                              bank(M + 1 + 4 * f)[:, 0:64].rearrange("p (q c) -> p q c", q=2))
                last.then_inc(ks_ready, 1)
                fill(L, GDN, 23)
                dve.wait_ge(r1_ps, L + 1)
                tt(vtok[:, 1, :], vtok[:, 1, :], bank(M + 2), ALU.subtract)
                dve.wait_ge(kst_ps, L + 1)
                tt(vtok[0:32, 2, :], vtok[0:32, 2, :], bank(M + 3)[0:32, :], ALU.subtract).then_inc(r1_ready, 1)
                fill(L, GDN, 24)
                dve.wait_ge(vn1_ps, L + 1)
                cp(vtok[:, 1, :], bank(M + 4))
                cp(vtok[0:32, 2, :], bank(M + 5)[0:32, :]).then_inc(vn1_ready, 1)
                fill(L, GDN, 25)
                scores(L, GDN, 26)
                state(L, GDN)
                fill(L, GDN, 30)
                out_norm(L, GDN, 31)
                for s in range(32, NSLOT[GDN]):
                    fill(L, GDN, s)

            def ssd(L):
                conv(L, SSD)
                fill(L, SSD, 0)
                take_vk(L, SSD)
                for s in range(1, 4):
                    fill(L, SSD, s)
                decays(L, SSD)
                tt(qg, cv[:, 5, 256:288].unsqueeze(1).to_broadcast([P, 4, SAMP]), egp, ALU.mult).then_inc(qg_ready, 1)
                scores(L, SSD, 8)
                state(L, SSD)
                fill(L, SSD, 16)
                out_norm(L, SSD, 17)

            def dense(L):
                for f in range(NF):
                    dve.wait_ge(tanh_ready, f + 1)
                    b = bank(M + 2 * (f % 2))
                    stt(silu_t[:, f % 2, :], tanh_t[:, f % 2, :], 1.0, b[:, 0:TOK], ALU.add, ALU.mult).then_inc(dve_step, 1)
                    dve.wait_ge(dve_step, steps.next())
                    dve.wait_ge(tile_done, T_OF[("up", L, 0, f)] + 1)
                    stt(hid[:, f, :], silu_t[:, f % 2, :], 0.5, bank(M + 1 + 2 * (f % 2))[:, 0:TOK], ALU.mult,
                        ALU.mult).then_inc(hid_ready, 1)
                    if f - 1 > 0:
                        dve.wait_ge(hid_ready, f - 1)
                dve.wait_ge(tile_done, T_OF[("down", L, 0, NF - 1)] + 1)
                tt(h, h, ps_t[:, :, 0:TOK], ALU.add).then_inc(ffn_added, 1)

            def experts(L):
                dve.wait_ge(logit_ps, 1)
                for r, bs in pads(0):
                    b0, b1 = bs.start, bs.stop
                    last = cp(logit[0:r, bs, :], bank(M)[0:r, 8 * b0:8 * b1].rearrange("p (b e) -> p b e", e=8))
                last.then_inc(dve_step, 1)
                dve.wait_ge(dve_step, steps.next())
                for r, bs in pads(0):
                    nb = bs.stop - bs.start
                    sh = [r, nb, 8, 8]
                    mine = logit[0:r, bs, :].unsqueeze(3).to_broadcast(sh)
                    other = logit[0:r, bs, :].unsqueeze(2).to_broadcast(sh)
                    less = C("less")[0:r].rearrange("p (e f) -> p e f", e=8).unsqueeze(1).to_broadcast(sh)
                    tt(rank_t[0:r, bs], other, mine, ALU.is_gt)
                    tt(less_t[0:r, bs], other, mine, ALU.is_equal).then_inc(dve_step, 1)
                    dve.wait_ge(dve_step, steps.next())
                    tt(less_t[0:r, bs], less_t[0:r, bs], less, ALU.mult).then_inc(dve_step, 1)
                    dve.wait_ge(dve_step, steps.next())
                    tt(rank_t[0:r, bs], rank_t[0:r, bs], less_t[0:r, bs], ALU.add).then_inc(dve_step, 1)
                    dve.wait_ge(dve_step, steps.next())
                    V.reduce_sum(sel[0:r, bs, :], rank_t[0:r, bs], AX.X).then_inc(dve_step, 1)
                    dve.wait_ge(dve_step, steps.next())
                    ts(sel[0:r, bs, :], sel[0:r, bs, :], float(TOP_K), None, ALU.is_lt).then_inc(dve_step, 1)
                    dve.wait_ge(dve_step, steps.next())
                    V.reduce_max(mx[0:r, bs], logit[0:r, bs, :], AX.X).then_inc(dve_step, 1)
                    dve.wait_ge(dve_step, steps.next())
                    tt(wts[0:r, bs, :], logit[0:r, bs, :], mx[0:r, bs].unsqueeze(2).to_broadcast([r, nb, 8]), ALU.subtract).then_inc(dve_step, 1)
                    dve.wait_ge(dve_step, steps.next())
                cp(slotrow, C("slot_row")).then_inc(sel_ready, 1)
                cp(slotcol, C("slot_col")).then_inc(shifted_ready, 1)
                dve.wait_ge(expw_ready, 1)
                for r, bs in pads(0):
                    nb = bs.stop - bs.start
                    tt(wts[0:r, bs, :], wts[0:r, bs, :], sel[0:r, bs, :], ALU.mult).then_inc(dve_step, 1)
                    dve.wait_ge(dve_step, steps.next())
                    V.reduce_sum(mx[0:r, bs], wts[0:r, bs, :], AX.X).then_inc(dve_step, 1)
                    dve.wait_ge(dve_step, steps.next())
                    V.reciprocal(mx[0:r, bs], mx[0:r, bs]).then_inc(dve_step, 1)
                    dve.wait_ge(dve_step, steps.next())
                    tt(wts[0:r, bs, :], wts[0:r, bs, :], mx[0:r, bs].unsqueeze(2).to_broadcast([r, nb, 8]), ALU.mult).then_inc(dve_step, 1)
                    dve.wait_ge(dve_step, steps.next())
                dve.wait_ge(pos_ps, 1)
                V.reduce_max(cnt[:, 2:3], bank(M)[:, 24:32], AX.X).then_inc(dve_step, 1)
                dve.wait_ge(dve_step, steps.next())
                for r, bs in pads(0):
                    b0, b1 = bs.start, bs.stop
                    stt(posm[0:r, bs, :], bank(M)[0:r, 8 * b0:8 * b1].rearrange("p (b e) -> p b e", e=8), 1.0,
                               sel[0:r, bs, :], ALU.add, ALU.mult).then_inc(dve_step, 1)
                    dve.wait_ge(dve_step, steps.next())
                    last = ts(posm[0:r, bs, :], posm[0:r, bs, :], -1.0, None, ALU.add)
                last.then_inc(pos_ready, 1)
                ts(cnt[:, 0:1], cnt[:, 2:3], 128.5, 1.0, ALU.is_gt, ALU.add).then_inc(dve_step, 1)
                dve.wait_ge(dve_step, steps.next())
                ts(cnt[:, 1:2], cnt[:, 2:3], 256.5, None, ALU.is_gt).then_inc(dve_step, 1)
                dve.wait_ge(dve_step, steps.next())
                tt(nrt, cnt[:, 0:1], cnt[:, 1:2], ALU.add).then_inc(rounds_ready, 1)
                for e in range(NE):
                    dve.wait_ge(rows_ps, e + 1)
                    b = M + 2 * (e % 2)
                    cp(posrow[:, e, :], bank(b)[:, 0:TOK])
                    cp(wrow[:, e, :], bank(b + 1)[:, 0:TOK]).then_inc(rows_taken, 1)
                dve.wait_ge(rounds_ready, 1)
                rounds = dve.value_load(nrt[0:1, 0:1], min_val=1, max_val=3)
                with dve.Fori(0, rounds) as r:
                    with dve.Fori(0, NE) as e:
                        it = dve.snap(r * NE + e)
                        for b, (t0, nt) in enumerate(TB):
                            last = tt(gath[0:nt, b, :], slotrow[0:nt], posm[0:nt, b, bass.ds(e, 1)].to_broadcast([nt, P]),
                                      ALU.is_equal)
                        last.then_inc(gather_ready, 1)
                        stt(scat, posrow[:, bass.ds(e, 1), :].rearrange("p a t -> p (a t)"), slotcol,
                            wrow[:, bass.ds(e, 1), :].rearrange("p a t -> p (a t)"), ALU.is_equal,
                            ALU.mult).then_inc(scatter_ready, 1)
                        for f in range(NF):
                            dve.wait_ge(etanh_ready, it * NF + (f + 1))
                            stt(esilu[:, f % 2, :], etanh[:, f % 2, :], 1.0, bank(M + 2 * (f % 2))[:, 0:P], ALU.add,
                                ALU.mult).then_inc(esilu_ready, 1)
                            dve.wait_ge(esilu_ready, it * NF + (f + 1))
                            dve.wait_ge(expert_slots, it * E_TILES + (RING + 2 * f + 2))
                            stt(ehid[:, f, :], esilu[:, f % 2, :], 0.5, bank(M + 1 + 2 * (f % 2))[:, 0:P], ALU.mult,
                                ALU.mult).then_inc(ehid_ready, 1)
                            if f:
                                dve.wait_ge(ehid_ready, it * NF + f)
                        dve.wait_ge(ehid_ready, it * NF + NF)
                        for g, (b0, k0, nk) in enumerate(((M, 0, 4), (0, 4, 2), (M + 4, 6, 2))):
                            dve.wait_ge(scatter_ps, it * 3 + (g + 1))
                            last = tt(h[:, k0:k0 + nk, :], h[:, k0:k0 + nk, :], ps_t[:, b0:b0 + nk, 0:TOK], ALU.add)
                        last.then_inc(expert_added, 1)
                        dve.wait_ge(expert_added, it + 1)
                    ts(slotrow, slotrow, float(P), None, ALU.add)
                    ts(slotcol, slotcol, float(P), None, ALU.add).then_inc(round_step, 1)
                    dve.wait_ge(round_step, r + 1)
                tt(mx[:, 0:1], mx[:, 0:1], mx[:, 0:1], ALU.add).then_inc(ffn_added, 1)

            dve.wait_ge(const_in, 16)
            dve.wait_ge(x_in, 16)
            for L in range(DEPTH):
                dve.wait_ge(small_in, 16 * 5 * (L + 1))
                norm(3 * L, "norm_mix")
                prep(L)
                gla(L)
                ret(L)
                gdn(L)
                ssd(L)
                for b in range(4):
                    branch_tile(("br", L, 3, b))
                ts(rs4[:, 1, 0:1], rs4[:, 1, 0:1], 1.0, None, ALU.mult).then_inc(acc_ready, 1)
                for b in range(KD):
                    x = ("out", L, 0, b)
                    t = T_OF[x]
                    dve.wait_ge(tile_done, t + 1)
                    stt(h[:, b, :], bank(t % 2)[:, 0:TOK], 0.5, h[:, b, :], ALU.mult, ALU.add).then_inc(stream_dve, 1)
                dve.wait_ge(stream_dve, taken_before(T_OF[("out", L, 0, 7)] + 1, "dve"))
                norm(3 * L + 1, "norm_ffn")
                dense(L) if L % 2 == 0 else experts(L)
                dve.wait_ge(ffn_added, L + 1)
                norm(3 * L + 2, "norm_ple")
                for b in range(KD):
                    dve.wait_ge(stream_ple, KD * L + b + 1)
                    dve.wait_ge(stream_act, taken_before(T_OF[("pproj", L, 0, 1)] + 1, "act"))
                    stt(silu_t[:, b % 2, :], tanh_t[:, b % 2, :], 1.0, ple_pj[:, b, :], ALU.add,
                        ALU.mult).then_inc(gate_used, 1)
                    dve.wait_ge(gate_used, KD * L + b + 1)
                    stt(h[:, b, :], silu_t[:, b % 2, :], 0.5, h[:, b, :], ALU.mult, ALU.add).then_inc(dve_step, 1)
                    dve.wait_ge(dve_step, steps.next())
            norm(3 * DEPTH, "norm_final")

        @block.gpsimd
        def _(pool):
            G = nc.gpsimd

            def small(L):
                for dst, src in ((pv[:, :], io["pv"][L]), (wsm.rearrange("p k c -> p (k c)"), io["wsm"][L]),
                                 (wgk[0:17, :], io["wgk"][L]), (rows[:, :], io["rows"][L]),
                                 (hist.rearrange("p b c -> p (b c)"), io["hist"][L])):
                    pool.dma_start(dst, src).then_inc(small_in, 16)
                pool.dma_start(st, io["state"][L, 0]).then_inc(state_in, 16)

            def pads_for(L, n):
                z = zset[n % 2][:, 0:NCONV[n], :]
                hs = hist[:, CONV0[n]:CONV0[n] + NCONV[n], :]
                pool.wait_ge(tile_done, T_OF[("br", L, n - 2, 3)] + 1)
                pool.wait_ge(small_in, 16 * 5 * (L + 1))
                G.memset(z[:, :, 0:3], 0.0)
                for b in range(NCONV[n]):
                    last = G.tensor_copy(z[:, b, 259:315].rearrange("p (s w) -> p s w", w=7)[:, :, 0:3],
                                         hs[:, b, :].rearrange("p (s w) -> p s w", w=3))
                last.then_inc(pads_ready, 1)

            def save_rows(L, n):
                pool.wait_ge(stream_act, taken_before(T_OF[("z", L, n, NCONV[n] - 1)] + 1, "act"))
                for b in range(NCONV[n]):
                    G.tensor_copy(csave[:, CONV0[n] + b, 0:3], zblk(n, b)[:, 256:259])
                    last = G.tensor_copy(csave[:, CONV0[n] + b, 3:27].rearrange("p (s w) -> p s w", w=3),
                                         zblk(n, b)[:, 259:315].rearrange("p (s w) -> p s w", w=7)[:, :, 4:7])
                last.then_inc(rows_saved, 1)
                pool.wait_ge(rows_saved, 2 * L + (1 if n == GDN else 2))

            def samples(L, n):
                m, dv = 4 * L + n, DV[n]
                if n == GDN:
                    pool.wait_ge(vn1_ready, L + 1)
                else:
                    pool.wait_ge(vk_taken, m + 1)
                for hh in range(HEADS[n]):
                    gh = L * NHEAD + HBASE[n] + hh
                    if n == SSD:
                        pool.wait_ge(vmask_used, gh - 1 if hh >= 2 else gh - hh)
                        dst = vmask[0:32, 512 * (hh % 2):512 * (hh % 2) + 512]
                    else:
                        if gh > 0:
                            pool.wait_ge(vmask_used, gh)
                        dst = vmask[0:32, :]
                    G.tensor_tensor(dst.rearrange("p (b v) -> p b v", b=NSEQ),
                                    vtok[0:32, 2, dv * hh:dv * hh + dv].unsqueeze(1).to_broadcast([32, NSEQ, dv]),
                                    C("seq_of")[0:32].unsqueeze(2).to_broadcast([32, NSEQ, dv]),
                                    ALU.mult).then_inc(vmask_ready, 1)
                    if hh == 0:
                        pool.wait_ge(o_ps, L * NHEAD + HBASE[n] + HEADS[n])
                        e = C("ret_eg").rearrange("p (q t) -> p q t", q=2) if n == RET else egp
                        for q in range(HEADS[n] // 2):
                            last = G.tensor_tensor(st_of(n)[:, q], st_of(n)[:, q],
                                                   e[:, q, 3::4].unsqueeze(2).to_broadcast([P, NSEQ, dv]), ALU.mult)
                        last.then_inc(state_decayed, 1)
                pool.wait_ge(state_new, m + 1)
                pool.dma_start(io["state_s"][L, n], st).then_inc(state_out, 16)
                pool.dma_start(io["state_p"][L, n], stp).then_inc(stp_out, 16)
                pool.wait_ge(state_out, 16 * (m + 1))
                if n < 3:
                    pool.dma_start(st, io["state"][L, n + 1]).then_inc(state_in, 16)

            def gla(L):
                pool.wait_ge(stream_act, taken_before(T_OF[("z", L, 0, 11)] + 1, "act"))
                pool.wait_ge(cum_taken_dve, L + 1)
                zq, zk = zset[0][:, 0:2, 0:TOK], zset[0][:, 2:4, 0:TOK]
                for jj in range(16):
                    if jj >= 2:
                        pool.wait_ge(sub_ready, 16 * L + jj - 1)
                    for q in range(2):
                        def v(x):
                            return x[:, q, 0:256].rearrange("p (s w) -> p s w", w=16)
                        last = G.tensor_tensor(v(qk[:, jj % 2])[:, :, jj:16], v(zq)[:, :, jj:16],
                                               v(zk)[:, :, jj:jj + 1].to_broadcast([P, 16, 16 - jj]), ALU.mult)
                        if jj < 4:
                            def v(x):
                                return x[:, q, 256:288].rearrange("p (s w) -> p s w", w=4)
                            last = G.tensor_tensor(v(qk[:, jj % 2])[:, :, jj:4], v(zq)[:, :, jj:4],
                                                   v(zk)[:, :, jj:jj + 1].to_broadcast([P, 8, 4 - jj]), ALU.mult)
                    last.then_inc(qk_prod, 1)

            def gdn(L):
                pool.wait_ge(qk_ready, L + 1)
                G.tensor_copy(xs_s[0:32], C("ident", 0, 32)[0:32].unsqueeze(1).to_broadcast([32, 4, 32]))
                G.tensor_copy(xt_s[0:32], C("ident", 0, 32)[0:32].unsqueeze(1).to_broadcast([32, 4, 32])).then_inc(inv_s_ready, 1)
                i8 = C("ident").unsqueeze(1).to_broadcast([P, 8, P])
                G.tensor_copy(xm.rearrange("p h b c -> p (h b) c"), i8)
                G.tensor_copy(xt.rearrange("p h b c -> p (h b) c"), i8).then_inc(inv_ready, 1)
                pool.wait_ge(mt_ready, L + 1)
                for lv in range(2):
                    if 2 * L + lv > 0:
                        pool.wait_ge(p_s_ps, 2 * L + lv)
                    G.tensor_tensor(ms_s[0:32], pt[0:32, :, 384:416],
                                    C("levels", 128 * lv, 128 * lv + 32)[0:32].unsqueeze(1).to_broadcast([32, 4, 32]),
                                    ALU.mult).then_inc(mask_s_ready, 1)
                for lv in range(7):
                    if 7 * L + lv > 0:
                        pool.wait_ge(p_ps, 7 * L + lv)
                    lm = C("levels", 128 * lv, 128 * lv + 128).unsqueeze(1).to_broadcast([P, 4, P])
                    for b in range(2):
                        last = G.tensor_tensor(msk[:, :, b, :], pt[:, :, 256 * b:256 * b + 128], lm, ALU.mult)
                    last.then_inc(mask_ready, 1)

            for L in range(DEPTH):
                if L > 0:
                    pool.wait_ge(u_ready, 3 * L)
                    pool.wait_ge(conv_out, 16 * L)
                    pool.wait_ge(state_out, 16 * 4 * L)
                small(L)
                gla(L)
                samples(L, GLA)
                samples(L, RET)
                pads_for(L, GDN)
                save_rows(L, GDN)
                gdn(L)
                samples(L, GDN)
                pads_for(L, SSD)
                save_rows(L, SSD)
                pool.dma_start(io["conv_out"][L], csave.rearrange("p b c -> p (b c)")).then_inc(conv_out, 16)
                samples(L, SSD)
                pool.wait_ge(tile_done, T_OF[("br", L, 3, 3)] + 1)
                pool.wait_ge(acc_ready, L + 1)
                pool.dma_start(ple_in.rearrange("p k t -> p (k t)"), io["ple"][L]).then_inc(ple_loaded, 16)
                if L == 1:
                    pool.dma_start(router.rearrange("p k e -> p (k e)"), io["router"]).then_inc(router_in, 16)
            pool.wait_ge(conv_out, 16 * DEPTH)
            pool.wait_ge(state_out, 16 * 4 * DEPTH)
            pool.wait_ge(stp_out, 16 * 4 * DEPTH)
            pool.wait_ge(u_ready, 3 * DEPTH + 1)
            pool.dma_start(io["y"], u.rearrange("p k t -> p (k t)")).then_inc(y_out, 16)
            pool.wait_ge(y_out, 16)


def lay_out(x):
    g = {k: np.asarray(v) for k, v in x.items()}
    a = {}

    def fm(t):
        return np.ascontiguousarray(t.T.reshape(-1, P, t.shape[0]).transpose(1, 0, 2))

    def join(p, s):
        return np.concatenate([p.reshape(SEQ, -1), s.reshape(SAMP, -1)], 0)

    a["x"] = fm(join(g["x_prompt"], g["x_sample"])).reshape(P, -1)
    a["ple"] = np.stack([fm(join(g["p_prompt"][L], g["p_sample"][L])).reshape(P, -1) for L in range(DEPTH)])
    total = len(PLAIN) + NE * E_TILES
    stream = np.empty((total, P, TILE), np.float32)

    def kblocks(w, c0, k0=0, nk=8):
        return w[k0 * P:(k0 + nk) * P, c0:c0 + P].reshape(nk, P, P).transpose(1, 0, 2)

    for t, (kind, L, n, b) in enumerate(PLAIN):
        row = stream[t if t < EXPERT_AT else t + NE * E_TILES].reshape(P, 8, P)
        if kind == "z":
            row[:] = kblocks(g["w_in"][L], ZCOLS[n][b])
        elif kind == "mg":
            row[:] = kblocks(g["w_in"][L], _C[16] + n * D_MODEL + P * b)
        elif kind == "br":
            for o in range(2):
                row[:, 4 * o:4 * o + 4] = kblocks(g["w_branch"][L, n], P * (2 * b + o), 0, 4)
        elif kind == "out":
            row[:] = kblocks(g["w_out"][L], P * b)
        elif kind == "gate":
            row[:] = kblocks(g["ffn_w_gate"][L // 2], P * b)
        elif kind == "up":
            row[:] = kblocks(g["ffn_w_up"][L // 2], P * b)
        elif kind == "down":
            row[:] = g["ffn_w_down"][L // 2][P * b:P * b + P].reshape(P, 8, P)
        elif kind == "pproj":
            for o in range(4):
                row[:, 2 * o:2 * o + 2] = kblocks(g["ple_w_proj"][L], P * (4 * b + o), 0, 2)
        elif kind == "pgate":
            row[:] = kblocks(g["ple_w_gate"][L], P * b)
    for e in range(NE):
        base = EXPERT_AT + e * E_TILES
        for f in range(NF):
            stream[base + 2 * f].reshape(P, 8, P)[:] = kblocks(g["moe_w_gate"][0, e], P * f)
            stream[base + 2 * f + 1].reshape(P, 8, P)[:] = kblocks(g["moe_w_up"][0, e], P * f)
            stream[base + 2 * NF + f] = g["moe_w_down"][0, e][P * f:P * f + P]
    a["stream"] = stream

    def halves(s, n):
        out = np.empty((2, 64, HEADS[n] // 2, NSEQ, DV[n]), np.float32)
        for hh in range(HEADS[n]):
            half, pair = half_pair(n, hh)
            out[half, :, pair] = s[:, hh].transpose(1, 0, 2)
        return out.reshape(P, 2048)

    names = ("state_gla", "state_ret", "state_gdn", "state_ssd")
    a["state"] = np.stack([np.stack([halves(g[names[n]][L], n) for n in range(4)]) for L in range(DEPTH)])
    a["hist"] = np.stack([np.concatenate([g[k][L].transpose(2, 0, 1).reshape(-1, P, 24).transpose(1, 0, 2)
                                          for k in ("state_gdn_conv", "state_ssd_conv")], 1).reshape(P, -1)
                          for L in range(DEPTH)])

    def cols(v):
        return v.reshape(-1, P).T

    pvs, wsm, wgk, rws = [], [], [], []
    for L in range(DEPTH):
        cw = np.concatenate([g["gdn_conv_w"][L], g["ssd_conv_w"][L]], 1)
        pvs.append(np.concatenate(
            [cols(g["norm_mix"][L]), cols(g["norm_ffn"][L]), cols(g["norm_ple"][L]), cols(g["norm_final"]),
             cols(g["gla_norm"][L]), cols(g["ret_norm"][L]), cols(g["gdn_norm"][L]), cols(g["ssd_norm"][L]),
             cw.reshape(4 * 14, P).T, np.zeros((P, 8), np.float32), cols(g["ssd_conv_b"][L]),
             cols(np.repeat(g["ssd_d"][L], 64))], 1))
        w = g["w_in"][L]
        w = np.concatenate([w[:, _C[3]:_C[4]], w[:, _C[10]:_C[12]], w[:, _C[15]:_C[16]]], 1)
        wsm.append(w.reshape(8, P, 32).transpose(1, 0, 2).reshape(P, -1))
        wgk.append(np.concatenate([g["gla_w_gk"][L], g["gla_b_gk"][L][None]], 0))
        z4 = np.zeros(4, np.float32)
        r = np.concatenate([z4, g["gdn_dt_bias"][L], g["ssd_dt_bias"][L], z4, g["gdn_a_log"][L], g["ssd_a_log"][L]])
        rws.append(np.broadcast_to(r, (P, 32)))
    a["pv"], a["wsm"], a["wgk"], a["rows"] = (np.ascontiguousarray(np.stack(v)) for v in (pvs, wsm, wgk, rws))
    a["router"] = g["moe_router"][0].reshape(8, P, NE).transpose(1, 0, 2).reshape(P, 64)
    a["const"] = np.concatenate([CONST[k] for k in CAT], 1)
    return {k: np.ascontiguousarray(v) for k, v in a.items()}


OUTS = {"y": (P, KD * TOK), "state_s": (DEPTH, 4, P, 2048), "state_p": (DEPTH, 4, P, 256), "conv_out": (DEPTH, P, 14 * 27)}


def gather_outputs(r):
    y = r["y"].reshape(P, KD, TOK).transpose(2, 1, 0).reshape(TOK, D_MODEL)
    pr, sa = [], []
    for n in range(4):
        s = r["state_s"][:, n].reshape(DEPTH, 2, 64, HEADS[n] // 2, NSEQ, DV[n])
        q = r["state_p"][:, n].reshape(DEPTH, 2, 64, HEADS[n] // 2, DV[n])
        hp = [half_pair(n, hh) for hh in range(HEADS[n])]
        sa.append(np.stack([s[:, a, :, b].transpose(0, 2, 1, 3) for a, b in hp], 2))
        pr.append(np.stack([q[:, a, :, b] for a, b in hp], 1)[:, None])
    c = r["conv_out"].reshape(DEPTH, P, 14, 9, 3).transpose(0, 3, 4, 2, 1).reshape(DEPTH, 9, 3, 14 * P)
    cp, cs = c[:, 0:1], c[:, 1:]
    w = 8 * P
    out = (y[:SEQ].reshape(1, SEQ, D_MODEL), y[SEQ:].reshape(NSEQ, DSEQ, D_MODEL),
           pr[0], pr[1], pr[2], cp[..., :w], pr[3], cp[..., w:],
           sa[0], sa[1], sa[2], cs[..., :w], sa[3], cs[..., w:])
    return tuple(np.ascontiguousarray(v) for v in out)


def kernel(**inputs):
    import concourse.bacc as bacc
    from concourse.bass_utils import run_bass_kernel_spmd

    nc = bacc.Bacc("TRN2", target_bir_lowering=False, num_devices=1)
    arrays = lay_out(inputs)
    io = {k: nc.dram_tensor(f"in_{k}", v.shape, F32, kind="ExternalInput").ap() for k, v in arrays.items()}
    io |= {k: nc.dram_tensor(k, s, F32, kind="ExternalOutput").ap() for k, s in OUTS.items()}
    build(nc, io)
    r = run_bass_kernel_spmd(nc, [{f"in_{k}": v for k, v in arrays.items()}], core_ids=[0])
    return gather_outputs({k: r.results[0][k] for k in OUTS})
```

```python
from contextlib import ExitStack
import concourse.bass as bass
from concourse import mybir
import numpy as np

F32 = mybir.dt.float32
F32R = mybir.dt.float32r
I32 = mybir.dt.int32
ALU = mybir.AluOpType
ACT = mybir.ActivationFunctionType
AX = mybir.AxisListType

P = 128
D_MODEL, DEPTH = 1024, 2
SEQ, NSEQ, DSEQ, PAST = 256, 8, 4, 2048
SAMP = NSEQ * DSEQ
PLACES = 128
TOK = SEQ + SAMP
KD = D_MODEL // P
D_PLE, D_FF, NE, TOP_K, NF = 256, 2816, 8, 2, 2816 // 128
EPS = 1e-6
PAIR = 416
RING, TILE = 11, 1024
SHARED = 15360
HIGHS, LOWS = 4, 3
ZW = 320
TB = [(0, 128), (128, 128), (256, 32)]
SEGS = [(128, 0, 256, 0), (128, 128, 256, 256), (32, 256, 288, 384)]

GLA, RET, GDN, SSD = range(4)
LEVELS = [128, 64, 32, 16, 8, 4]
DIRECT = 4
BAND = 4
HEADS = [4, 4, 4, 8]
HBASE = [0, 4, 8, 12]
NHEAD = 20
DV = [128, 128, 128, 64]
ZBLOCKS = [12, 12, 12, 10]
NCONV = [0, 0, 8, 6]
CONV0 = [0, 0, 0, 8]
GATE0 = [8, 8, 8, 6]
OUT0 = [4, 4, 0, 0]
SSD_COL = {GDN: 4, SSD: 8}

_SP = (256, 256, 512, 16, 512, 256, 256, 512, 512, 1024, 4, 4, 512, 512, 768, 8, 4096)
_C = np.concatenate([[0], np.cumsum(_SP)]).tolist()
ZCOLS = [
    [_C[0] + 128 * i for i in range(8)] + [_C[4] + 128 * i for i in range(4)],
    [_C[5] + 128 * i for i in range(12)],
    [_C[9] + 128 * i for i in range(8)] + [_C[12] + 128 * i for i in range(4)],
    [_C[14] + 128 * i for i in range(6)] + [_C[13] + 128 * i for i in range(4)],
]
ZSCALE = [
    [0.125] * 2 + [1.0] * 6 + [0.5] * 4,
    [1.0] * 2 + [0.125] * 2 + [1.0] * 4 + [0.5] * 4,
    [1.0] * 8 + [0.5] * 4,
    [1.0] * 6 + [0.5] * 4,
]


def half_pair(n, h):
    return (h // 4, h % 4) if n == SSD else (h % 2, h // 2)


def _block_masks():
    j, i = np.arange(P)[:, None], np.arange(P)[None, :]
    s, t = np.arange(SAMP)[:, None], np.arange(SAMP)[None, :]
    same = (s // DSEQ) == (t // DSEQ)
    return j, i, s, t, same


def constants():
    j, i, s, t, same = _block_masks()
    f = np.float32

    def packed(big, off, small):
        m = np.zeros((P, PAIR), f)
        m[:, 0:128], m[:, 128:256], m[:, 256:384], m[:32, 384:416] = big, off, big, small
        return m

    def pad(a):
        m = np.zeros((P, a.shape[1]), f)
        m[:a.shape[0]] = a
        return m

    c = {}
    c["ones"] = np.ones((P, P))
    c["eps"] = np.full((P, 1), EPS)
    c["ident"] = np.eye(P)
    c["halfones"] = (j // 64 == i // 64) * 1.0
    c["upto"] = np.concatenate([j <= i, np.ones((P, P))], 1)
    c["after"] = (j > i) * 1.0
    c["upto_s"] = pad((same & (s <= t)) * 1.0)
    c["after_s"] = pad((same & (s > t)) * 1.0)
    c["future"] = packed(np.where(j <= i, 0, -1e30), 0, np.where(same & (s <= t), 0, -1e30))
    c["strict"] = packed(j < i, 1, same & (s < t))
    c["seq_of"] = pad((np.arange(SAMP)[:, None] // DSEQ == np.arange(NSEQ)[None, :]) * 1.0)
    pos = np.concatenate([np.arange(SEQ), PAST + np.tile(np.arange(DSEQ), NSEQ)]).astype(np.float64)
    inv = 10000.0 ** (-np.arange(32, dtype=np.float32).astype(np.float64) / 32)
    inv = inv.astype(f)
    ang = (pos.astype(f)[None, :] * np.tile(inv, 4)[:, None]).astype(f).astype(np.float64)
    c["cos"], c["sin"] = np.cos(ang), np.sin(ang)
    rot = np.zeros((P, P))
    for q in range(P):
        d = q % 64
        if d < 32:
            rot[q + 32, q] = -1.0
        else:
            rot[q - 32, q] = 1.0
    c["rot"] = rot
    lgam = np.log(1.0 - 2.0 ** (-5.0 - np.arange(4)))
    seg, kd = [], np.zeros((P, 3, 16))
    eg = np.zeros((P, 2, SAMP))
    for h in range(4):
        big = np.where(j <= i, np.exp(np.minimum(i - j, 999) * lgam[h] * (j <= i)), 0)
        off = np.exp((i + P - j) * lgam[h])
        small = np.where(same & (s <= t), np.exp(np.where(same & (s <= t), t - s, 0) * lgam[h]), 0)
        seg.append(packed(big, off, small))
        kd[:, 0, h] = np.exp((SEQ - 1 - np.arange(P)) * lgam[h])
        kd[:, 1, h] = np.exp((P - 1 - np.arange(P)) * lgam[h])
        kd[:SAMP, 2, h] = np.exp((DSEQ - 1 - np.arange(SAMP) % DSEQ) * lgam[h])
        eg[64 * (h % 2):64 * (h % 2) + 64, h // 2, :] = np.exp((np.arange(SAMP) % DSEQ + 1) * lgam[h])
    c["ret_decay"] = np.concatenate(seg, 1)
    c["ret_kd"] = kd.reshape(P, 48)
    c["ret_eg"] = eg.reshape(P, 64)
    lv = []
    for w in (1, 2, 4, 8, 16, 32, 64):
        lv.append((j // (2 * w) == i // (2 * w)) & (j % (2 * w) < w) & (i % (2 * w) >= w))
    c["levels"] = np.concatenate(lv, 1)
    hs = np.zeros((P, 48))
    hs[:64, 15], hs[64:, 31] = 1, 1
    c["row_pick"] = hs
    rep = np.zeros((P, 2, P))
    reps = np.zeros((P, 2, SAMP))
    for h in range(2):
        for q in range(P):
            rep[16 * h + q % BAND, h, q] = 1
        for q in range(SAMP):
            reps[16 * h + q % DSEQ, h, q] = 1
    c["spread"] = rep.reshape(P, -1)
    c["spread_s"] = reps.reshape(P, -1)
    dm = np.zeros((P, TOK))
    dm[:, :128] = (j // BAND == i // BAND) & (j <= i)
    dm[:, 128:256] = dm[:, :128]
    dm[:SAMP, 256:] = same & (s <= t)
    c["sub_diag"] = dm
    c["less"] = np.tile((np.arange(8)[None, :] < np.arange(8)[:, None]).reshape(1, 64) * 1.0, (P, 1))
    c["slot_row"] = np.tile(np.arange(P)[None, :] * 1.0, (P, 1))
    c["slot_col"] = np.arange(P)[:, None] * 1.0
    return {k: np.ascontiguousarray(v, dtype=f) for k, v in c.items()}


CONST = constants()
CAT = {}
_n = 0
for _k, _v in CONST.items():
    CAT[_k] = (_n, _v.shape[1])
    _n += _v.shape[1]
NCONST = _n

PV = {}
_n = 0
for _k, _w in (("norm_mix", 8), ("norm_ffn", 8), ("norm_ple", 8), ("norm_final", 8), ("gla_norm", 1),
               ("ret_norm", 1), ("gdn_norm", 1), ("ssd_norm", 4), ("conv_w", 56), ("conv_b", 14), ("ssd_d", 4)):
    PV[_k] = (_n, _w)
    _n += _w
NPV = _n


def tile_table():
    out = []
    for L in range(DEPTH):
        def z(n):
            return [("z", L, n, b) for b in range(ZBLOCKS[n])]

        def mg(n):
            return [("mg", L, n, b) for b in range(KD)]

        def br(n):
            return [("br", L, n, b) for b in range(4)]

        out += z(0)
        out += z(1) + mg(0)
        out += br(0) + z(2) + mg(1)
        out += br(1) + z(3) + mg(2)
        out += br(2) + mg(3)
        out += br(3)
        out += [("out", L, 0, b) for b in range(KD)]
        if L % 2 == 0:
            for b in range(NF):
                out += [("gate", L, 0, b), ("up", L, 0, b)]
            out += [("down", L, 0, b) for b in range(NF)]
        else:
            out += [("experts", L, 0, 0)]
        out += [("pproj", L, 0, b) for b in range(2)]
        out += [("pgate", L, 0, b) for b in range(KD)]
    return out

TABLE = tile_table()
EXPERT_AT = next(i for i, x in enumerate(TABLE) if x[0] == "experts")
PLAIN = [x for x in TABLE if x[0] != "experts"]
T_OF = {x: i for i, x in enumerate(PLAIN)}
E_TILES = 3 * NF
SLOTS = [
    [2, 2, 2, 1, 1, 1, 1, 0, 1, 0, 1, 1, 1, 1, 1, 1, 1, 2],
    [3, 2, 2, 3, 3, 2, 2, 2, 2, 3],
    [1, 0, 1, 1, 0, 1, 0, 2, 0, 1, 0, 0, 2, 1, 0, 1, 0, 1, 0, 1, 0, 1, 0, 1, 0, 1, 1, 0, 0, 0, 1,
     1, 0, 0, 0, 0, 0, 1, 1, 1, 0],
    [0, 1, 1, 2, 1, 0, 1, 0, 0, 1, 0, 0, 0, 0, 0, 0, 0, 1, 0, 1, 0, 2, 1],
]
NSLOT = [len(x) for x in SLOTS]


def fill_tiles(L):
    out = []
    for n in range(4):
        mine = [x for x in PLAIN if x[1] == L and ((x[0] == "z" and x[2] == n + 1) or (x[0] == "mg" and x[2] == n) or
                                                  (x[0] == "br" and x[2] == n - 1))]
        mine.sort(key=lambda x: T_OF[x])
        assert sum(SLOTS[n]) == len(mine), (n, sum(SLOTS[n]), len(mine))
        at = np.cumsum([0] + SLOTS[n])
        out.append([mine[at[s]:at[s + 1]] for s in range(len(SLOTS[n]))])
    return out


FILL = [fill_tiles(L) for L in range(DEPTH)]
TAKER = {"z": "act", "mg": "act", "br": "dve", "out": "dve", "gate": "ffn", "up": "ffn", "down": "ffn",
         "pproj": "act", "pgate": "ple"}


def taken_before(t, who):
    return sum(2 if x[0] == "br" else 1 for x in PLAIN[:max(t, 0)] if TAKER[x[0]] == who)


def bank_free(t, o):
    for r in range(t - 1, -1, -1):
        kind = PLAIN[r][0]
        who = TAKER[kind]
        if kind == "br":
            return who, taken_before(r, who) + o + 1
        if kind in ("z", "mg", "out", "pgate") and r % 2 == o:
            return who, taken_before(r + 1, who)
    return None, 0


def build(nc, io):
    ctx = ExitStack()
    with ctx:
        def semaphore(name):
            return ctx.enter_context(nc.semaphore(name))

        slot_in = [semaphore(f"slot{j}_in") for j in range(RING)]
        expert_slot_in = [semaphore(f"expert_slot{j}_in") for j in range(RING)]
        const_in = semaphore("const_in")
        norm_const_in = semaphore("norm_const_in")
        x_in = semaphore("x_in")
        tile_done = semaphore("tile_done")
        branch_ps = semaphore("branch_ps")
        rounds_ready = semaphore("rounds_ready")
        expert_slots = semaphore("expert_slots")
        experts_done = semaphore("experts_done")
        o_final = semaphore("o_final")
        square_ready = semaphore("square_ready")
        sumsq_ps = semaphore("sumsq_ps")
        u_ready = semaphore("u_ready")
        params_in = [semaphore(f"params{L}_in") for L in range(DEPTH)]
        small_in = [semaphore(f"small{L}_in") for L in range(DEPTH)]
        small_ps = semaphore("small_ps")
        glr_ready = semaphore("glr_ready")
        gk_ps = semaphore("gk_ps")
        logd_ready = semaphore("logd_ready")
        cum_ps = semaphore("cum_ps")
        vk_ps = semaphore("vk_ps")
        grow_taken = semaphore("grow_taken")
        vk_taken = semaphore("vk_taken")
        grow_ps = semaphore("grow_ps")
        pt_ready = semaphore("pt_ready")
        o_taken = semaphore("o_taken")
        qg_ready = semaphore("qg_ready")
        state_in = semaphore("state_in")
        o_ps = semaphore("o_ps")
        scores_ps = semaphore("scores_ps")
        masked_ready = semaphore("masked_ready")
        masked_used = semaphore("masked_used")
        state_new = semaphore("state_new")
        osq_ready = semaphore("osq_ready")
        osum_ps = semaphore("osum_ps")
        cross_zero = semaphore("cross_zero")
        ldiff_ready = semaphore("ldiff_ready")
        lexp_ready = semaphore("lexp_ready")
        lev_ready = semaphore("lev_ready")
        lev_ps = semaphore("lev_ps")
        masked_taken = semaphore("masked_taken")
        sub_ready = semaphore("sub_ready")
        sub_ps = semaphore("sub_ps")
        band_ready = semaphore("band_ready")
        spread_ps = semaphore("spread_ps")
        qksq_ready = semaphore("qksq_ready")
        qksum_ps = semaphore("qksum_ps")
        qk_ready = semaphore("qk_ready")
        beta_ps = semaphore("beta_ps")
        kb_ready = semaphore("kb_ready")
        kk_ps = semaphore("kk_ps")
        mask_s_ready = semaphore("mask_s_ready")
        inv_s_ready = semaphore("inv_s_ready")
        p_s_ps = semaphore("p_s_ps")
        p_s_ready = semaphore("p_s_ready")
        x_s_ps = semaphore("x_s_ps")
        mask_ready = semaphore("mask_ready")
        mask1_ready = semaphore("mask1_ready")
        inv_ready = semaphore("inv_ready")
        p_ps = semaphore("p_ps")
        p_ready = semaphore("p_ready")
        x_ps = semaphore("x_ps")
        vn0_ps = semaphore("vn0_ps")
        kbg_ready = semaphore("kbg_ready")
        ks_ps = semaphore("ks_ps")
        vn0_ready = semaphore("vn0_ready")
        r1_ps = semaphore("r1_ps")
        ks_ready = semaphore("ks_ready")
        kst_ps = semaphore("kst_ps")
        r1_ready = semaphore("r1_ready")
        vn1_ps = semaphore("vn1_ps")
        vn1_ready = semaphore("vn1_ready")
        rot_ps = semaphore("rot_ps")
        rope_ready = semaphore("rope_ready")
        conv_ready = semaphore("conv_ready")
        hid_ready = semaphore("hid_ready")
        router_in = semaphore("router_in")
        logit_ps = semaphore("logit_ps")
        utok_ps = semaphore("utok_ps")
        sel_ready = semaphore("sel_ready")
        pos_ps = semaphore("pos_ps")
        pos_ready = semaphore("pos_ready")
        rows_taken = semaphore("rows_taken")
        rows_ps = semaphore("rows_ps")
        gather_ready = semaphore("gather_ready")
        gather_ps = semaphore("gather_ps")
        xg_ready = semaphore("xg_ready")
        ehid_ready = semaphore("ehid_ready")
        scatter_ready = semaphore("scatter_ready")
        y_taken = semaphore("y_taken")
        y_ps = semaphore("y_ps")
        ehid_low_ready = semaphore("ehid_low_ready")
        w_high_ready = semaphore("w_high_ready")
        w_low_ready = semaphore("w_low_ready")
        scatter_ps = semaphore("scatter_ps")
        expert_added = semaphore("expert_added")
        ple_loaded = semaphore("ple_loaded")
        stream_act = semaphore("stream_act")
        stream_ple = semaphore("stream_ple")
        cum_taken_dve = semaphore("cum_taken_dve")
        cum_taken_act = semaphore("cum_taken_act")
        acc_ready = semaphore("acc_ready")
        stream_dve = semaphore("stream_dve")
        rt_ready = semaphore("rt_ready")
        abs_small = semaphore("abs_small")
        abs_gate = semaphore("abs_gate")
        act_step = semaphore("act_step")
        logs_ready = semaphore("logs_ready")
        rows_saved = semaphore("rows_saved")
        gate_tanh = semaphore("gate_tanh")
        y_ready = semaphore("y_ready")
        ort_ready = semaphore("ort_ready")
        decay_ready = semaphore("decay_ready")
        eg_ready = semaphore("eg_ready")
        convsum_ready = semaphore("convsum_ready")
        ctan_ready = semaphore("ctan_ready")
        diff_ready = semaphore("diff_ready")
        ediff_ready = semaphore("ediff_ready")
        qkrt_ready = semaphore("qkrt_ready")
        tanh_ready = semaphore("tanh_ready")
        expw_ready = semaphore("expw_ready")
        etanh_ready = semaphore("etanh_ready")
        gate_used = semaphore("gate_used")
        dve_step = semaphore("dve_step")
        stp_out = semaphore("stp_out")
        state_decayed = semaphore("state_decayed")
        pads_ready = semaphore("pads_ready")
        qk_prod = semaphore("qk_prod")
        mt_ready = semaphore("mt_ready")
        esilu_ready = semaphore("esilu_ready")
        round_step = semaphore("round_step")
        state_out = semaphore("state_out")
        conv_out = semaphore("conv_out")
        y_out = semaphore("y_out")

        def sb(name, cols, dt=F32):
            return ctx.enter_context(nc.sbuf_tensor(name, [P, cols], dt))

        h = sb("h", KD * TOK)[:, :].rearrange("p (k t) -> p k t", k=KD)
        u = sb("u", KD * TOK)[:, :].rearrange("p (k t) -> p k t", k=KD)
        acc_t = sb("acc", KD * TOK)
        acc = acc_t[:, :].rearrange("p (k t) -> p k t", k=KD)
        ring = sb("ring", RING * TILE)
        const = sb("const", NCONST)
        pv = sb("pv", NPV)
        wsm = sb("wsm", 8 * 32)[:, :].rearrange("p (k c) -> p k c", k=KD)
        wgk = sb("wgk", 256)
        rows = sb("rows", 32)
        used = NCONST + 3 * KD * TOK + RING * TILE + NPV + 256 + 256 + 32
        arena = sb("arena", SHARED)
        TAIL = 212600 // 4 - used - 8 - SHARED
        at = [0]

        def carve(cols):
            at[0] += cols
            if at[0] <= SHARED:
                return arena[:, at[0] - cols:at[0]]
            assert at[0] <= SHARED + TAIL and at[0] - cols >= SHARED, at[0]
            return tail[:, at[0] - cols - SHARED:at[0] - SHARED]

        def C(name, a=0, b=None):
            o, w = CAT[name]
            return const[:, o + a:o + (w if b is None else b)]

        def PVc(name, k=0):
            return pv[:, PV[name][0] + k:PV[name][0] + k + 1]

        ps_t = ctx.enter_context(nc.psum_tensor("ps", [P, 8, 512], F32))

        def bank(k):
            return ps_t[:, k, :]

        M = 2

        with nc.sbuf_tensor("mixer_memory", [P, TAIL], F32) as tail:
            zset = [carve(12 * ZW).rearrange("p (b w) -> p b w", w=ZW) for _ in range(2)]
            mg = carve(KD * TOK).rearrange("p (k t) -> p k t", k=KD)
            cv = carve(KD * TOK).rearrange("p (k t) -> p k t", k=KD)
            vtok = carve(3 * 512).rearrange("p (b c) -> p b c", b=3)
            kdec = carve(3 * 512).rearrange("p (b c) -> p b c", b=3)
            st = carve(2048)
            stp = carve(256)
            masks = carve(1024)
            pt = carve(4 * PAIR).rearrange("p (h c) -> p h c", h=4)
            xs, ab, ls, gcol, kde = [carve(48).rearrange("p (b c) -> p b c", b=3) for _ in range(5)]
            ea = carve(16)
            egp = carve(4 * SAMP).rearrange("p (q t) -> p q t", q=4)
            qg = carve(4 * SAMP).rearrange("p (q t) -> p q t", q=4)
            tmp4 = carve(4 * TOK).rearrange("p (k t) -> p k t", k=4)
            rs4 = carve(4 * TOK).rearrange("p (k t) -> p k t", k=4)
            csave = carve(14 * 27).rearrange("p (b c) -> p b c", b=14)
            hist = carve(14 * 24).rearrange("p (b c) -> p b c", b=14)
            brt = carve(2 * TOK).rearrange("p (k t) -> p k t", k=2)
            shared = at[0]
            glrt = carve(TOK)
            gx = carve(3 * 256).rearrange("p (b c) -> p b c", b=3)
            gt = carve(2 * TOK).rearrange("p (q t) -> p q t", q=2)
            lev = carve(2 * 2 * SEQ).rearrange("p (a q t) -> p a q t", a=2, q=2)
            near = lev.rearrange("p a q t -> p (a q) t")
            dd = tmp4.rearrange("p (a q) t -> p a q t", a=2)
            qk = rs4.rearrange("p (a q) t -> p a q t", a=2)
            band = brt
            dtmp = carve(TOK)
            at[0] = shared
            dmat = carve(8 * PAIR).rearrange("p (h c) -> p h c", h=8)
            at[0] = shared + 4 * PAIR
            xm = rs4.rearrange("p k t -> p (k t)")[:, 0:1024].rearrange("p (h b c) -> p h b c", h=4, b=2)
            xt = carve(1024).rearrange("p (h b c) -> p h b c", h=4, b=2)
            msk = tmp4.rearrange("p k t -> p (k t)")[:, 0:1024].rearrange("p (h b c) -> p h b c", h=4, b=2)
            pb = masks.rearrange("p (h b c) -> p h b c", h=4, b=2)
            kb = carve(2 * TOK).rearrange("p (q t) -> p q t", q=2)
            kbg = carve(2 * SAMP).rearrange("p (q t) -> p q t", q=2)
            xs_s, xt_s, ms_s, pb_s = [carve(128).rearrange("p (h c) -> p h c", h=4) for _ in range(4)]
        at[0] = 0
        hid = carve(NF * TOK).rearrange("p (f t) -> p f t", f=NF)
        at[0] = 12 * 2 * ZW
        tanh_t = carve(2 * TOK).rearrange("p (a t) -> p a t", a=2)
        silu_t = carve(2 * TOK).rearrange("p (a t) -> p a t", a=2)
        at[0] = 12 * 2 * ZW + KD * TOK
        ple_in = carve(2 * TOK).rearrange("p (k t) -> p k t", k=2)
        ple_pj = hid[:, 0:KD, :]
        at[0] = 12 * 2 * ZW + 2 * KD * TOK
        utok = carve(3 * D_MODEL).rearrange("p (b c) -> p b c", b=3)
        at[0] = 2 * NE * TOK
        rank_t, less_t = [carve(3 * 64).rearrange("p (b e f) -> p b e f", b=3, e=8) for _ in range(2)]
        logit, sel, wts = [carve(3 * 8).rearrange("p (b e) -> p b e", b=3) for _ in range(3)]
        posm = carve(3 * 9).rearrange("p (b e) -> p b e", b=3)
        mx = carve(4)
        nrt = carve(1).bitcast(I32)
        cnt = carve(8)
        slotrow, slotcol = carve(PLACES), carve(1)
        gath = carve(3 * PLACES).rearrange("p (b c) -> p b c", b=3)
        scat = carve(TOK)
        yt = carve(D_MODEL)
        router = carve(64).rearrange("p (k e) -> p k e", k=KD)
        at[0] = 0
        posrow, wrow = [carve(NE * TOK).rearrange("p (e t) -> p e t", e=NE) for _ in range(2)]
        at[0] = 12 * 2 * ZW
        etanh, esilu = [carve(2 * PLACES).rearrange("p (a t) -> p a t", a=2) for _ in range(2)]
        xg = carve(KD * PLACES).rearrange("p (k c) -> p k c", k=KD)
        ehid = carve(2 * PLACES).rearrange("p (a c) -> p a c", a=2)
        e_high, e_low = [sb(f"hidden_{x}", NF * PLACES, F32R)[:, :].rearrange("p (f c) -> p f c", f=NF)
                         for x in ("high", "low")]
        w_high = sb("weights_high", HIGHS * TILE, F32R)[:, :].rearrange("p (a c) -> p a c", a=HIGHS)
        w_low = sb("weights_low", LOWS * TILE, F32R)[:, :].rearrange("p (a c) -> p a c", a=LOWS)

        cbuf = pt.rearrange("p h c -> p (h c)")[:, 0:640].rearrange("p (a c) -> p a c", a=2)
        ctan = pt.rearrange("p h c -> p (h c)")[:, 640:1280].rearrange("p (a c) -> p a c", a=2)

        class Steps:

            def __init__(self):
                self.n = 0

            def next(self):
                self.n += 1
                return self.n

        def zblk(n, b):
            return zset[n % 2][:, b, :]

        def ob(n, hh):
            if n == SSD:
                return zblk(n, hh // 2)[64 * (hh % 2):64 * (hh % 2) + 64, 0:TOK]
            return zblk(n, OUT0[n] + hh)[:, 0:TOK]

        def qk_of(n, hh):
            half, pair = half_pair(n, hh)
            r = slice(64 * half, 64 * half + 64)
            if n == GDN:
                return cv[r, 2 + pair, :], cv[r, pair, :]
            if n == SSD:
                return cv[r, 4, :], cv[r, 5, :]
            return zblk(n, 2 + pair)[r, 0:TOK], zblk(n, pair)[r, 0:TOK]

        def gate_of(n):
            if n == SSD:
                return dmat.rearrange("p h c -> p (h c)")[:, 0:4 * TOK].rearrange("p (k t) -> p k t", k=4)
            return cv[:, 4:8, :]

        def squares(k):
            return u if k % 3 == 1 else acc

        def sumsq_bank(k):
            return bank(0 if k % 3 == 2 else M)[:, 0:TOK]

        def halves_of(x, w):
            v = x[:, :, 0:SEQ].rearrange("p q (s w) -> p q s w", w=2 * w)
            return v[:, :, :, 0:w], v[:, :, :, w:2 * w]

        def runs(x, jj):
            return x.rearrange("p q (s w) -> p q s w", w=BAND)[:, :, :, jj:BAND]

        def st_of(n):
            return st.rearrange("p (q b v) -> p q b v", b=NSEQ, v=DV[n])

        def pads(rows_first):
            return [(P, slice(0, 2)), (SAMP, slice(2, 3))]

        block = ctx.enter_context(nc.Block())

        def small(L, queue):
            queue.dma_start(pv[:, :], io["pv"][L]).then_inc(params_in[L], 16)
            queue.dma_start(wsm.rearrange("p k c -> p (k c)"), io["wsm"][L]).then_inc(small_in[L], 16)
            queue.dma_start(wgk[0:17, :], io["wgk"][L]).then_inc(small_in[L], 16)
            queue.dma_start(rows[:, :], io["rows"][L]).then_inc(small_in[L], 16)
            queue.dma_start(hist.rearrange("p b c -> p (b c)"), io["hist"][L]).then_inc(small_in[L], 16)

        @block.sync
        def _(sp):
            sp.dma_start(h.rearrange("p k t -> p (k t)"), io["x"]).then_inc(x_in, 16)
            head = P + 1
            sp.dma_start(const[:, 0:head], io["const"][:, 0:head]).then_inc(norm_const_in, 16)

            def plain(lo, hi):
                for t in range(lo, hi):
                    if t >= RING:
                        sp.wait_ge(tile_done, t - RING + 1)
                    row = t if t < EXPERT_AT else t + NE * E_TILES
                    sp.dma_start(ring[:, (t % RING) * TILE:(t % RING + 1) * TILE],
                                 io["stream"][row]).then_inc(slot_in[t % RING], 16)

            small(0, sp)
            plain(0, 4)
            sp.dma_start(const[:, head:], io["const"][:, head:]).then_inc(const_in, 16)
            plain(4, RING)
            turns = EXPERT_AT // RING
            with sp.Fori(1, turns) as g:
                for j in range(RING):
                    sp.wait_ge(tile_done, (g - 1) * RING + (j + 1))
                    sp.dma_start(ring[:, j * TILE:(j + 1) * TILE],
                                 io["stream"][bass.ds(g * RING + j, 1)].rearrange("a p c -> p (a c)")
                                 ).then_inc(slot_in[j], 16)
            plain(turns * RING, EXPERT_AT)
            sp.wait_ge(rounds_ready, 1)
            rounds = sp.value_load(nrt[0:1, 0:1], min_val=1, max_val=3)
            with sp.Fori(0, rounds) as r:
                with sp.Fori(0, NE) as e:
                    for k in range(E_TILES):
                        j = k % RING
                        sp.wait_ge(expert_slots, r * (NE * E_TILES) + e * E_TILES + (k + 1))
                        sp.dma_start(ring[:, j * TILE:(j + 1) * TILE],
                                     io["stream"][bass.ds(e * E_TILES + (EXPERT_AT + k), 1)].rearrange("a p c -> p (a c)")
                                     ).then_inc(expert_slot_in[j], 16)
            sp.wait_ge(experts_done, 1)
            plain(EXPERT_AT, len(PLAIN))

        @block.tensor
        def _(pe):
            mm = nc.tensor.matmul

            def weights(x):
                t = T_OF[x]
                pe.wait_ge(slot_in[t % RING], 16 * (t // RING + 1))
                return [ring[:, (t % RING) * TILE + P * i:(t % RING) * TILE + P * i + P] for i in range(8)]

            def bank_is_free(t, o):
                who, count = bank_free(t, o)
                if who == "act":
                    pe.wait_ge(stream_act, count)
                elif who == "dve":
                    pe.wait_ge(stream_dve, count)
                elif who == "ple":
                    pe.wait_ge(stream_ple, count)

            def stream_tile(x):
                t = T_OF[x]
                kind, L, n, b = x
                if kind == "pproj" and b == 1:
                    pe.wait_ge(stream_act, taken_before(t, "act"))
                if kind == "br":
                    pe.wait_ge(o_final, 4 * L + n + 1)
                w = weights(x)
                if kind in ("z", "mg", "pgate", "out"):
                    bank_is_free(t, t % 2)
                    for k in range(KD):
                        if (kind, n, b) in (("z", 0, 0), ("pgate", 0, 0)):
                            pe.wait_ge(u_ready, KD * (3 * L + (2 if kind == "pgate" else 0)) + k + 1)
                        last = mm(bank(t % 2)[:, 0:TOK], w[k], (acc if kind == "out" else u)[:, k, :],
                                  start=k == 0, stop=k == KD - 1)
                elif kind == "br":
                    for o in range(2):
                        bank_is_free(t, o)
                        for k in range(4):
                            src = zblk(n, OUT0[n] + k)[:, 0:TOK]
                            last = mm(bank(o)[:, 0:TOK], w[4 * o + k], src, start=k == 0, stop=k == 3)
                        if o == 0:
                            last.then_inc(branch_ps, 1)
                elif kind == "pproj":
                    for o in range(4):
                        for k in range(2):
                            last = mm(bank(M + o)[:, 0:TOK], w[2 * o + k], ple_in[:, k, :], start=k == 0, stop=k == 1)
                last.then_inc(tile_done, 1)

            def fill(L, n, s):
                for x in FILL[L][n][s]:
                    stream_tile(x)

            def norm(k):
                for i in range(KD):
                    pe.wait_ge(square_ready, KD * k + i + 1)
                    last = mm(sumsq_bank(k), C("ones"), squares(k)[:, i, :], start=i == 0, stop=i == KD - 1)
                last.then_inc(sumsq_ps, 1)

            def pair_scores(dst, lhs, rhs):
                for n_rows, i0, i1, c0 in SEGS:
                    j0 = {0: 0, 256: 128, 384: 256}[c0]
                    last = mm(dst[0:n_rows, c0:c0 + i1 - i0], lhs[:, j0:j0 + n_rows], rhs[:, i0:i1],
                              start=True, stop=True)
                return last

            def prep(L):
                pe.wait_ge(small_in[L], 16 * 4)
                for k in range(KD):
                    mm(bank(M)[0:16, 0:TOK], wsm[:, k, 0:16], u[:, k, :], start=k == 0, stop=k == KD - 1)
                for b, (t0, nt) in enumerate(TB):
                    for k in range(KD):
                        last = mm(bank(M + 1)[0:nt, 16 * b:16 * b + 16], u[:, k, t0:t0 + nt], wsm[:, k, 16:32],
                                  start=k == 0, stop=k == KD - 1)
                last.then_inc(small_ps, 1)
                pe.wait_ge(glr_ready, L + 1)
                for b, (t0, nt) in enumerate(TB):
                    last = mm(bank(M + 2 + b // 2)[0:nt, 256 * (b % 2):256 * (b % 2) + 256],
                              glrt[0:17, t0:t0 + nt], wgk[0:17, :], start=True, stop=True)
                last.then_inc(gk_ps, 1)
                for b in range(4, ZBLOCKS[0]):
                    stream_tile(("z", L, 0, b))
                pe.wait_ge(logd_ready, L + 1)
                up, af, on = C("upto", 0, 128), C("after"), C("ones")
                g, r = bank(M), bank(M)[:, 48:96]
                mm(g[:, 0:16], up, ls[:, 0, :], start=True, stop=True)
                mm(g[:, 16:32], on, ls[:, 0, :], start=True, stop=False)
                mm(g[:, 16:32], up, ls[:, 1, :], start=False, stop=True)
                mm(g[0:32, 32:48], C("upto_s")[0:32], ls[0:32, 2, :], start=True, stop=True)
                mm(r[:, 0:16], on, ls[:, 1, :], start=True, stop=False)
                mm(r[:, 0:16], af, ls[:, 0, :], start=False, stop=True)
                mm(r[:, 16:32], af, ls[:, 1, :], start=True, stop=True)
                mm(r[0:32, 32:48], C("after_s")[0:32], ls[0:32, 2, :], start=True, stop=True)
                mm(bank(M + 1)[:, 0:256], on, gx[:, 1, :], start=True, stop=False)
                mm(bank(M + 1)[:, 0:256], af, gx[:, 0, :], start=False, stop=True)
                mm(bank(M + 1)[:, 256:512], af, gx[:, 1, :], start=True, stop=True)
                mm(bank(M + 2)[0:32, 0:256], C("after_s")[0:32], gx[0:32, 2, :], start=True, stop=True)
                for q in range(2):
                    c = slice(128 * q, 128 * q + 128)
                    d = bank(M + 3 + q)
                    mm(d[:, 0:256], gx[:, 0, c], C("upto"), start=True, stop=True)
                    mm(d[:, 128:256], gx[:, 1, c], up, start=False, stop=True, skip_group_check=True)
                    last = mm(d[:, 256:288], gx[0:32, 2, c], C("upto_s")[0:32], start=False, stop=True,
                              skip_group_check=True)
                last.then_inc(cum_ps, 1)

            def transposes(L, n):
                tr = nc.tensor.transpose
                for b, (t0, nt) in enumerate(TB):
                    for c in range(4):
                        if n == GDN:
                            src = cv[:, 4 + c, t0:t0 + nt]
                        elif n == SSD:
                            src = cv[:, c, t0:t0 + nt]
                        else:
                            src = zblk(n, 4 + c)[:, t0:t0 + nt]
                        tr(bank(M + b)[0:nt, 128 * c:128 * c + 128], src, C("ident"))
                    for c in range(1 if n == SSD else 2):
                        ksrc = {GDN: cv[:, 2 + c, :], SSD: cv[:, 4, :]}.get(n, None)
                        if ksrc is None:
                            ksrc = zblk(n, 2 + c)[:, 0:TOK]
                        last = tr(bank(M + 3 + b // 2)[0:nt, 256 * (b % 2) + 128 * c:256 * (b % 2) + 128 * c + 128],
                                  ksrc[:, t0:t0 + nt], C("ident"))
                last.then_inc(vk_ps, 1)

            def decays(L, n):
                for hh in range(HEADS[n]):
                    k = L * 12 + (hh if n == GDN else 4 + hh)
                    if hh >= 2:
                        pe.wait_ge(grow_taken, k - 1)
                    else:
                        pe.wait_ge(vk_taken, 4 * L + n + 1)
                    d = bank(M + 2 + hh % 2)
                    c = SSD_COL[n] + hh
                    mm(d[:, 0:256], ls[:, 0, c:c + 1].to_broadcast([P, P]), C("upto"), start=True, stop=True)
                    mm(d[:, 128:256], ls[:, 1, c:c + 1].to_broadcast([P, P]), C("upto", 0, 128),
                       start=False, stop=True, skip_group_check=True)
                    mm(d[:, 256:288], ls[0:32, 2, c:c + 1].to_broadcast([32, P]), C("upto_s")[0:32],
                       start=False, stop=True, skip_group_check=True).then_inc(grow_ps, 1)
                    if hh % 2:
                        fill(L, n, (11 if n == GDN else 9) + hh // 2)

            def core(L, n, slot):
                m, dv = 4 * L + n, DV[n]

                def outputs(hh):
                    half, pair = half_pair(n, hh)
                    kr = slice(64 * half, 64 * half + 64)
                    orow = slice(64 * (hh % 2), 64 * (hh % 2) + 64) if n == SSD else slice(0, P)
                    gh = L * NHEAD + HBASE[n] + hh
                    pe.wait_ge(pt_ready, gh + 1)
                    if (gh - 1 if hh >= 2 else gh - hh) > 0:
                        pe.wait_ge(o_taken, gh - 1 if hh >= 2 else gh - hh)
                    if hh == 0:
                        pe.wait_ge(qg_ready, m + 1)
                        pe.wait_ge(state_in, 16 * (m + 1))
                    o = bank(M + 4 + ((hh // 2) if n == SSD else hh) % 2)[orow, :]
                    if n == SSD and hh >= 4:
                        pe.wait_ge(o_taken, gh - gh % 2 - 2)
                    p = pt[:, hh % 4, :]
                    v = [vtok[0:nt, b, dv * hh:dv * hh + dv] for b, (t0, nt) in enumerate(TB)]
                    mm(o[:, 0:256], v[0], p[:, 0:256], start=True, stop=True)
                    mm(o[:, 128:256], v[1], p[:, 256:384], start=False, stop=True, skip_group_check=True)
                    mm(o[:, 256:288], v[2], p[0:32, 384:416], start=False, stop=False, skip_group_check=True)
                    for b in range(NSEQ):
                        last = mm(o[:, 256 + 4 * b:260 + 4 * b], st_of(n)[kr, pair, b, :],
                                  qg[kr, pair, 4 * b:4 * b + 4], start=False, stop=True, skip_group_check=True)
                    last.then_inc(o_ps, 1)

                for hh in range(HEADS[n]):
                    gh = L * NHEAD + HBASE[n] + hh
                    if n != GLA:
                        kT, qT = qk_of(n, hh)
                        if hh < 2:
                            pe.wait_ge(qg_ready, m + 1)
                        elif n != SSD:
                            pe.wait_ge(pt_ready, gh - 1)
                        if n != SSD or hh % 4 == 0:
                            pair_scores(bank(M + (hh // 4 if n == SSD else hh % 2)), kT, qT).then_inc(scores_ps, 1)
                        if hh >= 1:
                            outputs(hh - 1)
                    else:
                        outputs(hh)
                    fill(L, n, slot + hh)
                if n != GLA:
                    outputs(HEADS[n] - 1)

            def out_sums(L, n):
                m = 4 * L + n
                pe.wait_ge(osq_ready, m + 1)
                if n == SSD:
                    for g in range(2):
                        for b in range(2):
                            last = mm(bank(M + g)[:, 0:TOK], C("ones"), tmp4[:, 2 * g + b, :], start=b == 0, stop=b == 1)
                else:
                    for b in range(4):
                        last = mm(bank(M + b)[:, 0:TOK], C("ones"), tmp4[:, b, :], start=True, stop=True)
                last.then_inc(osum_ps, 1)

            def states(L, n):
                m, dv = 4 * L + n, DV[n]
                pe.wait_ge(ort_ready, m + 1)
                pe.wait_ge(o_taken, L * NHEAD + HBASE[n] + HEADS[n])
                for hh in range(HEADS[n]):
                    half, pair = half_pair(n, hh)
                    r = slice(64 * half, 64 * half + 64)
                    gh = L * NHEAD + HBASE[n] + hh
                    kc = slice(64 * hh, 64 * hh + 64)
                    o = bank(M + 4)[r, dv * pair:dv * pair + dv]
                    v = vtok[:, :, dv * hh:dv * hh + dv]
                    mm(o, kdec[:, 0, kc], v[:, 0], start=True, stop=False)
                    mm(o, kdec[:, 1, kc], v[:, 1], start=False, stop=True)
                    pe.wait_ge(masked_ready, gh + 1)
                    mk = masks[0:32, 512 * (hh % 2):512 * (hh % 2) + 512]
                    if n == SSD:
                        last = mm(bank(M + pair)[r, :], kdec[0:32, 2, kc], mk, start=True, stop=True)
                    else:
                        for b in range(NSEQ):
                            last = mm(bank(M + 2 * pair + b // 4)[r, dv * (b % 4):dv * (b % 4) + dv],
                                      mk[:, 64 * b:64 * b + 64], v[0:32, 2], start=True, stop=True)
                    last.then_inc(masked_used, 1)

            def gla(L):
                m = 4 * L
                for lv, w in enumerate(LEVELS):
                    fill(L, GLA, lv)
                    if lv == 0:
                        pe.wait_ge(cross_zero, L + 1)
                    pe.wait_ge(lev_ready, 6 * L + lv + 1)
                    if lv == DIRECT + 1:
                        pe.wait_ge(masked_taken, 2 * L + 1)
                    for hh in range(4):
                        r = slice(64 * (hh % 2), 64 * (hh % 2) + 64)
                        e = lev[r, lv % 2, hh // 2, :]
                        if lv < DIRECT:
                            for c in range(0, SEQ, 2 * w):
                                row, col = c % P, w if w == P else c + w + P * (c // P)
                                last = mm(bank(M + hh)[row:row + w, col:col + w], e[:, c:c + w], e[:, c + w:c + 2 * w],
                                          start=True, stop=True)
                        else:
                            for b in range(2):
                                col = SEQ * (hh // 2) + P * b
                                last = mm(bank(M + 4 + hh % 2)[:, col:col + P], e[:, P * b:P * b + P],
                                          e[:, P * b:P * b + P], start=True, stop=True)
                    last.then_inc(lev_ps, 1)
                pe.wait_ge(masked_taken, 2 * L + 2)
                for jj in range(BAND):
                    pe.wait_ge(sub_ready, BAND * L + jj + 1)
                    for q in range(2):
                        last = mm(bank(M + 4 + q)[0:32, 0:TOK], C("row_pick", 15 - jj, 47 - jj), dd[:, jj % 2, q, :],
                                  start=jj == 0, stop=jj == BAND - 1)
                    last.then_inc(sub_ps, 1)
                    fill(L, GLA, 6 + jj)
                pe.wait_ge(band_ready, L + 1)
                for hh in range(4):
                    if hh >= 2:
                        pe.wait_ge(pt_ready, L * NHEAD + hh - 1)
                    d = bank(M + 4 + hh % 2)
                    mm(d[:, 0:256], C("spread", 128 * (hh % 2), 128 * (hh % 2) + 128)[0:32], band[0:32, hh // 2, 0:256],
                       start=True, stop=True)
                    mm(d[0:32, 256:288], C("spread_s", 32 * (hh % 2), 32 * (hh % 2) + 32)[0:32],
                       band[0:32, hh // 2, 256:288], start=True, stop=True).then_inc(spread_ps, 1)
                fill(L, GLA, 10)
                pe.wait_ge(pt_ready, L * NHEAD + 4)
                core(L, GLA, 11)
                fill(L, GLA, 15)
                out_sums(L, GLA)
                fill(L, GLA, 16)
                states(L, GLA)
                fill(L, GLA, 17)

            def gdn(L):
                for s in range(5):
                    fill(L, GDN, s)
                pe.wait_ge(state_new, 4 * L + 2)
                pe.wait_ge(qksq_ready, L + 1)
                for b in range(4):
                    last = mm(bank(M + b)[:, 0:TOK], C("halfones"), tmp4[:, b, :], start=True, stop=True)
                last.then_inc(qksum_ps, 1)
                for s in range(5, 8):
                    fill(L, GDN, s)
                fill(L, GDN, 8)
                pe.wait_ge(qk_ready, L + 1)
                transposes(L, GDN)
                fill(L, GDN, 9)
                pe.wait_ge(vk_taken, 4 * L + GDN + 1)
                for hh in range(4):
                    r = slice(64 * (hh % 2), 64 * (hh % 2) + 64)
                    for b, (t0, nt) in enumerate(TB):
                        last = mm(bank(M + 4 + hh // 2)[r, t0:t0 + nt], ls[0:nt, b, hh:hh + 1].to_broadcast([nt, 64]),
                                  C("ident")[0:nt, 0:nt], start=True, stop=True)
                last.then_inc(beta_ps, 1)
                fill(L, GDN, 10)
                decays(L, GDN)
                pe.wait_ge(kb_ready, L + 1)
                pe.wait_ge(grow_taken, 12 * L + 4)
                for hh in range(4):
                    r = slice(64 * (hh % 2), 64 * (hh % 2) + 64)
                    pair_scores(bank(M + hh), cv[r, 2 + hh // 2, :], kb[r, hh // 2, :]).then_inc(kk_ps, 1)
                fill(L, GDN, 13)
                for lv in range(2):
                    pe.wait_ge(mask_s_ready, 2 * L + lv + 1)
                    pe.wait_ge(inv_s_ready, 3 * L + lv + 1)
                    for hh in range(4):
                        last = mm(bank(M + 4)[0:32, 32 * hh:32 * hh + 32], ms_s[0:32, hh, :], xs_s[0:32, hh, :],
                                  start=True, stop=True)
                    last.then_inc(p_s_ps, 1)
                    pe.wait_ge(p_s_ready, 2 * L + lv + 1)
                    for hh in range(4):
                        mm(bank(M + 4)[0:32, 128 + 32 * hh:160 + 32 * hh], xt_s[0:32, hh, :], pb_s[0:32, hh, :],
                           start=True, stop=True)
                        last = mm(bank(M + 4)[0:32, 256 + 32 * hh:288 + 32 * hh], pb_s[0:32, hh, :], xt_s[0:32, hh, :],
                                  start=True, stop=True)
                    last.then_inc(x_s_ps, 1)
                    fill(L, GDN, 14 + lv)
                pe.wait_ge(inv_s_ready, 3 * L + 3)
                for lv in range(7):
                    pe.wait_ge(mask_ready, 7 * L + lv + 1)
                    pe.wait_ge(mask1_ready, 7 * L + lv + 1)
                    pe.wait_ge(inv_ready, 8 * L + lv + 1)
                    for g in range(8):
                        last = mm(bank(M + g // 4)[:, 128 * (g % 4):128 * (g % 4) + 128], msk[:, g // 2, g % 2, :],
                                  xm[:, g // 2, g % 2, :], start=True, stop=True)
                    last.then_inc(p_ps, 1)
                    fill(L, GDN, 16 + 2 * lv)
                    pe.wait_ge(p_ready, 7 * L + lv + 1)
                    for g in range(8):
                        c = slice(128 * (g % 4), 128 * (g % 4) + 128)
                        mm(bank(M + 2 + g // 4)[:, c], xt[:, g // 2, g % 2, :], pb[:, g // 2, g % 2, :],
                           start=True, stop=True)
                        last = mm(bank(M + 4 + g // 4)[:, c], pb[:, g // 2, g % 2, :], xt[:, g // 2, g % 2, :],
                                  start=True, stop=True)
                    last.then_inc(x_ps, 1)
                    fill(L, GDN, 17 + 2 * lv)
                pe.wait_ge(inv_ready, 8 * L + 8)
                for hh in range(4):
                    last = mm(bank(M)[:, 128 * hh:128 * hh + 128], xt[:, hh, 0, :], vtok[:, 0, 128 * hh:128 * hh + 128],
                              start=True, stop=True)
                last.then_inc(vn0_ps, 1)
                pe.wait_ge(kbg_ready, L + 1)
                pe.wait_ge(state_in, 16 * (4 * L + GDN + 1))
                for hh in range(4):
                    r = slice(64 * (hh % 2), 64 * (hh % 2) + 64)
                    for b in range(NSEQ):
                        last = mm(bank(M + 1 + 4 * (hh % 2))[:, 32 * (hh // 2) + 4 * b:32 * (hh // 2) + 4 * b + 4], st_of(GDN)[r, hh // 2, b, :],
                                  kbg[r, hh // 2, 4 * b:4 * b + 4], start=True, stop=True)
                last.then_inc(ks_ps, 1)
                fill(L, GDN, 30)
                pe.wait_ge(vn0_ready, L + 1)
                for hh in range(4):
                    last = mm(bank(M + 2)[:, 128 * hh:128 * hh + 128], pt[:, hh, 128:256],
                              vtok[:, 0, 128 * hh:128 * hh + 128], start=True, stop=True)
                last.then_inc(r1_ps, 1)
                pe.wait_ge(ks_ready, L + 1)
                for hh in range(4):
                    last = nc.tensor.transpose(bank(M + 3)[0:32, 128 * hh:128 * hh + 128],
                                               pb.rearrange("p h b c -> p (h b c)")[:, 32 * hh:32 * hh + 32], C("ident"))
                last.then_inc(kst_ps, 1)
                fill(L, GDN, 31)
                pe.wait_ge(r1_ready, L + 1)
                for hh in range(4):
                    mm(bank(M + 4)[:, 128 * hh:128 * hh + 128], xt[:, hh, 1, :], vtok[:, 1, 128 * hh:128 * hh + 128],
                       start=True, stop=True)
                for hh in range(4):
                    last = mm(bank(M + 5)[0:32, 128 * hh:128 * hh + 128], xt_s[0:32, hh, :],
                              vtok[0:32, 2, 128 * hh:128 * hh + 128], start=True, stop=True)
                last.then_inc(vn1_ps, 1)
                fill(L, GDN, 32)
                pe.wait_ge(vn1_ready, L + 1)
                core(L, GDN, 33)
                fill(L, GDN, 37)
                out_sums(L, GDN)
                fill(L, GDN, 38)
                states(L, GDN)
                for s in range(39, NSLOT[GDN]):
                    fill(L, GDN, s)

            def ret(L):
                pe.wait_ge(state_new, 4 * L + 1)
                for b in range(4):
                    last = mm(bank(M + b)[:, 0:TOK], C("rot"), zblk(RET, b)[:, 0:TOK], start=True, stop=True)
                last.then_inc(rot_ps, 1)
                fill(L, RET, 0)
                pe.wait_ge(rope_ready, L + 1)
                transposes(L, RET)
                fill(L, RET, 1)
                pe.wait_ge(vk_taken, 4 * L + RET + 1)
                core(L, RET, 2)
                fill(L, RET, 6)
                out_sums(L, RET)
                fill(L, RET, 7)
                states(L, RET)
                for s in range(8, NSLOT[RET]):
                    fill(L, RET, s)

            def ssd(L):
                for b in range(NCONV[SSD]):
                    fill(L, SSD, b)
                pe.wait_ge(conv_ready, 14 * L + 14)
                pe.wait_ge(state_new, 4 * L + 3)
                transposes(L, SSD)
                for s in range(6, 9):
                    fill(L, SSD, s)
                decays(L, SSD)
                core(L, SSD, 13)
                fill(L, SSD, 21)
                out_sums(L, SSD)
                fill(L, SSD, 22)
                states(L, SSD)

            def dense(L):
                norm(3 * L + 1)
                for f in range(NF):
                    for kind in ("gate", "up"):
                        if f - 1 > 0:
                            pe.wait_ge(hid_ready, f - 1)
                        x = (kind, L, 0, f)
                        w = weights(x)
                        for k in range(KD):
                            if f == 0 and kind == "gate":
                                pe.wait_ge(u_ready, KD * (3 * L + 1) + k + 1)
                            last = mm(bank(M + 2 * (f % 2) + (kind == "up"))[:, 0:TOK], w[k], u[:, k, :],
                                      start=k == 0, stop=k == KD - 1)
                        last.then_inc(tile_done, 1)
                pe.wait_ge(hid_ready, NF)
                for f in range(NF):
                    w = weights(("down", L, 0, f))
                    for k in range(KD):
                        last = mm(bank(k)[:, 0:TOK], w[k], hid[:, f, :], start=f == 0, stop=f == NF - 1)
                    last.then_inc(tile_done, 1)

            def experts(L):
                norm(3 * L + 1)
                pe.wait_ge(router_in, 16)
                pe.wait_ge(u_ready, KD * (3 * L + 2))
                for b, (t0, nt) in enumerate(TB):
                    for k in range(KD):
                        last = mm(bank(M)[0:nt, 8 * b:8 * b + 8], u[:, k, t0:t0 + nt], router[:, k, :],
                                  start=k == 0, stop=k == KD - 1)
                        if b == 0 and k == 0:
                            last.then_inc(expert_slots, RING)
                last.then_inc(logit_ps, 1)
                for b, (t0, nt) in enumerate(TB):
                    for k in range(KD):
                        last = nc.tensor.transpose(bank((M + 1 + 2 * b + k // 4) % 8)[0:nt, P * (k % 4):P * (k % 4) + P],
                                                   u[:, k, t0:t0 + nt], C("ident"))
                last.then_inc(utok_ps, 1)
                pe.wait_ge(sel_ready, 1)
                pe.wait_ge(xg_ready, 1)
                d, before, on = bank(M), C("strict", 0, 128), C("ones")
                mm(d[:, 0:8], before, sel[:, 0, :], start=True, stop=True)
                mm(d[:, 8:16], on, sel[:, 0, :], start=True, stop=False)
                mm(d[:, 8:16], before, sel[:, 1, :], start=False, stop=True)
                for c, nr in ((16, 32), (24, 128)):
                    mm(d[0:nr, c:c + 8], on[:, 0:nr], sel[:, 0, :], start=True, stop=False)
                    mm(d[0:nr, c:c + 8], on[:, 0:nr], sel[:, 1, :], start=False, stop=False)
                    last = mm(d[0:nr, c:c + 8], (before if c == 16 else on)[0:32, 0:nr], sel[0:32, 2, :], start=False, stop=True)
                last.then_inc(pos_ps, 1)
                pe.wait_ge(pos_ready, 1)
                for e in range(NE):
                    if e - 1 > 0:
                        pe.wait_ge(rows_taken, e - 1)
                    for g, src in enumerate((posm, wts)):
                        for b, (t0, nt) in enumerate(TB):
                            last = mm(bank(M + 2 * (e % 2) + g)[:, t0:t0 + nt], src[0:nt, b, e:e + 1].to_broadcast([nt, P]),
                                      C("ident")[0:nt, 0:nt], start=True, stop=True)
                    last.then_inc(rows_ps, 1)
                pe.wait_ge(rows_taken, NE)
                pe.wait_ge(rounds_ready, 1)
                rounds = pe.value_load(nrt[0:1, 0:1], min_val=1, max_val=3)
                with pe.Fori(0, rounds) as r:
                    with pe.Fori(0, NE) as e:
                        it = pe.snap(r * NE + e)

                        def expert_tile(k):
                            pe.wait_ge(expert_slot_in[k % RING], it * (16 * E_TILES // RING) + 16 * (k // RING + 1))
                            o = (k % RING) * TILE
                            return [ring[:, o + P * i:o + P * i + P] for i in range(8)]

                        pe.wait_ge(gather_ready, it + 1)
                        pe.wait_ge(expert_added, it * 3 + 1)
                        for k in range(KD):
                            for b, (t0, nt) in enumerate(TB):
                                last = mm(bank(k // 4)[:, PLACES * (k % 4):PLACES * (k % 4 + 1)], utok[0:nt, b, P * k:P * k + P],
                                          gath[0:nt, b, :], start=b == 0, stop=b == 2)
                            if k % 4 == 3:
                                last.then_inc(gather_ps, 1)
                        pe.wait_ge(expert_added, it * 3 + 2)
                        for f in range(NF):
                            if f >= 2:
                                pe.wait_ge(ehid_ready, it * NF + (f - 1))
                            for g in range(2):
                                w = expert_tile(2 * f + g)
                                for k in range(KD):
                                    if f == 0 and g == 0 and k % 4 == 0:
                                        pe.wait_ge(xg_ready, it * 2 + (k // 4 + 2))
                                    last = mm(bank(M + 2 * (f % 2) + g)[:, 0:PLACES], w[k], xg[:, k, :], start=k == 0, stop=k == KD - 1)
                                last.then_inc(expert_slots, 1)
                        for f in range(NF):
                            pe.wait_ge(ehid_low_ready, it * NF + (f + 1))
                            pe.wait_ge(w_low_ready, it * NF + (f + 1))
                            if f == 0:
                                pe.wait_ge(expert_added, it * 3 + 3)
                            for g in range(2):
                                out, half = bank(M + 4 + g)[0:PLACES, :], slice(512 * g, 512 * g + 512)
                                mm(out, e_high[:, f, :], w_high[:, f % HIGHS, half], start=f == 0, stop=False)
                                mm(out, e_high[:, f, :], w_low[:, f % LOWS, half], start=False, stop=False)
                                last = mm(out, e_low[:, f, :], w_high[:, f % HIGHS, half], start=False, stop=f == NF - 1)
                                if f == NF - 1 and g == 0:
                                    last.then_inc(y_ps, 1)
                            last.then_inc(expert_slots, 1)
                        pe.wait_ge(scatter_ready, it + 1)
                        pe.wait_ge(y_taken, it * 2 + 1)
                        for g, (b0, k0, nk) in enumerate(((0, 0, 2), (M, 2, 4), (M + 4, 6, 2))):
                            for k in range(k0, k0 + nk):
                                if k == 4:
                                    pe.wait_ge(y_taken, it * 2 + 2)
                                last = mm(bank(b0 + k - k0)[:, 0:TOK], yt[0:PLACES, P * k:P * k + P], scat[0:PLACES, :], start=True, stop=True)
                            last.then_inc(scatter_ps, 1)
                pe.wait_ge(square_ready, KD * (3 * L + 2) + 1)
                mm(bank(0)[0:32, 0:32], C("ident", 0, 32), C("ident", 0, 32), start=True, stop=True).then_inc(experts_done, 1)

            def ple(L):
                norm(3 * L + 2)
                pe.wait_ge(ple_loaded, 16 * (L + 1))
                for b in range(2):
                    stream_tile(("pproj", L, 0, b))
                for b in range(KD):
                    stream_tile(("pgate", L, 0, b))
                pe.wait_ge(stream_ple, taken_before(T_OF[("pgate", L, 0, 7)] + 1, "ple"))

            pe.wait_ge(norm_const_in, 16)
            for L in range(DEPTH):
                norm(3 * L)
                for b in range(4):
                    stream_tile(("z", L, 0, b))
                if L == 0:
                    pe.wait_ge(const_in, 16)
                prep(L)
                pe.wait_ge(cum_taken_dve, L + 1)
                pe.wait_ge(cum_taken_act, L + 1)
                pe.wait_ge(stream_act, taken_before(T_OF[("z", L, 0, 11)] + 1, "act"))
                transposes(L, GLA)
                gla(L)
                pe.wait_ge(o_final, 4 * L + 1)
                pe.wait_ge(stream_act, taken_before(T_OF[("z", L, 1, 11)] + 1, "act"))
                ret(L)
                gdn(L)
                ssd(L)
                pe.wait_ge(o_final, 4 * L + 4)
                for b in range(4):
                    stream_tile(("br", L, 3, b))
                pe.wait_ge(acc_ready, L + 1)
                pe.wait_ge(state_new, 4 * L + 4)
                for b in range(KD):
                    stream_tile(("out", L, 0, b))
                dense(L) if L % 2 == 0 else experts(L)
                ple(L)
            norm(3 * DEPTH)

        @block.scalar
        def _(act):
            steps = Steps()
            A = nc.scalar.activation

            def fill(L, n, s):
                for x in FILL[L][n][s]:
                    take(x)

            def take(x):
                kind, L, n, b = x
                if TAKER[kind] != "act":
                    return
                t = T_OF[x]
                act.wait_ge(tile_done, t + 1)
                src = bank(t % 2)
                if kind == "mg":
                    if n > 0:
                        act.wait_ge(stream_dve, taken_before(T_OF[("br", L, n - 1, 3)] + 1, "dve"))
                    elif L > 0:
                        act.wait_ge(stream_dve, taken_before(T_OF[("br", L - 1, 3, 3)] + 1, "dve"))
                    A(mg[:, b, :], src[:, 0:TOK], ACT.Tanh, scale=0.5).then_inc(stream_act, 1)
                elif kind == "pproj":
                    A(ple_pj[:, 4 * b:4 * b + 4, :], ps_t[:, M:M + 4, 0:TOK], ACT.Copy).then_inc(stream_act, 1)
                elif b < NCONV[n]:
                    A(zblk(n, b)[:, 3:259], src[:, 0:SEQ], ACT.Copy)
                    A(zblk(n, b)[:, 259:315].rearrange("p (s w) -> p s w", w=7)[:, :, 3:7],
                      src[:, SEQ:TOK].rearrange("p (s w) -> p s w", w=4), ACT.Copy).then_inc(stream_act, 1)
                else:
                    A(zblk(n, b)[:, 0:TOK], src[:, 0:TOK], ACT.Copy, scale=ZSCALE[n][b]).then_inc(stream_act, 1)

            def norm(k):
                act.wait_ge(sumsq_ps, k + 1)
                A(rs4[:, 0, :], sumsq_bank(k), ACT.Sqrt, scale=1.0 / D_MODEL, bias=C("eps")).then_inc(rt_ready, 1)

            def prep(L):
                gab = tmp4.rearrange("p k t -> p (k t)")[:, 0:768].rearrange("p (b c) -> p b c", b=3)
                act.wait_ge(abs_small, L + 1)
                act.wait_ge(small_in[L], 16 * 4)
                for r, bs in pads(0):
                    A(ab[0:r, bs, 4:16], ab[0:r, bs, 4:16], ACT.Exp, scale=-1.0)
                    A(ab[0:r, bs, 0:4], xs[0:r, bs, 0:4], ACT.Tanh, scale=0.5)
                act.wait_ge(abs_gate, L + 1)
                for r, bs in pads(0):
                    A(gab[0:r, bs, :], gab[0:r, bs, :], ACT.Exp, scale=-1.0)
                A(ea, rows[:, 16:32], ACT.Exp).then_inc(act_step, 1)
                act.wait_ge(act_step, steps.next())
                for r, bs in pads(0):
                    A(ab[0:r, bs, 4:16], ab[0:r, bs, 4:16], ACT.Ln, bias=1.0)
                    last = A(gab[0:r, bs, :], gab[0:r, bs, :], ACT.Ln, bias=1.0)
                last.then_inc(logs_ready, 1)
                for b in range(4, ZBLOCKS[0]):
                    take(("z", L, 0, b))
                act.wait_ge(cum_ps, L + 1)
                for r, bs in pads(0):
                    b0, b1 = bs.start, bs.stop
                    A(kdec[0:r, bs, 0:256], bank(M + 1 + b0 // 2)[0:r, 0:256 * (b1 - b0)].rearrange("p (b c) -> p b c", c=256),
                      ACT.Exp)
                act.wait_ge(cum_taken_dve, L + 1)
                for r, bs in pads(0):
                    b0, b1 = bs.start, bs.stop
                    A(kde[0:r, bs, 4:16], bank(M)[0:r, 48 + 16 * b0:48 + 16 * b1].rearrange("p (b c) -> p b c", c=16)[:, :, 4:16],
                      ACT.Exp)
                A(egp[:, 0:2, :], gt[:, :, 256:288], ACT.Exp).then_inc(cum_taken_act, 1)

            def core(L, n, slot):
                for hh in range(HEADS[n]):
                    gh = L * NHEAD + HBASE[n] + hh

                    def take_o(q):
                        g = L * NHEAD + HBASE[n] + q
                        act.wait_ge(o_ps, g + 1)
                        r = slice(64 * (q % 2), 64 * (q % 2) + 64) if n == SSD else slice(0, P)
                        src = bank(M + 4 + (q // 2 if n == SSD else q) % 2)[r, 0:TOK]
                        if n in (GDN, SSD) and q == 0:
                            act.wait_ge(rows_saved, 2 * L + (1 if n == GDN else 2))
                        A(ob(n, q), src, ACT.Copy).then_inc(o_taken, 1)

                    if n == GLA:
                        take_o(hh)
                    elif hh >= 1:
                        take_o(hh - 1)
                    fill(L, n, slot + hh)
                if n != GLA:
                    take_o(HEADS[n] - 1)

            def gate(L, n):
                if 4 * L + n > 0:
                    act.wait_ge(o_final, 4 * L + n)
                A(gate_of(n), zset[n % 2][:, GATE0[n]:GATE0[n] + 4, 0:TOK], ACT.Tanh).then_inc(gate_tanh, 1)

            def out_norm(L, n, slot):
                m = 4 * L + n
                if n == SSD:
                    act.wait_ge(y_ready, L + 1)
                else:
                    act.wait_ge(o_taken, L * NHEAD + HBASE[n] + HEADS[n])
                A(tmp4, zset[n % 2][:, OUT0[n]:OUT0[n] + 4, 0:TOK], ACT.Square).then_inc(osq_ready, 1)
                fill(L, n, slot)
                act.wait_ge(osum_ps, m + 1)
                if n == SSD:
                    A(rs4[:, 0:2, :], ps_t[:, M:M + 2, 0:TOK], ACT.Sqrt, scale=1.0 / 256,
                      bias=C("eps")).then_inc(ort_ready, 1)
                else:
                    A(rs4, ps_t[:, M:M + 4, 0:TOK], ACT.Sqrt, scale=1.0 / 128, bias=C("eps")).then_inc(ort_ready, 1)
                for s in range(slot + 1, NSLOT[n]):
                    fill(L, n, s)

            def decays(L, n):
                for hh in range(HEADS[n]):
                    k = L * 12 + (hh if n == GDN else 4 + hh)
                    act.wait_ge(grow_taken, k + 1)
                    A(dmat[:, hh, 0:384], dmat[:, hh, 0:384], ACT.Exp)
                    A(dmat[0:32, hh, 384:416], dmat[0:32, hh, 384:416], ACT.Exp).then_inc(decay_ready, 1)
                    if hh % 2:
                        fill(L, n, (11 if n == GDN else 9) + hh // 2)
                q = HEADS[n] // 2
                A(egp[:, 0:q, :], egp[:, 0:q, :], ACT.Exp).then_inc(eg_ready, 1)

            def conv(L, n):
                for b in range(NCONV[n]):
                    c = 14 * L + CONV0[n] + b
                    fill(L, n, b)
                    act.wait_ge(convsum_ready, c + 1)
                    if c - 1 > 0:
                        act.wait_ge(conv_ready, c - 1)
                    A(ctan[:, b % 2, 0:312], cbuf[:, b % 2, 0:312], ACT.Tanh).then_inc(ctan_ready, 1)
                    if n == GDN and b == 4:
                        act.wait_ge(conv_ready, 14 * L + 4)
                        A(tmp4, cv[:, 0:4, :], ACT.Square).then_inc(qksq_ready, 1)
                    if n == GDN and b == 6:
                        act.wait_ge(qksum_ps, L + 1)
                        A(rs4, ps_t[:, M:M + 4, 0:TOK], ACT.Sqrt, bias=C("eps")).then_inc(qkrt_ready, 1)

            def gla(L):
                def level(lv):
                    act.wait_ge(ldiff_ready, 6 * L + lv + 1)
                    lo, up = halves_of(lev[:, lv % 2], LEVELS[lv])
                    A(lo, lo, ACT.Exp, scale=-1.0)
                    A(up, up, ACT.Exp).then_inc(lexp_ready, 1)

                level(0)
                for lv in range(6):
                    fill(L, GLA, lv)
                    if lv < 5:
                        level(lv + 1)
                for jj in range(BAND):
                    act.wait_ge(diff_ready, BAND * L + jj + 1)
                    d = runs(dd[:, jj % 2], jj)
                    A(d, d, ACT.Exp).then_inc(ediff_ready, 1)
                for jj in range(BAND):
                    fill(L, GLA, 6 + jj)
                fill(L, GLA, 10)
                core(L, GLA, 11)
                gate(L, GLA)
                out_norm(L, GLA, 15)

            def ret(L):
                fill(L, RET, 0)
                fill(L, RET, 1)
                core(L, RET, 2)
                gate(L, RET)
                out_norm(L, RET, 6)

            def gdn(L):
                conv(L, GDN)
                fill(L, GDN, 8)
                fill(L, GDN, 9)
                fill(L, GDN, 10)
                decays(L, GDN)
                fill(L, GDN, 13)
                for lv in range(2):
                    act.wait_ge(p_s_ps, 2 * L + lv + 1)
                    A(pb_s[0:32], bank(M + 4)[0:32, 0:128].rearrange("p (h c) -> p h c", h=4),
                      ACT.Copy).then_inc(p_s_ready, 1)
                    fill(L, GDN, 14 + lv)
                for lv in range(7):
                    act.wait_ge(p_ps, 7 * L + lv + 1)
                    A(pb.rearrange("p h b c -> p (h b c)").rearrange("p (k c) -> p k c", k=2), ps_t[:, M:M + 2, :],
                      ACT.Copy).then_inc(p_ready, 1)
                    fill(L, GDN, 16 + 2 * lv)
                    fill(L, GDN, 17 + 2 * lv)
                for s in (30, 31, 32):
                    fill(L, GDN, s)
                core(L, GDN, 33)
                gate(L, GDN)
                out_norm(L, GDN, 37)

            def ssd(L):
                conv(L, SSD)
                for s in range(6, 9):
                    fill(L, SSD, s)
                decays(L, SSD)
                core(L, SSD, 13)
                gate(L, SSD)
                out_norm(L, SSD, 21)

            def dense(L):
                for f in range(NF):
                    act.wait_ge(tile_done, T_OF[("gate", L, 0, f)] + 1)
                    if f - 1 > 0:
                        act.wait_ge(hid_ready, f - 1)
                    A(tanh_t[:, f % 2, :], bank(M + 2 * (f % 2))[:, 0:TOK], ACT.Tanh, scale=0.5).then_inc(tanh_ready, 1)

            def experts(L):
                act.wait_ge(state_out, 16 * 4 * (L + 1))
                act.wait_ge(stp_out, 16 * 4 * (L + 1))
                act.wait_ge(conv_out, 16 * (L + 1))
                act.wait_ge(utok_ps, 1)
                A(utok[:, 0:2, :].rearrange("p b (g c) -> p (b g) c", g=2), ps_t[:, M + 1:M + 5, :], ACT.Copy)
                A(utok[0:32, 2, 0:512], bank(M + 5)[0:32, :], ACT.Copy)
                A(utok[0:32, 2, 512:1024], bank(0)[0:32, :], ACT.Copy).then_inc(xg_ready, 1)
                act.wait_ge(sel_ready, 2)
                for r, bs in pads(0):
                    last = A(wts[0:r, bs, :], wts[0:r, bs, :], ACT.Exp)
                last.then_inc(expw_ready, 1)
                act.wait_ge(rounds_ready, 1)
                rounds = act.value_load(nrt[0:1, 0:1], min_val=1, max_val=3)
                with act.Fori(0, rounds) as r:
                    with act.Fori(0, NE) as e:
                        it = act.snap(r * NE + e)

                        def high(f):
                            t = 2 * NF + f
                            act.wait_ge(expert_slot_in[t % RING], it * (16 * E_TILES // RING) + 16 * (t // RING + 1))
                            if f >= HIGHS:
                                act.wait_ge(expert_slots, it * E_TILES + (RING + t - HIGHS + 1))
                            o = (t % RING) * TILE
                            A(w_high[:, f % HIGHS, :], ring[:, o:o + TILE], ACT.Copy).then_inc(w_high_ready, 1)

                        act.wait_ge(gather_ps, it * 2 + 1)
                        A(xg[:, 0:4, :].rearrange("p k c -> p (k c)"), bank(0)[:, 0:4 * PLACES], ACT.Copy).then_inc(xg_ready, 1)
                        act.wait_ge(gather_ps, it * 2 + 2)
                        A(xg[:, 4:8, :].rearrange("p k c -> p (k c)"), bank(1)[:, 0:4 * PLACES], ACT.Copy).then_inc(xg_ready, 1)
                        for f in range(NF):
                            act.wait_ge(expert_slots, it * E_TILES + (RING + 2 * f + 1))
                            if f >= 2:
                                act.wait_ge(ehid_ready, it * NF + (f - 1))
                            A(etanh[:, f % 2, :], bank(M + 2 * (f % 2))[:, 0:PLACES], ACT.Tanh, scale=0.5).then_inc(etanh_ready, 1)
                            if f == NF - 2:
                                high(0)
                        for f in range(1, NF):
                            high(f)
                        act.wait_ge(y_ps, it + 1)
                        A(yt[0:PLACES, 0:512], bank(M + 4)[0:PLACES, :], ACT.Copy).then_inc(y_taken, 1)
                        act.wait_ge(expert_slots, it * E_TILES + (RING + E_TILES))
                        A(yt[0:PLACES, 512:1024], bank(M + 5)[0:PLACES, :], ACT.Copy).then_inc(y_taken, 1)

            act.wait_ge(norm_const_in, 16)
            for L in range(DEPTH):
                norm(3 * L)
                for b in range(4):
                    take(("z", L, 0, b))
                if L == 0:
                    act.wait_ge(const_in, 16)
                prep(L)
                gla(L)
                ret(L)
                gdn(L)
                ssd(L)
                norm(3 * L + 1)
                dense(L) if L % 2 == 0 else experts(L)
                norm(3 * L + 2)
                for b in range(2):
                    take(("pproj", L, 0, b))
                for b in range(KD):
                    t = T_OF[("pgate", L, 0, b)]
                    act.wait_ge(tile_done, t + 1)
                    if KD * L + b - 1 > 0:
                        act.wait_ge(gate_used, KD * L + b - 1)
                    A(tanh_t[:, b % 2, :], bank(t % 2)[:, 0:TOK], ACT.Tanh, scale=0.5).then_inc(stream_ple, 1)
            norm(3 * DEPTH)

        @block.vector
        def _(dve):
            steps = Steps()
            V = nc.vector
            tt, ts, stt, cp = V.tensor_tensor, V.tensor_scalar, V.scalar_tensor_tensor, V.tensor_copy

            def fill(L, n, s):
                for x in FILL[L][n][s]:
                    if x[0] == "br":
                        branch_tile(x)

            def branch_tile(x):
                _, L, n, b = x
                t = T_OF[x]
                dve.wait_ge(stream_act, taken_before(T_OF[("mg", L, n, 7)] + 1, "act"))
                dst = acc[:, 2 * b:2 * b + 2, :] if n == 0 else brt
                for o in range(2):
                    if o == 0:
                        dve.wait_ge(branch_ps, 16 * L + 4 * n + b + 1)
                    else:
                        dve.wait_ge(tile_done, t + 1)
                    stt(dst[:, o, :], mg[:, 2 * b + o, :], 1.0, bank(o)[:, 0:TOK], ALU.add, ALU.mult).then_inc(stream_dve, 1)
                if n > 0:
                    dve.wait_ge(stream_dve, taken_before(t + 1, "dve"))
                    tt(acc[:, 2 * b:2 * b + 2, :], acc[:, 2 * b:2 * b + 2, :], brt, ALU.add).then_inc(dve_step, 1)
                    dve.wait_ge(dve_step, steps.next())

            def square(k, b):
                tt(squares(k)[:, b, :], h[:, b, :], h[:, b, :], ALU.mult).then_inc(square_ready, 1)

            def norm(k, gain):
                dve.wait_ge(rt_ready, k + 1)
                V.reciprocal(rs4[:, 1, :], rs4[:, 0, :]).then_inc(dve_step, 1)
                dve.wait_ge(dve_step, steps.next())
                for b in range(KD):
                    stt(u[:, b, :], h[:, b, :], PVc(gain, b), rs4[:, 1, :], ALU.mult, ALU.mult).then_inc(u_ready, 1)

            def prep(L):
                gab = tmp4.rearrange("p k t -> p (k t)")[:, 0:768].rearrange("p (b c) -> p b c", b=3)
                dve.wait_ge(small_ps, L + 1)
                dve.wait_ge(small_in[L], 16 * 4)
                taps = pv[:, PV["conv_w"][0]:PV["conv_w"][0] + 70]
                ts(taps, taps, 0.5, None, ALU.mult).then_inc(dve_step, 1)
                dve.wait_ge(dve_step, steps.next())
                V.memset(glrt[0:32, :], 1.0).then_inc(dve_step, 1)
                dve.wait_ge(dve_step, steps.next())
                cp(glrt[0:16, :], bank(M)[0:16, 0:TOK])
                for r, bs in pads(0):
                    b0, b1 = bs.start, bs.stop
                    last = tt(xs[0:r, bs, :], bank(M + 1)[0:r, 16 * b0:16 * b1].rearrange("p (b c) -> p b c", c=16),
                              rows[0:r, 0:16].unsqueeze(1).to_broadcast([r, b1 - b0, 16]), ALU.add)
                last.then_inc(glr_ready, 1)
                dve.wait_ge(glr_ready, L + 1)
                for r, bs in pads(0):
                    last = stt(ab[0:r, bs, :], xs[0:r, bs, :], -1.0, xs[0:r, bs, :], ALU.mult, ALU.max)
                last.then_inc(abs_small, 1)
                dve.wait_ge(gk_ps, L + 1)
                for r, bs in pads(0):
                    b0, b1 = bs.start, bs.stop
                    last = cp(gx[0:r, bs, :], bank(M + 2 + b0 // 2)[0:r, 0:256 * (b1 - b0)].rearrange("p (b c) -> p b c", c=256))
                last.then_inc(dve_step, 1)
                dve.wait_ge(dve_step, steps.next())
                for r, bs in pads(0):
                    last = stt(gab[0:r, bs, :], gx[0:r, bs, :], -1.0, gx[0:r, bs, :], ALU.mult, ALU.max)
                last.then_inc(abs_gate, 1)
                dve.wait_ge(logs_ready, L + 1)
                for r, bs in pads(0):
                    nb = bs.stop - bs.start
                    stt(xs[0:r, bs, 4:16], xs[0:r, bs, 4:16], 0.0, ab[0:r, bs, 4:16], ALU.max, ALU.add)
                    ts(ls[0:r, bs, 0:4], ab[0:r, bs, 0:4], 0.5, 0.5, ALU.mult, ALU.add)
                    last = stt(gx[0:r, bs, :], gx[0:r, bs, :], 0.0, gab[0:r, bs, :], ALU.min, ALU.subtract)
                last.then_inc(dve_step, 1)
                dve.wait_ge(dve_step, steps.next())
                for r, bs in pads(0):
                    nb = bs.stop - bs.start
                    stt(ls[0:r, bs, 4:16], xs[0:r, bs, 4:16], -1.0,
                        ea[0:r, 4:16].unsqueeze(1).to_broadcast([r, nb, 12]), ALU.mult, ALU.mult)
                    last = ts(gx[0:r, bs, :], gx[0:r, bs, :], 1.0 / 16, None, ALU.mult)
                last.then_inc(logd_ready, 1)
                dve.wait_ge(cum_ps, L + 1)
                for r, bs in pads(0):
                    b0, b1 = bs.start, bs.stop
                    cp(gcol[0:r, bs, :], bank(M)[0:r, 16 * b0:16 * b1].rearrange("p (b c) -> p b c", c=16))
                cp(gt, ps_t[:, M + 3:M + 5, 0:TOK]).then_inc(cum_taken_dve, 1)
                dve.wait_ge(cum_taken_dve, L + 1)
                dve.wait_ge(cum_taken_act, L + 1)

            def take_vk(L, n):
                dve.wait_ge(vk_ps, 4 * L + n + 1)
                for r, bs in pads(0):
                    b0, b1 = bs.start, bs.stop
                    nb = b1 - b0
                    src = ps_t[0:r, M + b0:M + b1, :]
                    ks = bank(M + 3 + b0 // 2)[0:r, 0:256 * nb].rearrange("p (b c) -> p b c", c=256)
                    if n in (GLA, RET):
                        cp(vtok[0:r, bs, :], src)
                    else:
                        nh = HEADS[n]
                        f = ls[0:r, bs, 0:4] if n == GDN else xs[0:r, bs, 8:16]
                        tt(vtok[0:r, bs, :].rearrange("p b (h v) -> p b h v", h=nh), src.rearrange("p b (h v) -> p b h v", h=nh),
                           f.unsqueeze(3).to_broadcast([r, nb, nh, DV[n]]), ALU.mult)
                    if n == GLA:
                        last = tt(kdec[0:r, bs, 0:256], kdec[0:r, bs, 0:256], ks, ALU.mult)
                    elif n in (RET, GDN):
                        f = (C("ret_kd").rearrange("p (b c) -> p b c", b=3)[0:r, bs, 0:4] if n == RET else kde[0:r, bs, 4:8])
                        last = tt(kdec[0:r, bs, 0:256].rearrange("p b (h v) -> p b h v", h=4),
                                  ks.rearrange("p b (h v) -> p b h v", h=4), f.unsqueeze(3).to_broadcast([r, nb, 4, 64]), ALU.mult)
                    else:
                        for g in range(2):
                            for b in range(b0, b1):
                                last = tt(kdec[0:r, b, 256 * g:256 * g + 256].rearrange("p (h v) -> p h v", h=4),
                                          ks[:, b - b0, 64 * g:64 * g + 64].unsqueeze(1).to_broadcast([r, 4, 64]),
                                          kde[0:r, b, 8 + 4 * g:12 + 4 * g].unsqueeze(2).to_broadcast([r, 4, 64]), ALU.mult)
                last.then_inc(vk_taken, 1)
                dve.wait_ge(vk_taken, 4 * L + n + 1)

            def scores(L, n, slot):
                for hh in range(HEADS[n]):
                    gh = L * NHEAD + HBASE[n] + hh
                    dve.wait_ge(scores_ps, L * 10 + HBASE[n] - 4 + (hh // 4 if n == SSD else hh) + 1)
                    if hh >= 4:
                        dve.wait_ge(o_ps, gh - 3)
                    d = C("ret_decay", PAIR * hh, PAIR * hh + PAIR) if n == RET else dmat[:, hh, :]
                    if n != RET:
                        dve.wait_ge(decay_ready, L * 12 + (0 if n == GDN else 4) + HEADS[n])
                    s = bank(M + (hh // 4 if n == SSD else hh % 2))
                    tt(pt[:, hh % 4, 0:384], s[:, 0:384], d[:, 0:384], ALU.mult)
                    tt(pt[0:32, hh % 4, 384:416], s[0:32, 384:416], d[0:32, 384:416], ALU.mult).then_inc(pt_ready, 1)
                    fill(L, n, slot + hh)

            def state(L, n):
                m = 4 * L + n
                dve.wait_ge(masked_used, L * NHEAD + HBASE[n] + HEADS[n])
                if m > 0:
                    dve.wait_ge(stp_out, 16 * m)
                dve.wait_ge(state_decayed, m + 1)
                cp(stp, bank(M + 4)[:, 0:256])
                tt(st.rearrange("p (k c) -> p k c", k=4), st.rearrange("p (k c) -> p k c", k=4), ps_t[:, M:M + 4, :],
                   ALU.add).then_inc(state_new, 1)

            def out_norm(L, n, slot):
                m = 4 * L + n
                gates, o4 = zset[n % 2][:, GATE0[n]:GATE0[n] + 4, 0:TOK], zset[n % 2][:, OUT0[n]:OUT0[n] + 4, 0:TOK]
                g4 = gate_of(n)
                dve.wait_ge(gate_tanh, m + 1)
                dve.wait_ge(o_taken, L * NHEAD + HBASE[n] + HEADS[n])
                if n == SSD:
                    for b in range(4):
                        stt(o4[:, b, :], cv[:, b, :], PVc("ssd_d", b), o4[:, b, :], ALU.mult, ALU.add)
                stt(g4, g4, 1.0, gates, ALU.add, ALU.mult).then_inc(dve_step, 1)
                dve.wait_ge(dve_step, steps.next())
                if n == SSD:
                    tt(o4, o4, g4, ALU.mult).then_inc(y_ready, 1)
                else:
                    stt(g4, o4, PVc(("gla_norm", "ret_norm", "gdn_norm")[n]), g4, ALU.mult, ALU.mult)
                fill(L, n, slot)
                dve.wait_ge(ort_ready, m + 1)
                w = 2 if n == SSD else 4
                V.reciprocal(rs4[:, 0:w, :], rs4[:, 0:w, :]).then_inc(dve_step, 1)
                dve.wait_ge(dve_step, steps.next())
                if n == SSD:
                    for b in range(4):
                        last = stt(o4[:, b, :], o4[:, b, :], PVc("ssd_norm", b), rs4[:, b // 2, :], ALU.mult, ALU.mult)
                else:
                    last = tt(o4, g4, rs4, ALU.mult)
                last.then_inc(o_final, 1)
                dve.wait_ge(o_final, m + 1)
                fill(L, n, slot + 1)
                state(L, n)
                for s in range(slot + 2, NSLOT[n]):
                    fill(L, n, s)

            def decays(L, n):
                for hh in range(HEADS[n]):
                    k = L * 12 + (hh if n == GDN else 4 + hh)
                    c = SSD_COL[n] + hh
                    half, pair = half_pair(n, hh)
                    dve.wait_ge(grow_ps, k + 1)
                    g = bank(M + 2 + hh % 2)
                    for b, (r, i0, i1, c0) in enumerate(SEGS):
                        stt(dmat[0:r, hh, c0:c0 + i1 - i0], g[0:r, i0:i1], gcol[0:r, b, c:c + 1],
                            C("future")[0:r, c0:c0 + i1 - i0], ALU.subtract, ALU.add)
                    cp(egp[64 * half:64 * half + 64, pair, :], g[64 * half:64 * half + 64, 256:288]).then_inc(grow_taken, 1)
                    if hh % 2:
                        fill(L, n, (11 if n == GDN else 9) + hh // 2)
                dve.wait_ge(eg_ready, 2 * L + (1 if n == GDN else 2))

            def conv(L, n):
                nb = NCONV[n]
                wv = pv[:, PV["conv_w"][0]:PV["conv_w"][0] + 56].rearrange("p (k b) -> p k b", b=14)

                def finish(b):
                    dve.wait_ge(ctan_ready, 14 * L + CONV0[n] + b + 1)
                    c, t = cbuf[:, b % 2, :], ctan[:, b % 2, :]
                    stt(cv[:, b, 0:256], t[:, 0:256], 1.0, c[:, 0:256], ALU.add, ALU.mult)
                    s7 = [q[:, 259:315].rearrange("p (s w) -> p s w", w=7)[:, :, 0:4] for q in (t, c)]
                    stt(cv[:, b, 256:288].rearrange("p (s w) -> p s w", w=4), s7[0], 1.0, s7[1],
                        ALU.add, ALU.mult).then_inc(conv_ready, 1)
                    dve.wait_ge(conv_ready, 14 * L + CONV0[n] + b + 1)

                for b in range(nb):
                    ci = CONV0[n] + b
                    dve.wait_ge(stream_act, taken_before(T_OF[("z", L, n, b)] + 1, "act"))
                    dve.wait_ge(pads_ready, 2 * L + (1 if n == GDN else 2))
                    src = zblk(n, b)
                    out = cbuf[:, b % 2, 0:312]
                    ts(out, src[:, 0:312], wv[:, 0, ci:ci + 1], PVc("conv_b", ci), ALU.mult, ALU.add).then_inc(dve_step, 1)
                    dve.wait_ge(dve_step, steps.next())
                    stt(out, src[:, 1:313], wv[:, 1, ci:ci + 1], out, ALU.mult, ALU.add).then_inc(dve_step, 1)
                    dve.wait_ge(dve_step, steps.next())
                    stt(out, src[:, 2:314], wv[:, 2, ci:ci + 1], out, ALU.mult, ALU.add).then_inc(dve_step, 1)
                    dve.wait_ge(dve_step, steps.next())
                    stt(out, src[:, 3:315], wv[:, 3, ci:ci + 1], out, ALU.mult, ALU.add).then_inc(convsum_ready, 1)
                    if b >= 1:
                        finish(b - 1)
                        fill(L, n, b - 1)
                finish(nb - 1)
                fill(L, n, nb - 1)

            def gla(L):
                zq, zk = zset[0][:, 0:2, 0:TOK], zset[0][:, 2:4, 0:TOK]
                for lv, w in enumerate(LEVELS):
                    if lv == 1:
                        take_vk(L, GLA)
                        V.memset(ps_t[:, M:M + 4, 0:PAIR], 0.0).then_inc(cross_zero, 1)
                        tt(qg[:, 0:2, :], zq[:, :, 256:288], egp[:, 0:2, :], ALU.mult).then_inc(qg_ready, 1)
                        V.memset(dd, 0.0)
                    if lv >= 2:
                        dve.wait_ge(lev_ps, 6 * L + lv - 1)
                    n = SEQ // (2 * w)
                    for q in range(2):
                        g = gt[:, q, 0:SEQ].rearrange("p (s w) -> p s w", w=2 * w)
                        last = tt(lev[:, lv % 2, q, :].rearrange("p (s w) -> p s w", w=2 * w), g,
                                  g[:, :, w - 1:w].to_broadcast([P, n, 2 * w]), ALU.subtract)
                    last.then_inc(ldiff_ready, 1)
                    fill(L, GLA, lv)

                def sub(jj):
                    if jj >= 2:
                        dve.wait_ge(sub_ps, BAND * L + jj - 1)
                    o, g = runs(dd[:, jj % 2], jj), runs(gt, jj)
                    tt(o, g, g[:, :, :, 0:1].to_broadcast([P, 2, TOK // BAND, BAND - jj]), ALU.subtract).then_inc(diff_ready, 1)

                def mul(jj):
                    dve.wait_ge(ediff_ready, BAND * L + jj + 1)
                    dve.wait_ge(qk_prod, BAND * L + jj + 1)
                    o = runs(dd[:, jj % 2], jj)
                    tt(o, o, runs(qk[:, jj % 2], jj), ALU.mult).then_inc(sub_ready, 1)

                sub(0)
                sub(1)
                def diagonal(x):
                    return x[:, :, 0:384].rearrange("p h (b c) -> p h b c", c=P)[:, :, 0::2, :]

                masked = [bank(M + 4 + g).rearrange("p (h b c) -> p h b c", h=2, b=2) for g in range(2)]
                dve.wait_ge(lev_ps, 6 * L + DIRECT + 1)
                lm = [C("levels", P * k, P * k + P).unsqueeze(1).unsqueeze(1).to_broadcast([P, 2, 2, P])
                      for k in (3, 2)]
                for g in range(2):
                    last = tt(diagonal(pt)[:, g::2], masked[g], lm[0], ALU.mult)
                last.then_inc(masked_taken, 1)
                dve.wait_ge(lev_ps, 6 * L + DIRECT + 2)
                near4 = near.rearrange("p h (b c) -> p h b c", b=2)
                for g in range(2):
                    last = tt(near4[:, g::2], masked[g], lm[1], ALU.mult)
                last.then_inc(masked_taken, 1)
                mul(0)
                sub(2)
                mul(1)
                sub(3)
                mul(2)
                mul(3)
                dve.wait_ge(masked_taken, 2 * L + 2)
                cp(pt[:, :, 128:256], ps_t[:, M:M + 4, 128:256])
                for b in range(2):
                    last = tt(near4[:, :, b, :], near4[:, :, b, :], diagonal(ps_t[:, M:M + 4, :])[:, :, b, :], ALU.add)
                last.then_inc(dve_step, 1)
                dve.wait_ge(dve_step, steps.next())
                for b in range(2):
                    last = tt(diagonal(pt)[:, :, b, :], diagonal(pt)[:, :, b, :], near4[:, :, b, :], ALU.add)
                last.then_inc(dve_step, 1)
                dve.wait_ge(dve_step, steps.next())
                for jj in range(BAND):
                    fill(L, GLA, 6 + jj)
                dve.wait_ge(sub_ps, BAND * L + BAND)
                cp(band[0:32], ps_t[0:32, M + 4:M + 6, 0:TOK]).then_inc(band_ready, 1)
                for hh in range(4):
                    dve.wait_ge(spread_ps, 4 * L + hh + 1)
                    if hh > 0:
                        dve.wait_ge(pt_ready, L * NHEAD + hh)
                    d = bank(M + 4 + hh % 2)
                    tt(pt[0:32, hh, 384:416], d[0:32, 256:288], C("sub_diag", 256, 288)[0:32], ALU.mult)
                    tt(dtmp[:, 0:256], d[:, 0:256], C("sub_diag", 0, 256), ALU.mult).then_inc(dve_step, 1)
                    dve.wait_ge(dve_step, steps.next())
                    dg = diagonal(pt)[:, hh]
                    tt(dg, dg, dtmp[:, 0:256].rearrange("p (b c) -> p b c", b=2), ALU.add).then_inc(pt_ready, 1)
                dve.wait_ge(pt_ready, L * NHEAD + 4)
                for s in range(10, 15):
                    fill(L, GLA, s)
                out_norm(L, GLA, 15)

            def ret(L):
                z4 = zset[1][:, 0:4, 0:TOK]
                for b in range(4):
                    dve.wait_ge(stream_act, taken_before(T_OF[("z", L, 1, b)] + 1, "act"))
                tt(tmp4, z4, C("cos").unsqueeze(1).to_broadcast([P, 4, TOK]), ALU.mult).then_inc(dve_step, 1)
                dve.wait_ge(dve_step, steps.next())
                fill(L, RET, 0)
                dve.wait_ge(rot_ps, L + 1)
                tt(z4, ps_t[:, M:M + 4, 0:TOK], C("sin").unsqueeze(1).to_broadcast([P, 4, TOK]), ALU.mult).then_inc(dve_step, 1)
                dve.wait_ge(dve_step, steps.next())
                tt(z4, z4, tmp4, ALU.add).then_inc(rope_ready, 1)
                dve.wait_ge(rope_ready, L + 1)
                tt(qg[:, 0:2, :], z4[:, 0:2, 256:288], C("ret_eg").rearrange("p (q t) -> p q t", q=2),
                   ALU.mult).then_inc(qg_ready, 1)
                take_vk(L, RET)
                fill(L, RET, 1)
                scores(L, RET, 2)
                out_norm(L, RET, 6)

            def gdn(L):
                conv(L, GDN)
                dve.wait_ge(qkrt_ready, L + 1)
                V.reciprocal(rs4, rs4).then_inc(dve_step, 1)
                dve.wait_ge(dve_step, steps.next())
                stt(cv[:, 0:2, :], cv[:, 0:2, :], 0.125, rs4[:, 0:2, :], ALU.mult, ALU.mult)
                tt(cv[:, 2:4, :], cv[:, 2:4, :], rs4[:, 2:4, :], ALU.mult).then_inc(qk_ready, 1)
                dve.wait_ge(qk_ready, L + 1)
                fill(L, GDN, 8)
                take_vk(L, GDN)
                fill(L, GDN, 9)
                dve.wait_ge(beta_ps, L + 1)
                tt(kb, cv[:, 2:4, :], ps_t[:, M + 4:M + 6, 0:TOK], ALU.mult).then_inc(kb_ready, 1)
                dve.wait_ge(kb_ready, L + 1)
                fill(L, GDN, 10)
                decays(L, GDN)
                tt(qg[:, 0:2, :], cv[:, 0:2, 256:288], egp[:, 0:2, :], ALU.mult).then_inc(qg_ready, 1)
                tt(kbg, kb[:, :, 256:288], egp[:, 0:2, :], ALU.mult).then_inc(kbg_ready, 1)
                for hh in range(4):
                    dve.wait_ge(kk_ps, 4 * L + hh + 1)
                    tt(pt[:, hh, 0:384], bank(M + hh)[:, 0:384], dmat[:, hh, 0:384], ALU.mult)
                    last = tt(pt[0:32, hh, 384:416], bank(M + hh)[0:32, 384:416], dmat[0:32, hh, 384:416], ALU.mult)
                last.then_inc(dve_step, 1)
                dve.wait_ge(dve_step, steps.next())
                tt(pt[:, :, 0:384], pt[:, :, 0:384], C("strict", 0, 384).unsqueeze(1).to_broadcast([P, 4, 384]), ALU.mult)
                tt(pt[0:32, :, 384:416], pt[0:32, :, 384:416],
                   C("strict", 384, 416)[0:32].unsqueeze(1).to_broadcast([32, 4, 32]), ALU.mult).then_inc(mt_ready, 1)
                dve.wait_ge(mt_ready, L + 1)

                def mask(lv):
                    if 7 * L + lv > 0:
                        dve.wait_ge(p_ps, 7 * L + lv)
                    tt(msk[:, :, 1, :], pt[:, :, 256:384],
                       C("levels", 128 * lv, 128 * lv + 128).unsqueeze(1).to_broadcast([P, 4, P]),
                       ALU.mult).then_inc(mask1_ready, 1)

                mask(0)
                fill(L, GDN, 13)
                for lv in range(2):
                    dve.wait_ge(x_s_ps, 2 * L + lv + 1)
                    d = bank(M + 4)
                    tt(xs_s[0:32], xs_s[0:32], d[0:32, 128:256].rearrange("p (h c) -> p h c", h=4), ALU.subtract)
                    tt(xt_s[0:32], xt_s[0:32], d[0:32, 256:384].rearrange("p (h c) -> p h c", h=4),
                       ALU.subtract).then_inc(inv_s_ready, 1)
                    fill(L, GDN, 14 + lv)
                v2 = [q.rearrange("p h b c -> p (h b c)").rearrange("p (k c) -> p k c", k=2) for q in (xm, xt)]
                for lv in range(7):
                    fill(L, GDN, 16 + 2 * lv)
                    if lv < 6:
                        mask(lv + 1)
                    dve.wait_ge(x_ps, 7 * L + lv + 1)
                    tt(v2[0], v2[0], ps_t[:, M + 2:M + 4, :], ALU.subtract)
                    tt(v2[1], v2[1], ps_t[:, M + 4:M + 6, :], ALU.subtract).then_inc(inv_ready, 1)
                    fill(L, GDN, 17 + 2 * lv)
                dve.wait_ge(vn0_ps, L + 1)
                cp(vtok[:, 0, :], bank(M)).then_inc(vn0_ready, 1)
                dve.wait_ge(ks_ps, L + 1)
                for f in range(2):
                    last = cp(pb.rearrange("p h b c -> p (h b c)")[:, 0:128].rearrange("p (q f c) -> p q f c", q=2, f=2)[:, :, f, :],
                              bank(M + 1 + 4 * f)[:, 0:64].rearrange("p (q c) -> p q c", q=2))
                last.then_inc(ks_ready, 1)
                fill(L, GDN, 30)
                dve.wait_ge(r1_ps, L + 1)
                tt(vtok[:, 1, :], vtok[:, 1, :], bank(M + 2), ALU.subtract)
                dve.wait_ge(kst_ps, L + 1)
                tt(vtok[0:32, 2, :], vtok[0:32, 2, :], bank(M + 3)[0:32, :], ALU.subtract).then_inc(r1_ready, 1)
                fill(L, GDN, 31)
                dve.wait_ge(vn1_ps, L + 1)
                cp(vtok[:, 1, :], bank(M + 4))
                cp(vtok[0:32, 2, :], bank(M + 5)[0:32, :]).then_inc(vn1_ready, 1)
                fill(L, GDN, 32)
                scores(L, GDN, 33)
                out_norm(L, GDN, 37)

            def ssd(L):
                conv(L, SSD)
                take_vk(L, SSD)
                for s in range(6, 9):
                    fill(L, SSD, s)
                decays(L, SSD)
                tt(qg, cv[:, 5, 256:288].unsqueeze(1).to_broadcast([P, 4, SAMP]), egp, ALU.mult).then_inc(qg_ready, 1)
                scores(L, SSD, 13)
                out_norm(L, SSD, 21)

            def dense(L):
                for f in range(NF):
                    dve.wait_ge(tanh_ready, f + 1)
                    b = bank(M + 2 * (f % 2))
                    stt(silu_t[:, f % 2, :], tanh_t[:, f % 2, :], 1.0, b[:, 0:TOK], ALU.add, ALU.mult).then_inc(dve_step, 1)
                    dve.wait_ge(dve_step, steps.next())
                    dve.wait_ge(tile_done, T_OF[("up", L, 0, f)] + 1)
                    stt(hid[:, f, :], silu_t[:, f % 2, :], 0.5, bank(M + 1 + 2 * (f % 2))[:, 0:TOK], ALU.mult,
                        ALU.mult).then_inc(hid_ready, 1)
                    if f - 1 > 0:
                        dve.wait_ge(hid_ready, f - 1)
                dve.wait_ge(tile_done, T_OF[("down", L, 0, NF - 1)] + 1)
                for b in range(KD):
                    tt(h[:, b, :], h[:, b, :], bank(b)[:, 0:TOK], ALU.add).then_inc(dve_step, 1)
                    dve.wait_ge(dve_step, steps.next())
                    square(3 * L + 2, b)

            def experts(L):
                dve.wait_ge(state_out, 16 * 4 * (L + 1))
                dve.wait_ge(stp_out, 16 * 4 * (L + 1))
                dve.wait_ge(conv_out, 16 * (L + 1))
                dve.wait_ge(logit_ps, 1)
                for r, bs in pads(0):
                    b0, b1 = bs.start, bs.stop
                    last = cp(logit[0:r, bs, :], bank(M)[0:r, 8 * b0:8 * b1].rearrange("p (b e) -> p b e", e=8))
                last.then_inc(dve_step, 1)
                dve.wait_ge(dve_step, steps.next())
                for r, bs in pads(0):
                    nb = bs.stop - bs.start
                    sh = [r, nb, 8, 8]
                    mine = logit[0:r, bs, :].unsqueeze(3).to_broadcast(sh)
                    other = logit[0:r, bs, :].unsqueeze(2).to_broadcast(sh)
                    less = C("less")[0:r].rearrange("p (e f) -> p e f", e=8).unsqueeze(1).to_broadcast(sh)
                    tt(rank_t[0:r, bs], other, mine, ALU.is_gt)
                    tt(less_t[0:r, bs], other, mine, ALU.is_equal).then_inc(dve_step, 1)
                    dve.wait_ge(dve_step, steps.next())
                    tt(less_t[0:r, bs], less_t[0:r, bs], less, ALU.mult).then_inc(dve_step, 1)
                    dve.wait_ge(dve_step, steps.next())
                    tt(rank_t[0:r, bs], rank_t[0:r, bs], less_t[0:r, bs], ALU.add).then_inc(dve_step, 1)
                    dve.wait_ge(dve_step, steps.next())
                    V.reduce_sum(sel[0:r, bs, :], rank_t[0:r, bs], AX.X).then_inc(dve_step, 1)
                    dve.wait_ge(dve_step, steps.next())
                    ts(sel[0:r, bs, :], sel[0:r, bs, :], float(TOP_K), None, ALU.is_lt).then_inc(dve_step, 1)
                    dve.wait_ge(dve_step, steps.next())
                    V.reduce_max(mx[0:r, bs], logit[0:r, bs, :], AX.X).then_inc(dve_step, 1)
                    dve.wait_ge(dve_step, steps.next())
                    tt(wts[0:r, bs, :], logit[0:r, bs, :], mx[0:r, bs].unsqueeze(2).to_broadcast([r, nb, 8]), ALU.subtract).then_inc(dve_step, 1)
                    dve.wait_ge(dve_step, steps.next())
                cp(slotrow, C("slot_row", 0, PLACES)).then_inc(sel_ready, 1)
                cp(slotcol, C("slot_col")).then_inc(sel_ready, 1)
                dve.wait_ge(expw_ready, 1)
                for r, bs in pads(0):
                    nb = bs.stop - bs.start
                    tt(wts[0:r, bs, :], wts[0:r, bs, :], sel[0:r, bs, :], ALU.mult).then_inc(dve_step, 1)
                    dve.wait_ge(dve_step, steps.next())
                    V.reduce_sum(mx[0:r, bs], wts[0:r, bs, :], AX.X).then_inc(dve_step, 1)
                    dve.wait_ge(dve_step, steps.next())
                    V.reciprocal(mx[0:r, bs], mx[0:r, bs]).then_inc(dve_step, 1)
                    dve.wait_ge(dve_step, steps.next())
                    tt(wts[0:r, bs, :], wts[0:r, bs, :], mx[0:r, bs].unsqueeze(2).to_broadcast([r, nb, 8]), ALU.mult).then_inc(dve_step, 1)
                    dve.wait_ge(dve_step, steps.next())
                dve.wait_ge(pos_ps, 1)
                V.reduce_max(cnt[:, 2:3], bank(M)[:, 24:32], AX.X).then_inc(dve_step, 1)
                dve.wait_ge(dve_step, steps.next())
                for r, bs in pads(0):
                    b0, b1 = bs.start, bs.stop
                    stt(posm[0:r, bs, 0:8], bank(M)[0:r, 8 * b0:8 * b1].rearrange("p (b e) -> p b e", e=8), 1.0,
                               sel[0:r, bs, :], ALU.add, ALU.mult).then_inc(dve_step, 1)
                    dve.wait_ge(dve_step, steps.next())
                    last = ts(posm[0:r, bs, 0:8], posm[0:r, bs, 0:8], -1.0, None, ALU.add)
                last.then_inc(pos_ready, 1)
                ts(cnt[:, 0:1], cnt[:, 2:3], PLACES + 0.5, 1.0, ALU.is_gt, ALU.add).then_inc(dve_step, 1)
                dve.wait_ge(dve_step, steps.next())
                ts(cnt[:, 1:2], cnt[:, 2:3], 2 * PLACES + 0.5, None, ALU.is_gt).then_inc(dve_step, 1)
                dve.wait_ge(dve_step, steps.next())
                tt(nrt, cnt[:, 0:1], cnt[:, 1:2], ALU.add).then_inc(rounds_ready, 1)
                for e in range(NE):
                    dve.wait_ge(rows_ps, e + 1)
                    b = M + 2 * (e % 2)
                    cp(posrow[:, e, :], bank(b)[:, 0:TOK])
                    cp(wrow[:, e, :], bank(b + 1)[:, 0:TOK]).then_inc(rows_taken, 1)
                dve.wait_ge(rounds_ready, 1)
                for r, bs in pads(0):
                    last = ts(posm[0:r, bs, 8:9], posm[0:r, bs, 0:1], -float(PLACES), None, ALU.add)
                last.then_inc(expert_added, 3)
                for b, (t0, nt) in enumerate(TB):
                    last = tt(gath[0:nt, b, :], slotrow[0:nt], posm[0:nt, b, 0:1].to_broadcast([nt, PLACES]), ALU.is_equal)
                last.then_inc(gather_ready, 1)
                dve.wait_ge(expert_added, 3)
                rounds = dve.value_load(nrt[0:1, 0:1], min_val=1, max_val=3)
                with dve.Fori(0, rounds) as r:
                    with dve.Fori(0, NE) as e:
                        it = dve.snap(r * NE + e)

                        def low(f):
                            t = 2 * NF + f
                            dve.wait_ge(w_high_ready, it * NF + (f + 1))
                            if f >= LOWS:
                                dve.wait_ge(expert_slots, it * E_TILES + (RING + t - LOWS + 1))
                            o = (t % RING) * TILE
                            tt(w_low[:, f % LOWS, :], ring[:, o:o + TILE], w_high[:, f % HIGHS, :].bitcast(F32),
                               ALU.subtract).then_inc(w_low_ready, 1)

                        stt(scat[0:PLACES], posrow[0:PLACES, bass.ds(e, 1), :].rearrange("p a t -> p (a t)"), slotcol[0:PLACES],
                            wrow[0:PLACES, bass.ds(e, 1), :].rearrange("p a t -> p (a t)"), ALU.is_equal,
                            ALU.mult).then_inc(scatter_ready, 1)
                        for f in range(NF):
                            dve.wait_ge(etanh_ready, it * NF + (f + 1))
                            stt(esilu[:, f % 2, :], etanh[:, f % 2, :], 1.0, bank(M + 2 * (f % 2))[:, 0:PLACES], ALU.add,
                                ALU.mult).then_inc(esilu_ready, 1)
                            dve.wait_ge(esilu_ready, it * (2 * NF) + (2 * f + 1))
                            dve.wait_ge(expert_slots, it * E_TILES + (RING + 2 * f + 2))
                            stt(ehid[:, f % 2, :], esilu[:, f % 2, :], 0.5, bank(M + 1 + 2 * (f % 2))[:, 0:PLACES], ALU.mult,
                                ALU.mult).then_inc(ehid_ready, 1)
                            dve.wait_ge(ehid_ready, it * NF + (f + 1))
                            cp(e_high[:, f, :], ehid[:, f % 2, :]).then_inc(esilu_ready, 1)
                            dve.wait_ge(esilu_ready, it * (2 * NF) + (2 * f + 2))
                            tt(e_low[:, f, :], ehid[:, f % 2, :], e_high[:, f, :].bitcast(F32), ALU.subtract).then_inc(ehid_low_ready, 1)
                            if f == NF - 2:
                                low(0)
                        for f in range(1, NF):
                            low(f)
                        dve.wait_ge(gather_ps, it * 2 + 2)
                        for b, (t0, nt) in enumerate(TB):
                            last = tt(gath[0:nt, b, :], slotrow[0:nt], posm[0:nt, b, bass.ds(e + 1, 1)].to_broadcast([nt, PLACES]),
                                      ALU.is_equal)
                        last.then_inc(gather_ready, 1)
                        for g, (b0, k0, nk) in enumerate(((0, 0, 2), (M, 2, 4), (M + 4, 6, 2))):
                            dve.wait_ge(scatter_ps, it * 3 + (g + 1))
                            tt(h[:, k0:k0 + nk, :], h[:, k0:k0 + nk, :], ps_t[:, b0:b0 + nk, 0:TOK],
                               ALU.add).then_inc(expert_added, 1)
                        dve.wait_ge(expert_added, it * 3 + 6)
                    ts(slotrow, slotrow, float(PLACES), None, ALU.add)
                    ts(slotcol, slotcol, float(PLACES), None, ALU.add).then_inc(round_step, 1)
                    dve.wait_ge(round_step, r + 1)
                for b in range(KD):
                    square(3 * L + 2, b)

            dve.wait_ge(x_in, 16)
            for b in range(KD):
                square(0, b)
            for L in range(DEPTH):
                dve.wait_ge(params_in[L], 16)
                norm(3 * L, "norm_mix")
                if L == 0:
                    dve.wait_ge(const_in, 16)
                prep(L)
                gla(L)
                ret(L)
                gdn(L)
                ssd(L)
                for b in range(4):
                    branch_tile(("br", L, 3, b))
                ts(rs4[:, 1, 0:1], rs4[:, 1, 0:1], 1.0, None, ALU.mult).then_inc(acc_ready, 1)
                for b in range(KD):
                    x = ("out", L, 0, b)
                    t = T_OF[x]
                    dve.wait_ge(tile_done, t + 1)
                    stt(h[:, b, :], bank(t % 2)[:, 0:TOK], 0.5, h[:, b, :], ALU.mult, ALU.add).then_inc(stream_dve, 1)
                    dve.wait_ge(stream_dve, taken_before(t + 1, "dve"))
                    square(3 * L + 1, b)
                norm(3 * L + 1, "norm_ffn")
                dense(L) if L % 2 == 0 else experts(L)
                norm(3 * L + 2, "norm_ple")
                for b in range(KD):
                    dve.wait_ge(stream_ple, KD * L + b + 1)
                    dve.wait_ge(stream_act, taken_before(T_OF[("pproj", L, 0, 1)] + 1, "act"))
                    stt(silu_t[:, b % 2, :], tanh_t[:, b % 2, :], 1.0, ple_pj[:, b, :], ALU.add,
                        ALU.mult).then_inc(gate_used, 1)
                    dve.wait_ge(gate_used, KD * L + b + 1)
                    stt(h[:, b, :], silu_t[:, b % 2, :], 0.5, h[:, b, :], ALU.mult, ALU.add).then_inc(dve_step, 1)
                    dve.wait_ge(dve_step, steps.next())
                    square(3 * L + 3, b)
            norm(3 * DEPTH, "norm_final")

        @block.gpsimd
        def _(pool):
            G = nc.gpsimd

            def pads_for(L, n):
                z = zset[n % 2][:, 0:NCONV[n], :]
                hs = hist[:, CONV0[n]:CONV0[n] + NCONV[n], :]
                pool.wait_ge(tile_done, T_OF[("br", L, n - 2, 3)] + 1)
                pool.wait_ge(small_in[L], 16 * 4)
                G.memset(z[:, :, 0:3], 0.0)
                for b in range(NCONV[n]):
                    last = G.tensor_copy(z[:, b, 259:315].rearrange("p (s w) -> p s w", w=7)[:, :, 0:3],
                                         hs[:, b, :].rearrange("p (s w) -> p s w", w=3))
                last.then_inc(pads_ready, 1)

            def save_rows(L, n):
                pool.wait_ge(stream_act, taken_before(T_OF[("z", L, n, NCONV[n] - 1)] + 1, "act"))
                for b in range(NCONV[n]):
                    G.tensor_copy(csave[:, CONV0[n] + b, 0:3], zblk(n, b)[:, 256:259])
                    last = G.tensor_copy(csave[:, CONV0[n] + b, 3:27].rearrange("p (s w) -> p s w", w=3),
                                         zblk(n, b)[:, 259:315].rearrange("p (s w) -> p s w", w=7)[:, :, 4:7])
                last.then_inc(rows_saved, 1)
                pool.wait_ge(rows_saved, 2 * L + (1 if n == GDN else 2))

            def samples(L, n):
                m, dv = 4 * L + n, DV[n]
                if n == GDN:
                    pool.wait_ge(vn1_ready, L + 1)
                else:
                    pool.wait_ge(vk_taken, m + 1)
                for hh in range(HEADS[n]):
                    gh = L * NHEAD + HBASE[n] + hh
                    if hh == 2:
                        pool.wait_ge(o_ps, L * NHEAD + HBASE[n] + HEADS[n])
                        e = C("ret_eg").rearrange("p (q t) -> p q t", q=2) if n == RET else egp
                        for q in range(HEADS[n] // 2):
                            last = G.tensor_tensor(st_of(n)[:, q], st_of(n)[:, q],
                                                   e[:, q, 3::4].unsqueeze(2).to_broadcast([P, NSEQ, dv]), ALU.mult)
                        last.then_inc(state_decayed, 1)
                    if hh >= 2:
                        pool.wait_ge(masked_used, gh - 1)
                    elif gh > hh:
                        pool.wait_ge(masked_used, gh - hh)
                    src = vtok[0:32, 2, dv * hh:dv * hh + dv] if n == SSD else kdec[0:32, 2, 64 * hh:64 * hh + 64]
                    G.tensor_tensor(masks[0:32, 512 * (hh % 2):512 * (hh % 2) + 512].rearrange("p (b v) -> p b v", b=NSEQ),
                                    src.unsqueeze(1).to_broadcast([32, NSEQ, 64]),
                                    C("seq_of")[0:32].unsqueeze(2).to_broadcast([32, NSEQ, 64]),
                                    ALU.mult).then_inc(masked_ready, 1)
                pool.wait_ge(state_new, m + 1)
                pool.dma_start(io["state_s"][L, n], st).then_inc(state_out, 16)
                pool.dma_start(io["state_p"][L, n], stp).then_inc(stp_out, 16)
                pool.wait_ge(state_out, 16 * (m + 1))
                if n < 3:
                    pool.dma_start(st, io["state"][L, n + 1]).then_inc(state_in, 16)

            def gla(L):
                pool.wait_ge(stream_act, taken_before(T_OF[("z", L, 0, 11)] + 1, "act"))
                pool.wait_ge(cum_taken_dve, L + 1)
                zq, zk = zset[0][:, 0:2, 0:TOK], zset[0][:, 2:4, 0:TOK]

                def product(jj):
                    if jj >= 2:
                        pool.wait_ge(sub_ready, BAND * L + jj - 1)
                    k = runs(zk, jj)[:, :, :, 0:1].to_broadcast([P, 2, TOK // BAND, BAND - jj])
                    G.tensor_tensor(runs(qk[:, jj % 2], jj), runs(zq, jj), k, ALU.mult).then_inc(qk_prod, 1)

                for lv, w in enumerate(LEVELS):
                    pool.wait_ge(lexp_ready, 6 * L + lv + 1)
                    lo, up = halves_of(lev[:, lv % 2], w)
                    klo, qup = halves_of(zk, w)[0], halves_of(zq, w)[1]
                    G.tensor_tensor(lo, lo, klo, ALU.mult)
                    G.tensor_tensor(up, up, qup, ALU.mult).then_inc(lev_ready, 1)
                    if lv in (0, 1):
                        product(lv)
                product(2)
                product(3)

            def gdn(L):
                pool.wait_ge(qk_ready, L + 1)
                G.tensor_copy(xs_s[0:32], C("ident", 0, 32)[0:32].unsqueeze(1).to_broadcast([32, 4, 32]))
                G.tensor_copy(xt_s[0:32], C("ident", 0, 32)[0:32].unsqueeze(1).to_broadcast([32, 4, 32])).then_inc(inv_s_ready, 1)
                i8 = C("ident").unsqueeze(1).to_broadcast([P, 8, P])
                G.tensor_copy(xm.rearrange("p h b c -> p (h b) c"), i8)
                G.tensor_copy(xt.rearrange("p h b c -> p (h b) c"), i8).then_inc(inv_ready, 1)
                pool.wait_ge(mt_ready, L + 1)
                for lv in range(2):
                    if 2 * L + lv > 0:
                        pool.wait_ge(p_s_ps, 2 * L + lv)
                    G.tensor_tensor(ms_s[0:32], pt[0:32, :, 384:416],
                                    C("levels", 128 * lv, 128 * lv + 32)[0:32].unsqueeze(1).to_broadcast([32, 4, 32]),
                                    ALU.mult).then_inc(mask_s_ready, 1)
                for lv in range(7):
                    if 7 * L + lv > 0:
                        pool.wait_ge(p_ps, 7 * L + lv)
                    lm = C("levels", 128 * lv, 128 * lv + 128).unsqueeze(1).to_broadcast([P, 4, P])
                    G.tensor_tensor(msk[:, :, 0, :], pt[:, :, 0:128], lm, ALU.mult).then_inc(mask_ready, 1)

            for L in range(DEPTH):
                if L > 0:
                    pool.wait_ge(u_ready, KD * 3 * L)
                    pool.wait_ge(conv_out, 16 * L)
                    pool.wait_ge(state_out, 16 * 4 * L)
                if L > 0:
                    small(L, pool)
                else:
                    pool.wait_ge(const_in, 16)
                pool.dma_start(st, io["state"][L, 0]).then_inc(state_in, 16)
                gla(L)
                samples(L, GLA)
                pads_for(L, GDN)
                samples(L, RET)
                save_rows(L, GDN)
                gdn(L)
                pads_for(L, SSD)
                samples(L, GDN)
                save_rows(L, SSD)
                pool.dma_start(io["conv_out"][L], csave.rearrange("p b c -> p (b c)")).then_inc(conv_out, 16)
                samples(L, SSD)
                pool.wait_ge(tile_done, T_OF[("br", L, 3, 3)] + 1)
                pool.wait_ge(acc_ready, L + 1)
                pool.dma_start(ple_in.rearrange("p k t -> p (k t)"), io["ple"][L]).then_inc(ple_loaded, 16)
                if L == 1:
                    pool.dma_start(router.rearrange("p k e -> p (k e)"), io["router"]).then_inc(router_in, 16)
            pool.wait_ge(conv_out, 16 * DEPTH)
            pool.wait_ge(state_out, 16 * 4 * DEPTH)
            pool.wait_ge(stp_out, 16 * 4 * DEPTH)
            pool.wait_ge(u_ready, KD * (3 * DEPTH + 1))
            pool.dma_start(io["y"], u.rearrange("p k t -> p (k t)")).then_inc(y_out, 16)
            pool.wait_ge(y_out, 16)


def lay_out(x):
    g = {k: np.asarray(v) for k, v in x.items()}
    a = {}

    def fm(t):
        return np.ascontiguousarray(t.T.reshape(-1, P, t.shape[0]).transpose(1, 0, 2))

    def join(p, s):
        return np.concatenate([p.reshape(SEQ, -1), s.reshape(SAMP, -1)], 0)

    a["x"] = fm(join(g["x_prompt"], g["x_sample"])).reshape(P, -1)
    a["ple"] = np.stack([fm(join(g["p_prompt"][L], g["p_sample"][L])).reshape(P, -1) for L in range(DEPTH)])
    total = len(PLAIN) + NE * E_TILES
    stream = np.empty((total, P, TILE), np.float32)

    def kblocks(w, c0, k0=0, nk=8):
        return w[k0 * P:(k0 + nk) * P, c0:c0 + P].reshape(nk, P, P).transpose(1, 0, 2)

    for t, (kind, L, n, b) in enumerate(PLAIN):
        row = stream[t if t < EXPERT_AT else t + NE * E_TILES].reshape(P, 8, P)
        if kind == "z":
            row[:] = kblocks(g["w_in"][L], ZCOLS[n][b])
        elif kind == "mg":
            row[:] = kblocks(g["w_in"][L], _C[16] + n * D_MODEL + P * b)
        elif kind == "br":
            for o in range(2):
                row[:, 4 * o:4 * o + 4] = kblocks(g["w_branch"][L, n], P * (2 * b + o), 0, 4)
        elif kind == "out":
            row[:] = kblocks(g["w_out"][L], P * b)
        elif kind == "gate":
            row[:] = kblocks(g["ffn_w_gate"][L // 2], P * b)
        elif kind == "up":
            row[:] = kblocks(g["ffn_w_up"][L // 2], P * b)
        elif kind == "down":
            row[:] = g["ffn_w_down"][L // 2][P * b:P * b + P].reshape(P, 8, P)
        elif kind == "pproj":
            for o in range(4):
                row[:, 2 * o:2 * o + 2] = kblocks(g["ple_w_proj"][L], P * (4 * b + o), 0, 2)
        elif kind == "pgate":
            row[:] = kblocks(g["ple_w_gate"][L], P * b)
    for e in range(NE):
        base = EXPERT_AT + e * E_TILES
        for f in range(NF):
            stream[base + 2 * f].reshape(P, 8, P)[:] = kblocks(g["moe_w_gate"][0, e], P * f)
            stream[base + 2 * f + 1].reshape(P, 8, P)[:] = kblocks(g["moe_w_up"][0, e], P * f)
            stream[base + 2 * NF + f] = g["moe_w_down"][0, e][P * f:P * f + P]
    a["stream"] = stream

    def halves(s, n):
        out = np.empty((2, 64, HEADS[n] // 2, NSEQ, DV[n]), np.float32)
        for hh in range(HEADS[n]):
            half, pair = half_pair(n, hh)
            out[half, :, pair] = s[:, hh].transpose(1, 0, 2)
        return out.reshape(P, 2048)

    names = ("state_gla", "state_ret", "state_gdn", "state_ssd")
    a["state"] = np.stack([np.stack([halves(g[names[n]][L], n) for n in range(4)]) for L in range(DEPTH)])
    a["hist"] = np.stack([np.concatenate([g[k][L].transpose(2, 0, 1).reshape(-1, P, 24).transpose(1, 0, 2)
                                          for k in ("state_gdn_conv", "state_ssd_conv")], 1).reshape(P, -1)
                          for L in range(DEPTH)])

    def cols(v):
        return v.reshape(-1, P).T

    pvs, wsm, wgk, rws = [], [], [], []
    for L in range(DEPTH):
        cw = np.concatenate([g["gdn_conv_w"][L], g["ssd_conv_w"][L]], 1)
        pvs.append(np.concatenate(
            [cols(g["norm_mix"][L]), cols(g["norm_ffn"][L]), cols(g["norm_ple"][L]), cols(g["norm_final"]),
             cols(g["gla_norm"][L]), cols(g["ret_norm"][L]), cols(g["gdn_norm"][L]), cols(g["ssd_norm"][L]),
             cw.reshape(4 * 14, P).T, np.zeros((P, 8), np.float32), cols(g["ssd_conv_b"][L]),
             cols(np.repeat(g["ssd_d"][L], 64))], 1))
        w = g["w_in"][L]
        w = np.concatenate([w[:, _C[3]:_C[4]], w[:, _C[10]:_C[12]], w[:, _C[15]:_C[16]]], 1)
        wsm.append(w.reshape(8, P, 32).transpose(1, 0, 2).reshape(P, -1))
        wgk.append(np.concatenate([g["gla_w_gk"][L], g["gla_b_gk"][L][None]], 0))
        z4 = np.zeros(4, np.float32)
        r = np.concatenate([z4, g["gdn_dt_bias"][L], g["ssd_dt_bias"][L], z4, g["gdn_a_log"][L], g["ssd_a_log"][L]])
        rws.append(np.broadcast_to(r, (P, 32)))
    a["pv"], a["wsm"], a["wgk"], a["rows"] = (np.ascontiguousarray(np.stack(v)) for v in (pvs, wsm, wgk, rws))
    a["router"] = g["moe_router"][0].reshape(8, P, NE).transpose(1, 0, 2).reshape(P, 64)
    a["const"] = np.concatenate([CONST[k] for k in CAT], 1)
    return {k: np.ascontiguousarray(v) for k, v in a.items()}


OUTS = {"y": (P, KD * TOK), "state_s": (DEPTH, 4, P, 2048), "state_p": (DEPTH, 4, P, 256), "conv_out": (DEPTH, P, 14 * 27)}


def gather_outputs(r):
    y = r["y"].reshape(P, KD, TOK).transpose(2, 1, 0).reshape(TOK, D_MODEL)
    pr, sa = [], []
    for n in range(4):
        s = r["state_s"][:, n].reshape(DEPTH, 2, 64, HEADS[n] // 2, NSEQ, DV[n])
        q = r["state_p"][:, n].reshape(DEPTH, 2, 64, HEADS[n] // 2, DV[n])
        hp = [half_pair(n, hh) for hh in range(HEADS[n])]
        sa.append(np.stack([s[:, a, :, b].transpose(0, 2, 1, 3) for a, b in hp], 2))
        pr.append(np.stack([q[:, a, :, b] for a, b in hp], 1)[:, None])
    c = r["conv_out"].reshape(DEPTH, P, 14, 9, 3).transpose(0, 3, 4, 2, 1).reshape(DEPTH, 9, 3, 14 * P)
    cp, cs = c[:, 0:1], c[:, 1:]
    w = 8 * P
    out = (y[:SEQ].reshape(1, SEQ, D_MODEL), y[SEQ:].reshape(NSEQ, DSEQ, D_MODEL),
           pr[0], pr[1], pr[2], cp[..., :w], pr[3], cp[..., w:],
           sa[0], sa[1], sa[2], cs[..., :w], sa[3], cs[..., w:])
    return tuple(np.ascontiguousarray(v) for v in out)


def kernel(**inputs):
    import concourse.bacc as bacc
    from concourse.bass_utils import run_bass_kernel_spmd

    nc = bacc.Bacc("TRN2", target_bir_lowering=False, num_devices=1)
    arrays = lay_out(inputs)
    io = {k: nc.dram_tensor(f"in_{k}", v.shape, F32, kind="ExternalInput").ap() for k, v in arrays.items()}
    io |= {k: nc.dram_tensor(k, s, F32, kind="ExternalOutput").ap() for k, s in OUTS.items()}
    build(nc, io)
    r = run_bass_kernel_spmd(nc, [{f"in_{k}": v for k, v in arrays.items()}], core_ids=[0])
    return gather_outputs({k: r.results[0][k] for k in OUTS})
```
